# Optimizing a Trainium2 kernel written in Bass

```python
import math
import jax, jax.numpy as jnp
from jax import lax
import numpy as np

D_MODEL = 1024
BATCH = 1
SEQ = 256
DEPTH = 1

HEAD_DIM = 64
N_HEADS_MOBA = 8
N_HEADS_SB = 8
MOBA_WIDTH = N_HEADS_MOBA * HEAD_DIM
SB_WIDTH = N_HEADS_SB * HEAD_DIM
N_BRANCHES = 2
IN_WIDTH = 3 * MOBA_WIDTH + 3 * SB_WIDTH + N_BRANCHES * D_MODEL
MOBA_BLOCK = 256
MOBA_TOPK = 3
MOBA_Q_CHUNK = 16
SB_Q_BLOCK = 128
D_FF = 2816
CONV_WIDTH = 3
REL_BUCKETS = 32
REL_MAX_DIST = 128
NORM_EPS = 1e-6
NEG_INF = -1e30


def rms_norm(x, g):
    xf = x.astype(jnp.float32)
    y = xf * lax.rsqrt(jnp.mean(xf * xf, axis=-1, keepdims=True) + NORM_EPS)
    return (y * g.astype(jnp.float32)).astype(x.dtype)

def modulate(h, shift, scale):
    return h * (1.0 + scale[:, None, :]) + shift[:, None, :]

def to_heads(t, n_heads):
    b, s, _ = t.shape
    return t.reshape(b, s, n_heads, HEAD_DIM).transpose(0, 2, 1, 3)

def merge_heads(t):
    b, h, s, hd = t.shape
    return t.transpose(0, 2, 1, 3).reshape(b, s, h * hd)

def t5_bucket(rel):
    n = jnp.maximum(rel, 0)
    max_exact = REL_BUCKETS // 2
    n_f = jnp.maximum(n, max_exact).astype(jnp.float32)
    large = max_exact + (jnp.log(n_f / max_exact) / math.log(REL_MAX_DIST / max_exact)
                         * (REL_BUCKETS - max_exact)).astype(jnp.int32)
    large = jnp.minimum(large, REL_BUCKETS - 1)
    return jnp.where(n < max_exact, n, large)

def moba_attention(q, k, v, rel_table):
    b, h, s, hd = q.shape
    n_blk = -(-s // MOBA_BLOCK)
    s_pad = n_blk * MOBA_BLOCK
    pad = ((0, 0), (0, 0), (0, s_pad - s), (0, 0))
    q = jnp.pad(q, pad)
    k = jnp.pad(k, pad)
    v = jnp.pad(v, pad)
    k_blk = k.reshape(b, h, n_blk, MOBA_BLOCK, hd)
    v_blk = v.reshape(b, h, n_blk, MOBA_BLOCK, hd)
    k_mean = jnp.mean(k_blk.astype(jnp.float32), axis=3).astype(q.dtype)
    n_sel = min(MOBA_TOPK, n_blk)
    scale = hd ** -0.5
    n_chunks = s_pad // MOBA_Q_CHUNK
    q_chunks = jnp.moveaxis(q.reshape(b, h, n_chunks, MOBA_Q_CHUNK, hd), 2, 0)
    b_idx = jnp.arange(b)[:, None, None, None]
    h_idx = jnp.arange(h)[None, :, None, None]
    offs = jnp.arange(MOBA_BLOCK)
    blk_ids = jnp.arange(n_blk)

    def chunk(args):
        qc, ci = args
        q_start = ci * MOBA_Q_CHUNK
        q_pos = q_start + jnp.arange(MOBA_Q_CHUNK)
        own = q_start // MOBA_BLOCK
        gate = jnp.einsum('bhqd,bhnd->bhqn', qc, k_mean).astype(jnp.float32)
        gate = jnp.where(blk_ids < own, gate, NEG_INF)
        _, sel = lax.top_k(gate, n_sel)
        sel_ok = sel < own
        k_sel = k_blk[b_idx, h_idx, sel]
        v_sel = v_blk[b_idx, h_idx, sel]
        s_sel = jnp.einsum('bhqd,bhqnkd->bhqnk', qc, k_sel).astype(jnp.float32) * scale
        rel_sel = q_pos[:, None, None] - (sel[..., None] * MOBA_BLOCK + offs)
        bias_sel = rel_table[h_idx[..., None], t5_bucket(rel_sel)]
        s_sel = jnp.where(sel_ok[..., None], s_sel + bias_sel, NEG_INF)
        k_own = lax.dynamic_slice_in_dim(k, own * MOBA_BLOCK, MOBA_BLOCK, axis=2)
        v_own = lax.dynamic_slice_in_dim(v, own * MOBA_BLOCK, MOBA_BLOCK, axis=2)
        s_own = jnp.einsum('bhqd,bhkd->bhqk', qc, k_own).astype(jnp.float32) * scale
        rel_own = q_pos[:, None] - (own * MOBA_BLOCK + offs)[None, :]
        bias_own = rel_table[:, t5_bucket(rel_own)]
        s_own = jnp.where(rel_own >= 0, s_own + bias_own, NEG_INF)
        logits = jnp.concatenate(
            [s_sel.reshape(b, h, MOBA_Q_CHUNK, n_sel * MOBA_BLOCK), s_own], axis=-1)
        p = jax.nn.softmax(logits, axis=-1).astype(v.dtype)
        p_sel = p[..., :n_sel * MOBA_BLOCK].reshape(b, h, MOBA_Q_CHUNK, n_sel, MOBA_BLOCK)
        p_own = p[..., n_sel * MOBA_BLOCK:]
        return (jnp.einsum('bhqnk,bhqnkd->bhqd', p_sel, v_sel)
                + jnp.einsum('bhqk,bhkd->bhqd', p_own, v_own))

    out = lax.map(chunk, (q_chunks, jnp.arange(n_chunks)))
    return jnp.moveaxis(out, 0, 2).reshape(b, h, s_pad, hd)[:, :, :s]

def stick_breaking_attention(q, k, v):
    b, h, s, hd = q.shape
    n_qb = s // SB_Q_BLOCK
    scale = hd ** -0.5
    k_pos = jnp.arange(s)
    q_blocks = jnp.moveaxis(q.reshape(b, h, n_qb, SB_Q_BLOCK, hd), 2, 0)

    def block(args):
        qb, bi = args
        q_pos = bi * SB_Q_BLOCK + jnp.arange(SB_Q_BLOCK)
        z = jnp.einsum('bhqd,bhkd->bhqk', qb, k).astype(jnp.float32) * scale
        past = k_pos[None, :] < q_pos[:, None]
        log_beta = jax.nn.log_sigmoid(z)
        log_keep = jnp.where(past, jax.nn.log_sigmoid(-z), 0.0)
        log_later = lax.cumsum(log_keep, axis=3, reverse=True) - log_keep
        a = jnp.where(past, jnp.exp(log_beta + log_later), 0.0)
        return jnp.einsum('bhqk,bhkd->bhqd', a.astype(v.dtype), v)

    out = lax.map(block, (q_blocks, jnp.arange(n_qb)))
    return jnp.moveaxis(out, 0, 2).reshape(b, h, s, hd)

def causal_depthwise_conv(u, w, bias):
    ch = u.shape[-1]
    out = lax.conv_general_dilated(
        u, w[:, None, :], window_strides=(1,), padding=[(CONV_WIDTH - 1, 0)],
        dimension_numbers=('NWC', 'WIO', 'NWC'), feature_group_count=ch)
    return out + bias

def first_inputs(seed: int = 0) -> dict:
    key = jax.random.key(seed)
    ks = jax.random.split(key, 16)
    f32 = jnp.float32
    nrm = lambda k, shp, sc: jax.random.normal(k, shp, f32) * sc
    return {
        'x': nrm(ks[0], (BATCH, SEQ, D_MODEL), 1.0),
        'c': nrm(ks[1], (BATCH, D_MODEL), 1.0),
        'w_ada': nrm(ks[2], (DEPTH, D_MODEL, 6 * D_MODEL), D_MODEL ** -0.5),
        'b_ada': nrm(ks[3], (DEPTH, 6 * D_MODEL), 0.02),
        'g_mix': 1.0 + nrm(ks[4], (DEPTH, D_MODEL), 0.05),
        'w_in': nrm(ks[5], (DEPTH, D_MODEL, IN_WIDTH), D_MODEL ** -0.5),
        'w_br_moba': nrm(ks[6], (DEPTH, MOBA_WIDTH, D_MODEL), MOBA_WIDTH ** -0.5),
        'w_br_sb': nrm(ks[7], (DEPTH, SB_WIDTH, D_MODEL), SB_WIDTH ** -0.5),
        'w_out': nrm(ks[8], (DEPTH, D_MODEL, D_MODEL), D_MODEL ** -0.5),
        'rel_bias': nrm(ks[9], (N_HEADS_MOBA, REL_BUCKETS), 0.5),
        'g_ffn': 1.0 + nrm(ks[10], (DEPTH, D_MODEL), 0.05),
        'w_up': nrm(ks[11], (DEPTH, D_MODEL, 2 * D_FF), D_MODEL ** -0.5),
        'w_conv': nrm(ks[12], (DEPTH, CONV_WIDTH, 2 * D_FF), CONV_WIDTH ** -0.5),
        'b_conv': nrm(ks[13], (DEPTH, 2 * D_FF), 0.02),
        'w_down': nrm(ks[14], (DEPTH, D_FF, D_MODEL), D_FF ** -0.5),
        'g_final': 1.0 + nrm(ks[15], (D_MODEL,), 0.05),
    }

def first_block(x, c, w_ada, b_ada, g_mix, w_in, w_br_moba, w_br_sb, w_out, rel_bias,
              g_ffn, w_up, w_conv, b_conv, w_down, g_final):
    splits = list(np.cumsum([MOBA_WIDTH, MOBA_WIDTH, MOBA_WIDTH, SB_WIDTH, SB_WIDTH, SB_WIDTH]))
    c_act = jax.nn.silu(c)
    for l in range(DEPTH):
        mod = c_act @ w_ada[l] + b_ada[l]
        sh_m, sc_m, gt_m, sh_f, sc_f, gt_f = jnp.split(mod, 6, axis=-1)
        h = modulate(rms_norm(x, g_mix[l]), sh_m, sc_m)
        proj = jnp.einsum('bsd,de->bse', h, w_in[l])
        qa, ka, va, qb, kb, vb, gate_logits = jnp.split(proj, splits, axis=-1)
        oa = moba_attention(to_heads(qa, N_HEADS_MOBA), to_heads(ka, N_HEADS_MOBA),
                            to_heads(va, N_HEADS_MOBA), rel_bias)
        ob = stick_breaking_attention(to_heads(qb, N_HEADS_SB), to_heads(kb, N_HEADS_SB),
                                      to_heads(vb, N_HEADS_SB))
        ya = jnp.einsum('bse,ed->bsd', merge_heads(oa), w_br_moba[l])
        yb = jnp.einsum('bse,ed->bsd', merge_heads(ob), w_br_sb[l])
        gates = jax.nn.sigmoid(gate_logits.astype(jnp.float32)).astype(x.dtype)
        g_a, g_b = jnp.split(gates, 2, axis=-1)
        mixed = jnp.einsum('bsd,de->bse', g_a * ya + g_b * yb, w_out[l])
        x = x + gt_m[:, None, :] * mixed
        h2 = modulate(rms_norm(x, g_ffn[l]), sh_f, sc_f)
        u = jnp.einsum('bsd,df->bsf', h2, w_up[l])
        u = causal_depthwise_conv(u, w_conv[l], b_conv[l])
        u_val, u_gate = jnp.split(u, 2, axis=-1)
        y = jnp.einsum('bsf,fd->bsd', jax.nn.gelu(u_gate) * u_val, w_down[l])
        x = x + gt_f[:, None, :] * y
    return rms_norm(x, g_final)


DEPTH_2 = 2

GRID_W = 64
CTX_LEN = 256
EPS = 1e-6
A_WIDTH = D_MODEL // 2
A_CONV_W = 31
B_GROUPS = 4
B_WIDTH = D_MODEL // 2
B_GROUP_DIM = B_WIDTH // B_GROUPS
C_WIDTH = D_MODEL // 2
C_CONV_W = 3
N_Q_HEADS = (D_MODEL // 2) // HEAD_DIM
N_KV_HEADS = max(N_Q_HEADS // 4, 1)
Q_GROUP = N_Q_HEADS // N_KV_HEADS
ATT_WIDTH = N_Q_HEADS * HEAD_DIM
KV_WIDTH = N_KV_HEADS * HEAD_DIM
WINDOW = 128
BLOCK = 128
ROPE_BASE = 10000.0
NEG_INF_2 = -1e30
EVEN_IN = 3 * A_WIDTH + 2 * B_WIDTH
EVEN_MIX = A_WIDTH + B_WIDTH
ODD_IN = 4 * C_WIDTH + 2 * ATT_WIDTH + 2 * KV_WIDTH
ODD_MIX = C_WIDTH + ATT_WIDTH


def _rmsnorm(x, g):
    xf = x.astype(jnp.float32)
    y = xf * lax.rsqrt(jnp.mean(xf * xf, axis=-1, keepdims=True) + EPS)
    return (y * g.astype(jnp.float32)).astype(x.dtype)

def _layernorm(x, g, b):
    xf = x.astype(jnp.float32)
    mu = jnp.mean(xf, axis=-1, keepdims=True)
    var = jnp.mean(jnp.square(xf - mu), axis=-1, keepdims=True)
    y = (xf - mu) * lax.rsqrt(var + EPS)
    return (y * g.astype(jnp.float32) + b.astype(jnp.float32)).astype(x.dtype)

def _split(t, widths):
    cuts, acc = [], 0
    for w in widths[:-1]:
        acc += w
        cuts.append(acc)
    return jnp.split(t, cuts, axis=-1)

def _modulation(cvec, w_mod, b_mod):
    h = jax.nn.silu(cvec) @ w_mod + b_mod
    shift, scale, gate = jnp.split(h[:, None, :], 3, axis=-1)
    return shift, scale, gate

def _pre(x, g, shift, scale):
    return _rmsnorm(x, g) * (1 + scale) + shift

def _dwconv(u, w):
    pad = (w.shape[0] - 1) // 2
    return lax.conv_general_dilated(
        u, w[:, None, :].astype(u.dtype), window_strides=(1,), padding=[(pad, pad)],
        dimension_numbers=('NWC', 'WIO', 'NWC'), feature_group_count=u.shape[-1])

def _fourier_mix(v, fw):
    b, l, _ = v.shape
    vg = v.reshape(b, l, B_GROUPS, B_GROUP_DIM).astype(jnp.float32)
    f = jnp.fft.fftn(vg, axes=(1, 3), norm='ortho').real.astype(v.dtype)
    return jnp.einsum('blgd,gde->blge', f, fw).reshape(b, l, B_WIDTH)

def _even_mix(h, w_in, a_conv_w, a_conv_b, a_ln_g, a_ln_b, a_pw_w, a_pw_b, b_fw, w_out):
    a_val, a_glu, a_gate, b_val, b_gate = _split(h @ w_in, [A_WIDTH, A_WIDTH, A_WIDTH, B_WIDTH, B_WIDTH])
    u = a_val * jax.nn.sigmoid(a_glu)
    u = jax.nn.silu(_layernorm(_dwconv(u, a_conv_w) + a_conv_b, a_ln_g, a_ln_b))
    y_a = (u @ a_pw_w + a_pw_b) * jax.nn.silu(a_gate)
    y_b = _fourier_mix(b_val, b_fw) * jax.nn.silu(b_gate)
    return jnp.concatenate([y_a, y_b], axis=-1) @ w_out

def _rope_tables(row, col):
    nf = HEAD_DIM // 4
    inv = jnp.power(ROPE_BASE, -jnp.arange(nf, dtype=jnp.float32) / nf)
    ang = jnp.stack([row.astype(jnp.float32)[:, None] * inv,
                     col.astype(jnp.float32)[:, None] * inv], axis=1)
    return jnp.cos(ang), jnp.sin(ang)

def _apply_rope(t, cos, sin):
    b, l, h, d = t.shape
    tr = t.astype(jnp.float32).reshape(b, l, h, 2, 2, d // 4)
    t1, t2 = tr[..., 0, :], tr[..., 1, :]
    cs, sn = cos[None, :, None], sin[None, :, None]
    out = jnp.stack([t1 * cs - t2 * sn, t2 * cs + t1 * sn], axis=-2)
    return out.reshape(b, l, h, d).astype(t.dtype)

def _sink_softmax(logits, sink):
    m = sink
    for s in logits:
        m = jnp.maximum(m, jnp.max(s, axis=-1, keepdims=True))
    ps = [jnp.exp(s - m) for s in logits]
    denom = jnp.exp(sink - m)
    for p in ps:
        denom = denom + jnp.sum(p, axis=-1, keepdims=True)
    return [p / denom for p in ps]

def _window_attention(q, k, v, kc, vc, sink):
    b, l, hq, hd = q.shape
    nb = l // BLOCK
    scale = HEAD_DIM ** -0.5
    qb = q.reshape(b, nb, BLOCK, N_KV_HEADS, Q_GROUP, hd)

    def band(t):
        tp = jnp.pad(t, ((0, 0), (BLOCK, BLOCK), (0, 0), (0, 0))).reshape(b, nb + 2, BLOCK, N_KV_HEADS, hd)
        return jnp.concatenate([tp[:, :-2], tp[:, 1:-1], tp[:, 2:]], axis=2)

    kw, vw = band(k), band(v)
    qpos = jnp.arange(l).reshape(nb, BLOCK)
    kpos = jnp.arange(-BLOCK, l + BLOCK).reshape(nb + 2, BLOCK)
    kwpos = jnp.concatenate([kpos[:-2], kpos[1:-1], kpos[2:]], axis=1)
    valid = ((jnp.abs(qpos[:, :, None] - kwpos[:, None, :]) <= WINDOW)
             & (kwpos >= 0)[:, None, :] & (kwpos < l)[:, None, :])
    s_win = jnp.einsum('bnqhgd,bnkhd->bnhgqk', qb, kw).astype(jnp.float32) * scale
    s_win = jnp.where(valid[None, :, None, None], s_win, NEG_INF_2)
    s_ctx = jnp.einsum('bnqhgd,bchd->bnhgqc', qb, kc).astype(jnp.float32) * scale
    sink_b = sink.astype(jnp.float32).reshape(N_KV_HEADS, Q_GROUP)[None, None, :, :, None, None]
    p_win, p_ctx = _sink_softmax([s_win, s_ctx], sink_b)
    o = (jnp.einsum('bnhgqk,bnkhd->bnqhgd', p_win.astype(v.dtype), vw)
         + jnp.einsum('bnhgqc,bchd->bnqhgd', p_ctx.astype(v.dtype), vc))
    return o.reshape(b, l, hq * hd)

def _context_attention(q, k, v, sink):
    b, lc, hq, hd = q.shape
    qg = q.reshape(b, lc, N_KV_HEADS, Q_GROUP, hd)
    s = jnp.einsum('bqhgd,bkhd->bhgqk', qg, k).astype(jnp.float32) * (HEAD_DIM ** -0.5)
    sink_b = sink.astype(jnp.float32).reshape(N_KV_HEADS, Q_GROUP)[None, :, :, None, None]
    (p,) = _sink_softmax([s], sink_b)
    o = jnp.einsum('bhgqk,bkhd->bqhgd', p.astype(v.dtype), v)
    return o.reshape(b, lc, hq * hd)

def _odd_proj(h, w_in):
    cb, cc, cx, cg, q, k, v, ag = _split(
        h @ w_in, [C_WIDTH, C_WIDTH, C_WIDTH, C_WIDTH, ATT_WIDTH, KV_WIDTH, KV_WIDTH, ATT_WIDTH])
    b, l, _ = h.shape
    return (cb, cc, cx, cg,
            q.reshape(b, l, N_Q_HEADS, HEAD_DIM),
            k.reshape(b, l, N_KV_HEADS, HEAD_DIM),
            v.reshape(b, l, N_KV_HEADS, HEAD_DIM), ag)

def _odd_out(cb, cc, cx, cg, att, ag, c_conv_w, w_out):
    y_c = cb * _dwconv(cc * cx, c_conv_w) * jax.nn.silu(cg)
    y_d = att * jax.nn.silu(ag)
    return jnp.concatenate([y_c, y_d], axis=-1) @ w_out

def second_inputs(seed: int = 0) -> dict:
    key = jax.random.key(seed)
    ks = jax.random.split(key, 24)
    ne, no = (DEPTH_2 + 1) // 2, DEPTH_2 // 2

    def nrm(k, shape):
        return jax.random.normal(k, shape, jnp.float32)

    return {
        'x': nrm(ks[0], (BATCH, SEQ, D_MODEL)),
        'c': nrm(ks[1], (BATCH, D_MODEL)),
        'ctx': nrm(ks[2], (BATCH, CTX_LEN, D_MODEL)),
        'c_ctx': nrm(ks[3], (D_MODEL,)),
        'e_norm': 1.0 + 0.02 * nrm(ks[4], (ne, D_MODEL)),
        'e_w_mod': nrm(ks[5], (ne, D_MODEL, 3 * D_MODEL)) * (0.5 * D_MODEL ** -0.5),
        'e_b_mod': 0.02 * nrm(ks[6], (ne, 3 * D_MODEL)),
        'e_w_in': nrm(ks[7], (ne, D_MODEL, EVEN_IN)) * D_MODEL ** -0.5,
        'e_a_conv_w': nrm(ks[8], (ne, A_CONV_W, A_WIDTH)) * A_CONV_W ** -0.5,
        'e_a_conv_b': 0.02 * nrm(ks[9], (ne, A_WIDTH)),
        'e_a_ln_g': 1.0 + 0.02 * nrm(ks[10], (ne, A_WIDTH)),
        'e_a_ln_b': 0.02 * nrm(ks[11], (ne, A_WIDTH)),
        'e_a_pw_w': nrm(ks[12], (ne, A_WIDTH, A_WIDTH)) * A_WIDTH ** -0.5,
        'e_a_pw_b': 0.02 * nrm(ks[13], (ne, A_WIDTH)),
        'e_b_fw': nrm(ks[14], (ne, B_GROUPS, B_GROUP_DIM, B_GROUP_DIM)) * B_GROUP_DIM ** -0.5,
        'e_w_out': nrm(ks[15], (ne, EVEN_MIX, D_MODEL)) * EVEN_MIX ** -0.5,
        'o_norm': 1.0 + 0.02 * nrm(ks[16], (no, D_MODEL)),
        'o_w_mod': nrm(ks[17], (no, D_MODEL, 3 * D_MODEL)) * (0.5 * D_MODEL ** -0.5),
        'o_b_mod': 0.02 * nrm(ks[18], (no, 3 * D_MODEL)),
        'o_w_in': nrm(ks[19], (no, D_MODEL, ODD_IN)) * D_MODEL ** -0.5,
        'o_c_conv_w': nrm(ks[20], (no, C_CONV_W, C_WIDTH)) * C_CONV_W ** -0.5,
        'o_sink': 0.5 * nrm(ks[21], (no, N_Q_HEADS)),
        'o_w_out': nrm(ks[22], (no, ODD_MIX, D_MODEL)) * ODD_MIX ** -0.5,
        'final_norm': 1.0 + 0.02 * nrm(ks[23], (D_MODEL,)),
    }

def second_block(x, c, ctx, c_ctx, e_norm, e_w_mod, e_b_mod, e_w_in, e_a_conv_w, e_a_conv_b,
              e_a_ln_g, e_a_ln_b, e_a_pw_w, e_a_pw_b, e_b_fw, e_w_out,
              o_norm, o_w_mod, o_b_mod, o_w_in, o_c_conv_w, o_sink, o_w_out, final_norm):
    l = x.shape[1]
    rows = l // GRID_W
    row = jnp.broadcast_to(jnp.arange(rows)[:, None], (rows, GRID_W)).reshape(l)
    col = jnp.broadcast_to(jnp.arange(GRID_W)[None, :], (rows, GRID_W)).reshape(l)
    cos, sin = _rope_tables(row, col)
    c_ctx2 = c_ctx[None, :]
    xc = ctx
    for layer in range(DEPTH_2):
        i = layer // 2
        ctx_needed = layer < DEPTH_2 - 1
        if layer % 2 == 0:
            args = (e_w_in[i], e_a_conv_w[i], e_a_conv_b[i], e_a_ln_g[i], e_a_ln_b[i],
                    e_a_pw_w[i], e_a_pw_b[i], e_b_fw[i], e_w_out[i])
            sh, sc, gt = _modulation(c, e_w_mod[i], e_b_mod[i])
            x_new = x + gt * _even_mix(_pre(x, e_norm[i], sh, sc), *args)
            if ctx_needed:
                sh_c, sc_c, gt_c = _modulation(c_ctx2, e_w_mod[i], e_b_mod[i])
                xc = xc + gt_c * _even_mix(_pre(xc, e_norm[i], sh_c, sc_c), *args)
            x = x_new
        else:
            sh, sc, gt = _modulation(c, o_w_mod[i], o_b_mod[i])
            sh_c, sc_c, gt_c = _modulation(c_ctx2, o_w_mod[i], o_b_mod[i])
            cb_c, cc_c, cx_c, cg_c, q_c, k_c, v_c, ag_c = _odd_proj(_pre(xc, o_norm[i], sh_c, sc_c), o_w_in[i])
            cb, cc, cx, cg, q, k, v, ag = _odd_proj(_pre(x, o_norm[i], sh, sc), o_w_in[i])
            att = _window_attention(_apply_rope(q, cos, sin), _apply_rope(k, cos, sin), v, k_c, v_c, o_sink[i])
            x_new = x + gt * _odd_out(cb, cc, cx, cg, att, ag, o_c_conv_w[i], o_w_out[i])
            if ctx_needed:
                att_c = _context_attention(q_c, k_c, v_c, o_sink[i])
                xc = xc + gt_c * _odd_out(cb_c, cc_c, cx_c, cg_c, att_c, ag_c, o_c_conv_w[i], o_w_out[i])
            x = x_new
    return _rmsnorm(x, final_norm)


def setup_inputs(seed=0):
    out = dict(first_inputs(seed))
    for name, value in second_inputs(seed + 1).items():
        if name != "x":
            out[name + "_2"] = value
    return out


def reference(
    x, c, w_ada, b_ada, g_mix, w_in, w_br_moba, w_br_sb, w_out, rel_bias, g_ffn, w_up, w_conv,
    b_conv, w_down, g_final, c_2, ctx_2, c_ctx_2, e_norm_2, e_w_mod_2, e_b_mod_2, e_w_in_2,
    e_a_conv_w_2, e_a_conv_b_2, e_a_ln_g_2, e_a_ln_b_2, e_a_pw_w_2, e_a_pw_b_2, e_b_fw_2,
    e_w_out_2, o_norm_2, o_w_mod_2, o_b_mod_2, o_w_in_2, o_c_conv_w_2, o_sink_2, o_w_out_2,
    final_norm_2,
):
    x = first_block(
        x, c, w_ada, b_ada, g_mix, w_in, w_br_moba, w_br_sb, w_out, rel_bias, g_ffn, w_up,
        w_conv, b_conv, w_down, g_final,
    )
    return second_block(
        x, c_2, ctx_2, c_ctx_2, e_norm_2, e_w_mod_2, e_b_mod_2, e_w_in_2, e_a_conv_w_2,
        e_a_conv_b_2, e_a_ln_g_2, e_a_ln_b_2, e_a_pw_w_2, e_a_pw_b_2, e_b_fw_2, e_w_out_2,
        o_norm_2, o_w_mod_2, o_b_mod_2, o_w_in_2, o_c_conv_w_2, o_sink_2, o_w_out_2,
        final_norm_2,
    )


_drawn_inputs = setup_inputs


def setup_inputs(seed=0):
    import zlib

    import numpy as np

    out = dict(_drawn_inputs(seed))
    spreads = {}
    factors = {'b_conv': 4.628,
     'ctx_2': 16.248,
     'c_ctx_2': 7.575,
     'e_norm_2': 8.0,
     'e_b_mod_2': 5.238,
     'e_a_conv_b_2': 8.0,
     'e_a_ln_g_2': 8.0,
     'e_a_ln_b_2': 8.0,
     'e_a_pw_b_2': 8.0,
     'o_norm_2': 7.673,
     'o_b_mod_2': 3.637,
     'o_sink_2': 8.0,
     'final_norm_2': 8.43}
    for name, (base, spread) in spreads.items():
        noise = np.random.default_rng([zlib.crc32(name.encode()), seed]).standard_normal(out[name].shape)
        drawn = base * np.exp(spread * noise) if base else spread * noise
        out[name] = __import__('jax').numpy.asarray(drawn.astype(out[name].dtype))
    for name, factor in factors.items():
        out[name] = (out[name] * factor).astype(out[name].dtype)
    return out
```

```python
import numpy as np
from contextlib import ExitStack

import concourse.bass as bass
from concourse import mybir

F32 = mybir.dt.float32
F32R = mybir.dt.float32r
BF16 = mybir.dt.bfloat16
ALU = mybir.AluOpType
ACT = mybir.ActivationFunctionType
AX_X = mybir.AxisListType.X

P = 128
T = 256
D = 1024
KT = D // P
HD = 64
NH = 8
FF_STEPS = 11
CHUNK = 2048
RAW = 4
SPL = 3
EPS = 1e-6
NEG = -1e30
BIG = 3.0e38
QK = 0.125

LIN_QKV, LIN_GATE, LIN_BR, LIN_OUT, LIN_FFN = 0, 12, 20, 24, 28
LIN_EIN = LIN_FFN + 3 * FF_STEPS
LIN_PW = LIN_EIN + 10
LIN_EOUT = LIN_PW + 1
LIN_OIN = LIN_EOUT + 4
LIN_OOUT = LIN_OIN + 13
N_LIN = LIN_OOUT + 4
MOD_FIRST = 9
N_MOD = 48


def stream_order():
    order = [("mod", m) for m in range(MOD_FIRST)]
    m = MOD_FIRST
    for j in range(LIN_FFN):
        order += [("mod", m), ("lin", j)]
        m += 1
    order += [("lin", LIN_FFN), ("mod", m), ("lin", LIN_FFN + 1)]
    m += 1
    for i in range(FF_STEPS - 1):
        j = LIN_FFN + 2 + 3 * i
        order += [("lin", j), ("lin", j + 1), ("mod", m), ("lin", j + 2)]
        m += 1
    order += [("lin", j) for j in range(LIN_EIN - 1, N_LIN)]
    assert m == N_MOD
    return order


ORDER = stream_order()
RAW_OF_LIN = [0] * N_LIN
RAW_OF_MOD = [0] * N_MOD
for _r, (_kind, _n) in enumerate(ORDER):
    (RAW_OF_LIN if _kind == "lin" else RAW_OF_MOD)[_n] = _r

VEC_SIZES = [("cact", 32), ("mod_bias", 4 * N_MOD), ("g_mix", 8), ("g_ffn", 8), ("g_final", 8),
             ("e_norm", 8), ("o_norm", 8), ("final_norm", 8), ("w_conv", 132), ("b_conv", 44),
             ("a_conv_w", 124), ("a_conv_b", 4), ("ln_g", 4), ("ln_b", 4), ("pw_b", 4),
             ("o_conv", 12), ("sink", 8)]
VEC = {}
_at = 0
for _n, _s in VEC_SIZES:
    VEC[_n] = _at
    _at += _s
N_VEC = _at

C0 = {"ident": 0, "ones": 128}
N_C0 = 256
C1 = {"anti8": 0, "tri8": 128, "all8": 256, "past": 384, "bound": 768, "onehot": 1152}
N_C1 = 1536
C2 = {"cos_l": 0, "sin_l": 512, "dft_d": 1024, "cos": 1280, "sin": 1536, "swap": 1792, "band": 1920}
N_C2 = 2176


def mod_col(m, t, v):
    return 4 * m + 2 * t + v


def build(nc, xs_d, vec_d, rel_d, w_d, fw_d, c0_d, c1_d, c2_d, diff_d, out_d):
    ctx = ExitStack()
    with ctx:
        def sb(name, shape, dt=F32):
            return ctx.enter_context(nc.sbuf_tensor(name, shape, dt))

        sems = {}

        def sem(name):
            if name not in sems:
                sems[name] = ctx.enter_context(nc.semaphore(name))
            return sems[name]

        raw = sb("raw", [P, RAW, CHUNK])
        w_hi = sb("w_hi", [P, SPL, CHUNK], F32R)
        w_lo = sb("w_lo", [P, SPL, CHUNK], F32R)
        h_hi = sb("h_hi", [P, KT, 2 * T], F32R)
        h_lo = sb("h_lo", [P, KT, 2 * T], F32R)
        g_hi = sb("g_hi", [P, 2, T], F32R)
        g_lo = sb("g_lo", [P, 2, T], F32R)
        xs = sb("xs", [P, KT, 2 * T])
        vec = sb("vec", [P, N_VEC])
        c0 = sb("c0", [P, N_C0])
        modv = sb("modv", [P, 4 * N_MOD])
        coef = sb("coef", [P, 48])
        small = sb("small", [P, 64])
        zeros = sb("zeros", [P, 512], BF16)
        rel = sb("rel", [33, 8])
        consts = sb("consts", [P, 4224])
        arena = sb("arena", [P, 10496])
        att = sb("att", [P, 7 * 384])
        rstd = sb("rstd", [P, 2 * T])
        bank = [ctx.enter_context(nc.psum_tensor(f"bank{i}", [P, 512], F32)) for i in range(4)]
        wide = ctx.enter_context(nc.psum_tensor("wide", [P, 4, 512], F32))

        proj = arena[:, 0:6144].rearrange("p (c n) -> p c n", n=512)
        gate = arena[:, 6144:10240]
        norm_tmp = att[:, 0:2048].rearrange("p (k n) -> p k n", n=T)
        trev = consts[:, 0:2048].rearrange("p (h n) -> p h n", n=T)
        c1 = consts[:, 2048:2048 + N_C1]
        urow = consts[0:8, 3584:3968]
        anti8, tri8, all8 = (c1[:, C1[n]:C1[n] + P] for n in ("anti8", "tri8", "all8"))
        past, bound = (c1[:, C1[n]:C1[n] + 384] for n in ("past", "bound"))
        onehot = c1[0:33, C1["onehot"]:C1["onehot"] + 384]
        prob, sb_t, sb_r, sb_e = (att[:, 384 * i:384 * (i + 1)] for i in range(4))
        pt = [att[:, 384 * 4:384 * 5], att[:, 384 * 5:384 * 6]]
        aw = att[:, 384 * 6:384 * 7]
        mix = arena[:, 0:2048]
        mix2 = arena[:, 2048:3072]
        cv = arena[:, 3072:3584].rearrange("p (t n) -> p t n", n=T)
        cg = arena[:, 3584:4096].rearrange("p (t n) -> p t n", n=T)
        c2 = consts[:, 0:N_C2]
        cos_l = c2[:, 0:512].rearrange("p (l n) -> p l n", n=T)
        sin_l = c2[:, 512:1024].rearrange("p (l n) -> p l n", n=T)
        dft_d = c2[:, 1024:1280]
        rope_cos, rope_sin = c2[:, 1280:1536], c2[:, 1536:1792]
        swap = c2[:, 1792:1920]
        band = c2[:, 1920:2176]
        fw = consts[:, N_C2:N_C2 + 512]
        fold = consts[:, N_C2 + 512:N_C2 + 1536].rearrange("p (g c n) -> p g c n", g=4, c=2)
        UW = T + 30
        u_pad = arena[:, 0:4 * 2 * UW].rearrange("p (t s n) -> p t s n", t=4, s=2)
        b_val = arena[:, 2304:4352].rearrange("p (t n) -> p t n", n=512)
        sgate = arena[:, 4352:8448].rearrange("p (t n) -> p t n", n=512)
        conv = arena[:, 8448:10496].rearrange("p (t n) -> p t n", n=512)
        ln_tmp = arena[:, 0:2048].rearrange("p (t n) -> p t n", n=512)
        glu = arena[:, 8448:9472].rearrange("p (t n) -> p t n", n=512)
        y_b = b_val
        four = [att[:, 0:512], att[:, 512:1024]]
        conv_tmp = att[:, 1024:1536].rearrange("p (s n) -> p s n", s=2)
        q_raw = arena[:, 0:1024]
        q_rot = arena[:, 1024:2048].rearrange("p (t n) -> p t n", n=T)
        k_all = arena[:, 2048:2560]
        k_raw = arena[:, 2560:2816]
        v_tok = arena[:, 3072:3584].rearrange("p (t n) -> p t n", n=P)
        rot_tmp = arena[:, 3584:4608]
        ccx = arena[:, 4608:4608 + 4 * 258].rearrange("p (t n) -> p t n", n=258)
        cb = arena[:, 5696:6720].rearrange("p (t n) -> p t n", n=T)
        cg_ag = arena[:, 6720:8768].rearrange("p (t n) -> p t n", n=T)
        y_c = arena[:, 8768:9792].rearrange("p (t n) -> p t n", n=T)
        w_prob = [att[:, 0:512], att[:, 512:1024]]
        w_pt = [att[:, 1024:1536], att[:, 1536:2048]]

        def col(name, i):
            return vec[:, bass.ds(VEC[name] + i, 1)]

        def modc(m, t, v=0):
            return modv[:, mod_col(m, t, v):mod_col(m, t, v) + 1]

        def shift_col(base, k, v=0):
            return modc(base + k // 2, k % 2, v)

        ADA_SC_M, ADA_SH_M, ADA_GT_M, ADA_SH_F, ADA_SC_F, ADA_GT_F = 0, 4, 8, 12, 16, 20
        E_SC, E_SH, E_GT, O_SC, O_SH, O_GT = 24, 28, 32, 36, 40, 44

        def mod_row(base, v):
            return modv[:, 4 * base:4 * base + 16].rearrange("p (k v) -> p k v", v=2)[:, :, v]

        class Steps:

            def __init__(self, eng, name):
                self.eng, self.sem, self.base, self.off = eng, sem(name), 0, 0

            def mark(self, ins):
                self.base += 1
                ins.then_inc(self.sem, 1)

            def value(self):
                return self.off + self.base

            def wait(self):
                self.eng.wait_ge(self.sem, self.value())

            def enter(self, i, per):
                self.off, self.per, self.start = i * per, per, self.base

            def leave(self, count):
                assert self.base - self.start == self.per, (self.base, self.start, self.per)
                self.base = self.start + self.per * count
                self.off = 0

        NORMS = {"mix": (0, 0, (ADA_SH_M, 0)), "ffn": (0, 8, (ADA_SH_F, 0)),
                 "even_ctx": (1, 24, (E_SH, 1)), "even_x": (0, 16, (E_SH, 0)),
                 "odd_x": (0, 32, (O_SH, 0)), "odd_ctx": (1, 40, (O_SH, 1)),
                 "final": (0, None, None), "last": (0, None, None)}

        block = ctx.enter_context(nc.Block())

        @block.sync
        def _(sp):
            def load(r, slot, freed=None):
                if freed is not None:
                    sp.wait_ge(sem("lo_done" if freed[0] == "lin" else "mod_done"), freed[1] + 1)
                src = w_d[bass.ds(r, 1), :, :].rearrange("a p n -> (a p) n")
                sp.dma_start(raw[:, slot, :], src).then_inc(sem(f"arrived{slot}"), 16)

            for r in range(MOD_FIRST + 4):
                load(r, r % RAW, ORDER[r - RAW] if r >= RAW else None)
            with sp.Fori(0, (LIN_FFN - 2) // 2) as i:
                for n in range(4):
                    m_or_j = 2 * i + (MOD_FIRST if n % 2 == 0 else 0) + n // 2
                    load(4 * i + MOD_FIRST + 4 + n, (MOD_FIRST + n) % RAW, ("mod" if n % 2 == 0 else "lin", m_or_j))
            r0 = MOD_FIRST + 2 * LIN_FFN
            for r in range(r0, r0 + 3):
                load(r, r % RAW, ORDER[r - RAW])
            with sp.Fori(0, FF_STEPS - 1) as i:
                for n, (kind, first, step) in enumerate((("lin", LIN_FFN - 1, 3), ("lin", LIN_FFN, 3),
                                                         ("mod", MOD_FIRST + LIN_FFN, 1), ("lin", LIN_FFN + 1, 3))):
                    load(4 * i + r0 + 3 + n, (r0 + 3 + n) % RAW, (kind, step * i + first))
            r1 = r0 + 3 + 4 * (FF_STEPS - 1)
            for r in range(r1, len(ORDER)):
                load(r, r % RAW, ORDER[r - RAW])
            for half in range(2):
                sp.wait_ge(sem("last_done"), 4 * (half + 1))
                sp.dma_start(out_d[:, 4 * half:4 * half + 4, :], xs[:, 4 * half:4 * half + 4, 0:T]).then_inc(sem("stored"), 16)
            sp.wait_ge(sem("stored"), 32)

        @block.gpsimd
        def _(pool):
            me = Steps(pool, "pool_steps")
            pool.memset(zeros[:, :], 0.0).then_inc(sem("zeros_set"), 1)
            for h in range(NH):
                pool.wait_ge(sem("sb_ln"), h + 1)
                pool.wait_ge(sem("sb_relu"), h + 1)
                if h == 0:
                    pool.wait_ge(sem("c1_loaded"), 16)
                nc.gpsimd.tensor_tensor(sb_r, sb_r, sb_t, ALU.add).then_inc(sem("sb_sum"), 1)
                pool.wait_ge(sem("sb_sum"), h + 1)
                nc.gpsimd.tensor_tensor(sb_r, sb_r, past, ALU.mult).then_inc(sem("sb_kept"), 1)
            pool.wait_ge(sem("ffn_mult"), FF_STEPS)
            pool.wait_ge(sem("ffn_down_evac"), 8)
            pool.memset(u_pad[:, :, :, 0:15], 0.0).then_inc(sem("pads_set"), 1)
            pool.memset(u_pad[:, :, :, 15 + T:UW], 0.0).then_inc(sem("pads_set"), 1)
            t = 3
            pool.wait_ge(sem("glu_done"), 2)
            pool.wait_ge(sem("pads_set"), 2)
            acc = conv[:, t, :].rearrange("p (s n) -> p s n", s=2)
            me.mark(nc.gpsimd.tensor_scalar(acc, u_pad[:, t, :, 0:T], col("a_conv_w", t), col("a_conv_b", t),
                                            ALU.mult, ALU.add))
            for k in range(1, 31):
                me.mark(nc.gpsimd.tensor_scalar(conv_tmp, u_pad[:, t, :, k:k + T], col("a_conv_w", 4 * k + t), None,
                                                ALU.mult))
                me.wait()
                last = nc.gpsimd.tensor_tensor(acc, acc, conv_tmp, ALU.add)
                if k < 30:
                    me.mark(last)
                    me.wait()
            last.then_inc(sem("conv_pool"), 1)

        @block.scalar
        def _(act):
            me = Steps(act, "act_steps")
            act.dma_start(vec[:, :], vec_d).then_inc(sem("vec_loaded"), 16)
            act.dma_start(c0[:, :], c0_d).then_inc(sem("c0_loaded"), 16)
            act.dma_start(xs[:, :, 0:T], xs_d[:, :, 0:T]).then_inc(sem("x_loaded"), 16)
            act.dma_start(rel[0:32, :], rel_d).then_inc(sem("rel_loaded"), 16)
            act.dma_start(c1, c1_d).then_inc(sem("c1_loaded"), 16)
            act.dma_start(xs[:, :, T:2 * T], xs_d[:, :, T:2 * T]).then_inc(sem("ctx_loaded"), 16)

            def split(j, slot=None, rslot=None, arrived=None):
                if isinstance(j, int):
                    if j >= N_LIN:
                        return
                    r = RAW_OF_LIN[j]
                    slot, rslot, arrived = j % SPL, r % RAW, 16 * (r // RAW + 1)
                act.wait_ge(sem(f"arrived{rslot}"), arrived)
                if not isinstance(j, int) or j >= SPL:
                    act.wait_ge(sem("lin_done"), j - (SPL - 1))
                nc.scalar.copy(w_hi[:, slot, :], raw[:, rslot, :]).then_inc(sem("hi_done"), 1)

            def rms(name, n_before, ready, tmp):
                s = NORMS[name][0]
                for (sname, v) in ready:
                    act.wait_ge(sem(sname), v)
                nc.scalar.activation(tmp, xs[:, :, s * T:(s + 1) * T], ACT.Square).then_inc(sem("squares"), 1)
                act.wait_ge(sem("sumsq"), n_before + 1)
                out = rstd[:, s * T:(s + 1) * T]
                me.mark(nc.scalar.activation(out, bank[2][:, s * T:(s + 1) * T], ACT.Ln, bias=EPS_AP, scale=1.0 / D))
                me.wait()
                nc.scalar.activation(out, out, ACT.Exp, scale=-0.5).then_inc(sem("rstd_ready"), 1)

            def shift_hi(name, tiles_before, tmp):
                s, _, (sh, v) = NORMS[name]
                for k in range(KT):
                    act.wait_ge(sem("normed"), tiles_before + k + 1)
                    nc.scalar.activation(h_hi[:, k, s * T:(s + 1) * T], tmp[:, k, :], ACT.Identity,
                                         bias=shift_col(sh, k, v), scale=1.0).then_inc(sem("norm_hi"), 1)

            eps_col = small[:, 63:64]
            EPS_AP = eps_col
            act.wait_ge(sem("vec_loaded"), 16)
            nc.scalar.activation(vec[:, VEC["cact"]:VEC["cact"] + 32], vec[:, VEC["cact"]:VEC["cact"] + 32],
                                 ACT.Silu).then_inc(sem("cact_ready"), 1)
            act.wait_ge(sem("bias_row"), 1)
            nc.scalar.copy(urow, bank[0][0:8, 0:384]).then_inc(sem("bias_row_out"), 1)
            act.wait_ge(sem("bias_row_out"), 1)
            act.dma_start(diff_d, urow).then_inc(sem("bias_stored"), 16)
            act.wait_ge(sem("bias_stored"), 16)
            skew = bass.AP(diff_d.tensor, 0, [[1, P], [384, 8], [1, T]])
            act.dma_start(trev, skew).then_inc(sem("trev_loaded"), 16)
            act.wait_ge(sem("eps_set"), 1)
            rms("mix", 0, [("x_loaded", 16)], norm_tmp)
            shift_hi("mix", 0, norm_tmp)
            split(0)
            split(1)
            with act.Fori(0, 2) as i:
                for n in range(6):
                    j = 6 * i + n
                    r_ahead = MOD_FIRST + 2 * (n + 2) + 1
                    split(j + 2, (n + 2) % SPL, r_ahead % RAW, 48 * i + 16 * (r_ahead // RAW + 1))
                    act.wait_ge(sem("lin_done"), j + 1)
                    nc.scalar.copy(proj[:, bass.ds(j, 1), :].rearrange("p a n -> p (a n)"),
                                   bank[n % 2][:, :]).then_inc(sem("proj_evac"), 1)
            for h in range(NH):
                j = LIN_GATE + h
                split(j + 2)
                act.wait_ge(sem("qk_done"), h + 1)
                if h:
                    act.wait_ge(sem("sb_sum"), h)
                me.mark(nc.scalar.activation(sb_t, wide[:, 2, 0:384], ACT.Abs))
                me.wait()
                me.mark(nc.scalar.activation(sb_t, sb_t, ACT.Exp, scale=-QK))
                me.wait()
                nc.scalar.activation(sb_t, sb_t, ACT.Ln, bias=1.0).then_inc(sem("sb_ln"), 1)
                if h:
                    act.wait_ge(sem("e_done"), h)
                nc.scalar.activation(sb_r, wide[:, 2, 0:384], ACT.Relu, scale=QK).then_inc(sem("sb_relu"), 1)
                act.wait_ge(sem("neg_max"), h + 1)
                if h:
                    act.wait_ge(sem("pt_done"), h)
                for qt, (a, b) in enumerate(((0, 128), (128, 384))):
                    nc.scalar.activation(prob[:, a:b], wide[:, 0, a:b], ACT.Exp, bias=small[:, 2 + qt:3 + qt], scale=QK,
                                         accum_out=small[:, 4 + qt:5 + qt]).then_inc(sem("exp_done"), 1)
                act.wait_ge(sem("lin_done"), j + 1)
                nc.scalar.copy(gate[:, 512 * h:512 * (h + 1)], bank[j % 2][:, :]).then_inc(sem("gate_evac"), 1)
                if h >= 2 and h % 2 == 0:
                    pair_hi = h // 2 - 1
                    act.wait_ge(sem("pv_done"), h)
                    nc.scalar.copy(h_hi[:, pair_hi::4, T:2 * T],
                                   wide[:, 3, :].rearrange("p (a n) -> p a n", a=2)).then_inc(sem("att_hi"), 1)
                act.wait_ge(sem("pt_done"), h + 1)
                if h >= 2:
                    act.wait_ge(sem("pv_done"), h - 1)
                nc.scalar.copy(pt[h % 2], wide[:, 1, 0:384]).then_inc(sem("pt_ready"), 1)
                act.wait_ge(sem("sb_min"), h + 1)
                if h:
                    act.wait_ge(sem("pv_done"), h)
                nc.scalar.activation(aw, sb_e, ACT.Exp, scale=QK).then_inc(sem("aw_ready"), 1)
            act.wait_ge(sem("pv_done"), NH)
            nc.scalar.copy(h_hi[:, 3::4, T:2 * T], wide[:, 3, :].rearrange("p (a n) -> p a n", a=2)).then_inc(sem("att_hi"), 1)
            act.wait_ge(sem("gate_evac"), NH)
            nc.scalar.activation(gate, gate, ACT.Sigmoid).then_inc(sem("gates_ready"), 1)
            act.wait_ge(sem("e_done"), NH)
            act.wait_ge(sem("qk_done"), NH)
            act.wait_ge(sem("sb_kept"), NH)
            act.wait_ge(sem("sb_min"), NH)
            act.dma_start(c2, c2_d).then_inc(sem("c2_loaded"), 16)
            act.dma_start(fw, fw_d).then_inc(sem("c2_loaded"), 16)
            for i in range(4):
                split(LIN_BR + i + 2)
                if i % 2:
                    n = i // 2
                    act.wait_ge(sem("mixed"), n + 1)
                    nc.scalar.copy(h_hi[:, 4 * n:4 * n + 4, 0:T],
                                   mix[:, 1024 * n:1024 * (n + 1)].rearrange("p (k n) -> p k n", n=T)).then_inc(sem("mixed_hi"), 1)
            for i in range(4):
                split(LIN_OUT + i + 2)
            rms("ffn", 1, [("out_evac", 8)], norm_tmp)
            shift_hi("ffn", 8, norm_tmp)

            def conv_first(which, dst, c):
                for t in range(2):
                    tile = 2 * c + t + (22 if which else 0)
                    nc.scalar.activation(dst[:, t, :], bank[which][:, t * T:(t + 1) * T], ACT.Identity,
                                         bias=col("b_conv", tile), scale=col("w_conv", 88 + tile)).then_inc(sem("tap2"), 1)

            split(LIN_FFN + 2)
            act.wait_ge(sem("lin_done"), LIN_FFN + 1)
            conv_first(0, cv, 0)
            split(LIN_FFN + 3)
            act.wait_ge(sem("lin_done"), LIN_FFN + 2)
            conv_first(1, cg, 0)
            act.wait_ge(sem("gate_conv"), 1)
            nc.scalar.activation(cg, cg, ACT.Gelu_apprx_tanh).then_inc(sem("gelu_done"), 1)
            act.wait_ge(sem("ffn_mult"), 1)
            nc.scalar.copy(g_hi[:, :, :], cv).then_inc(sem("g_hi_done"), 1)
            j0, r0 = LIN_FFN + 2, RAW_OF_LIN[LIN_FFN + 2]
            with act.Fori(0, FF_STEPS - 1) as i:
                j = 3 * i + j0
                split(j + 2, (j0 + 2) % SPL, (r0 + 3) % RAW, 16 * i + 16 * ((r0 + 3) // RAW + 1))
                act.wait_ge(sem("lin_done"), j + 1)
                act.wait_ge(sem("g_lo_done"), i + 1)
                conv_first(0, cv, i + 1)
                split(j + 3, (j0 + 3) % SPL, (r0 + 4) % RAW, 16 * i + 16 * ((r0 + 4) // RAW + 1))
                act.wait_ge(sem("lin_done"), j + 2)
                conv_first(1, cg, i + 1)
                act.wait_ge(sem("gate_conv"), i + 2)
                nc.scalar.activation(cg, cg, ACT.Gelu_apprx_tanh).then_inc(sem("gelu_done"), 1)
                split(j + 4, (j0 + 4) % SPL, (r0 + 5) % RAW, 16 * i + 16 * ((r0 + 5) // RAW + 1))
                act.wait_ge(sem("ffn_mult"), i + 2)
                act.wait_ge(sem("lin_done"), j + 3)
                nc.scalar.copy(g_hi[:, :, :], cv).then_inc(sem("g_hi_done"), 1)
            split(LIN_EIN + 1)
            rms("even_ctx", 2, [("ctx_loaded", 16)], norm_tmp)
            shift_hi("even_ctx", 16, norm_tmp)
            rms("final", 3, [("ffn_down_evac", 8)], norm_tmp)
            rms("even_x", 4, [("final_scaled", 8)], norm_tmp)
            shift_hi("even_x", 24, norm_tmp)

            act.wait_ge(sem("fold_done"), 1)
            nc.scalar.copy(fold[:, :, 0, :], bank[0][:, :].rearrange("p (g n) -> p g n", g=4)).then_inc(sem("fold_ready"), 1)
            nc.scalar.copy(fold[:, :, 1, :], bank[1][:, :].rearrange("p (g n) -> p g n", g=4)).then_inc(sem("fold_ready"), 1)

            def chunk_banks(i):
                b = 2 * (i % 2)
                return wide[:, b:b + 2, :]

            def fourier_evac(n):
                act.wait_ge(sem("four_a"), n + 1)
                if n >= 2:
                    act.wait_ge(sem("four_b"), n - 1)
                nc.scalar.copy(four[n % 2], bank[0][:, :]).then_inc(sem("four_ready"), 1)

            def fourier_out(n):
                act.wait_ge(sem("four_b"), n + 1)
                g, s = n // 2, n % 2
                nc.scalar.copy(y_b[:, g, s * T:(s + 1) * T], bank[1][:, 0:T]).then_inc(sem("y_b_raw"), 1)

            for i in range(10):
                split(LIN_EIN + i + 2)
                act.wait_ge(sem("lin_done"), LIN_EIN + i + 1)
                src = chunk_banks(i)
                if i < 2:
                    ins = nc.scalar.copy(b_val[:, 2 * i:2 * i + 2, :], src)
                elif i < 6 and i % 2 == 0:
                    t = i - 2
                    ins = nc.scalar.copy(u_pad[:, t:t + 2, :, 15:15 + T], src.rearrange("p t (s n) -> p t s n", s=2))
                elif i < 6:
                    if i == 5:
                        act.wait_ge(sem("glu_done"), 1)
                    ins = nc.scalar.activation(glu, src, ACT.Sigmoid)
                else:
                    t = 2 * (i - 6)
                    ins = nc.scalar.activation(sgate[:, t:t + 2, :], src, ACT.Silu)
                ins.then_inc(sem("ein_evac"), 1)
                if i >= 2:
                    fourier_evac(i - 2)
                if i >= 3:
                    fourier_out(i - 3)
            fourier_out(7)
            act.wait_ge(sem("centered"), 4)
            nc.scalar.activation(ln_tmp, conv, ACT.Square).then_inc(sem("ln_squares"), 1)
            act.wait_ge(sem("ln_sumsq"), 1)
            me.mark(nc.scalar.activation(rstd[:, :], bank[3][:, :], ACT.Ln, bias=EPS_AP, scale=1.0 / 512))
            me.wait()
            nc.scalar.activation(rstd[:, :], rstd[:, :], ACT.Exp, scale=-0.5).then_inc(sem("ln_rstd"), 1)
            act.wait_ge(sem("ln_scaled"), 1)
            for t in range(4):
                nc.scalar.activation(conv[:, t, :], conv[:, t, :], ACT.Silu, bias=col("ln_b", t),
                                     scale=col("ln_g", t)).then_inc(sem("u_silu"), 1)
            for t in range(4):
                act.wait_ge(sem("u_silu"), t + 1)
                nc.scalar.copy(h_hi[:, 4 + t, :], conv[:, t, :]).then_inc(sem("u_hi"), 1)
            split(LIN_PW + 2)
            for t in range(4):
                act.wait_ge(sem("y_a"), t + 1)
                nc.scalar.copy(h_hi[:, t, :], ln_tmp[:, t, :]).then_inc(sem("y_hi"), 1)
            act.wait_ge(sem("y_b"), 1)
            nc.scalar.copy(h_hi[:, 4:8, :], y_b).then_inc(sem("y_hi"), 1)
            for i in range(4):
                split(LIN_EOUT + i + 2)
            rms("odd_x", 5, [("eout_evac", 16)], norm_tmp)
            shift_hi("odd_x", 32, norm_tmp)
            rms("odd_ctx", 6, [("norm_lo", 5 * KT)], norm_tmp)
            shift_hi("odd_ctx", 40, norm_tmp)
            for i in range(3):
                j = LIN_OIN + i
                split(j + 2)
                act.wait_ge(sem("lin_done"), j + 1)
                if i < 2:
                    nc.scalar.copy(q_raw[:, 512 * i:512 * (i + 1)], wide[:, i, :]).then_inc(sem("q_raw"), 1)
                else:
                    nc.scalar.copy(k_raw, wide[:, 2, 0:T]).then_inc(sem("q_raw"), 1)
                    nc.scalar.copy(k_all[:, T:2 * T], wide[:, 2, T:2 * T]).then_inc(sem("kv_evac"), 1)
                    nc.scalar.copy(v_tok, wide[:, 3, :].rearrange("p (t n) -> p t n", n=P)).then_inc(sem("kv_evac"), 1)

            def window_pt(u):
                act.wait_ge(sem("wt_done"), u + 1)
                if u >= 2:
                    act.wait_ge(sem("wpv_done"), u - 1)
                nc.scalar.copy(w_pt[u % 2], bank[2 + u % 2][:, :]).then_inc(sem("wpt_ready"), 1)

            for u in range(18):
                if u < 10:
                    split(LIN_OIN + 3 + u + 2)
                if u < 16:
                    act.wait_ge(sem("wneg_max"), u + 1)
                    if u >= 2:
                        act.wait_ge(sem("wt_done"), u - 1)
                    nb = small[:, 16 + u:17 + u]
                    nc.scalar.activation(w_prob[u % 2], bank[u % 2][:, :], ACT.Exp, bias=nb, scale=QK,
                                         accum_out=small[:, 32 + 2 * (u % 2):33 + 2 * (u % 2)]).then_inc(sem("wexp"), 1)
                    t, b = (u // 2) % 4, u // 8
                    nc.scalar.activation(small[:, 33 + 2 * (u % 2):34 + 2 * (u % 2)], nb, ACT.Exp, scale=1.0,
                                         bias=col("sink", t + 4 * b)).then_inc(sem("wexp"), 1)
                if u < 10:
                    act.wait_ge(sem("lin_done"), LIN_OIN + 3 + u + 1)
                    src = wide[:, u % 2, :].rearrange("p (t n) -> p t n", n=T)
                    t = 2 * ((u // 2) % 2) if u < 4 else 2 * (u % 2)
                    if u < 4 and u % 2 == 0:
                        nc.scalar.copy(ccx[:, t:t + 2, 1:1 + T], src).then_inc(sem("oin_evac"), 1)
                    elif u in (4, 5):
                        nc.scalar.copy(cb[:, t:t + 2, :], src).then_inc(sem("oin_evac"), 1)
                    elif u >= 6:
                        nc.scalar.copy(cg_ag[:, 2 * (u - 6):2 * (u - 6) + 2, :], src).then_inc(sem("oin_evac"), 1)
                if 1 <= u < 17:
                    window_pt(u - 1)
            me.mark(nc.scalar.activation(cg_ag, cg_ag, ACT.Silu))
            me.wait()
            nc.scalar.copy(small[:, 62:63], small[:, 63:64]).then_inc(sem("silu_gates"), 1)
            act.wait_ge(sem("y_c"), 1)
            nc.scalar.copy(h_hi[:, 0:4, 0:T], y_c).then_inc(sem("yo_hi"), 1)
            act.wait_ge(sem("y_d"), 1)
            nc.scalar.copy(h_hi[:, 4:8, 0:T], rot_tmp.rearrange("p (t n) -> p t n", n=T)).then_inc(sem("yo_hi"), 1)
            for i in range(4):
                split(LIN_OOUT + i + 2)
            rms("last", 7, [("oout_evac", 8)], norm_tmp)

        @block.vector
        def _(dve):
            me = Steps(dve, "dve_steps")

            def split(j, slot=None, rslot=None):
                if isinstance(j, int):
                    if j >= N_LIN:
                        return
                    slot, rslot = j % SPL, RAW_OF_LIN[j] % RAW
                dve.wait_ge(sem("hi_done"), j + 1)
                nc.vector.tensor_tensor(w_lo[:, slot, :], raw[:, rslot, :], w_hi[:, slot, :].bitcast(F32),
                                        ALU.subtract).then_inc(sem("lo_done"), 1)

            def coefficients(at, gain, scale_cols):
                nc.vector.scalar_tensor_tensor(coef[:, at:at + 8], scale_cols, 1.0, vec[:, VEC[gain]:VEC[gain] + 8],
                                               ALU.add, ALU.mult).then_inc(sem("coef_ready"), 1)

            def mod_evac(m0, m1, done):
                dve.wait_ge(sem("mod_done"), done)
                a, b = 4 * m0, 4 * m1
                nc.vector.tensor_tensor(modv[:, a:b], bank[3][:, a:b], vec[:, VEC["mod_bias"] + a:VEC["mod_bias"] + b],
                                        ALU.add).then_inc(sem("mod_read"), 1)
                dve.wait_ge(sem("mod_read"), 1 if m0 == 0 else 2 if m0 < 24 else 3)

            def norm(name, n_before, tiles_before, tmp, coefs_before):
                s, at, (sh, v) = NORMS[name]
                dve.wait_ge(sem("rstd_ready"), n_before + 1)
                dve.wait_ge(sem("coef_ready"), coefs_before)
                for k in range(KT):
                    nc.vector.scalar_tensor_tensor(tmp[:, k, :], xs[:, k, s * T:(s + 1) * T], coef[:, at + k:at + k + 1],
                                                   rstd[:, s * T:(s + 1) * T], ALU.mult, ALU.mult).then_inc(sem("normed"), 1)
                for k in range(KT):
                    dve.wait_ge(sem("norm_hi"), tiles_before + k + 1)
                    nc.vector.scalar_tensor_tensor(h_lo[:, k, s * T:(s + 1) * T], tmp[:, k, :], shift_col(sh, k, v),
                                                   h_hi[:, k, s * T:(s + 1) * T].bitcast(F32),
                                                   ALU.add, ALU.subtract).then_inc(sem("norm_lo"), 1)

            nc.vector.memset(rel[32:33, :], 1.0).then_inc(sem("rel_one"), 1)
            nc.vector.memset(small[:, 63:64], EPS).then_inc(sem("eps_set"), 1)
            dve.wait_ge(sem("vec_loaded"), 16)
            mod_evac(0, 8, 8)
            coefficients(0, "g_mix", mod_row(ADA_SC_M, 0))
            norm("mix", 0, 0, norm_tmp, 1)
            split(0)
            split(1)
            with dve.Fori(0, 2) as i:
                for n in range(6):
                    split(6 * i + n + 2, (n + 2) % SPL, (MOD_FIRST + 2 * (n + 2) + 1) % RAW)
            for h in range(NH):
                j = LIN_GATE + h
                split(j + 2)
                dve.wait_ge(sem("qk_done"), h + 1)
                if h:
                    dve.wait_ge(sem("exp_done"), 2 * h)
                me.mark(nc.vector.reduce_max(small[:, 0:1], wide[:, 0, 0:128], AX_X, negate=True))
                me.mark(nc.vector.reduce_max(small[:, 1:2], wide[:, 0, 128:384], AX_X, negate=True))
                me.wait()
                nc.vector.tensor_scalar(small[:, 2:4], small[:, 0:2], QK, None, ALU.mult).then_inc(sem("neg_max"), 1)
                dve.wait_ge(sem("exp_done"), 2 * h + 2)
                me.mark(nc.vector.reciprocal(small[:, 6:8], small[:, 4:6]))
                me.wait()
                me.mark(nc.vector.tensor_scalar(prob[:, 0:128], prob[:, 0:128], small[:, 6:7], None, ALU.mult))
                nc.vector.tensor_scalar(prob[:, 128:384], prob[:, 128:384], small[:, 7:8], None,
                                        ALU.mult).then_inc(sem("prob_ready"), 1)
                if h >= 2 and h % 2 == 0:
                    pair = h // 2 - 1
                    dve.wait_ge(sem("att_hi"), pair + 1)
                    nc.vector.tensor_tensor(h_lo[:, pair::4, T:2 * T], wide[:, 3, :].rearrange("p (a n) -> p a n", a=2),
                                            h_hi[:, pair::4, T:2 * T].bitcast(F32), ALU.subtract).then_inc(sem("att_lo"), 1)
                dve.wait_ge(sem("e_done"), h + 1)
                if h:
                    dve.wait_ge(sem("aw_ready"), h)
                nc.vector.tensor_tensor(sb_e, bank[2][:, 0:384], bound, ALU.min).then_inc(sem("sb_min"), 1)
            dve.wait_ge(sem("att_hi"), 4)
            nc.vector.tensor_tensor(h_lo[:, 3::4, T:2 * T], wide[:, 3, :].rearrange("p (a n) -> p a n", a=2),
                                    h_hi[:, 3::4, T:2 * T].bitcast(F32), ALU.subtract).then_inc(sem("att_lo"), 1)
            mod_evac(8, 24, MOD_FIRST + 20)
            coefficients(8, "g_ffn", mod_row(ADA_SC_F, 0))
            for i in range(4):
                split(LIN_BR + i + 2)
                n, two = i // 2, i % 2
                dve.wait_ge(sem("lin_done"), LIN_BR + i + 1)
                if i == 0:
                    dve.wait_ge(sem("gates_ready"), 1)
                src = wide[:, 2 * two:2 * two + 2, :].rearrange("p b n -> p (b n)")
                g = gate[:, 2048 * two + 1024 * n:2048 * two + 1024 * (n + 1)]
                m = mix[:, 1024 * n:1024 * (n + 1)]
                if not two:
                    nc.vector.tensor_tensor(m, src, g, ALU.mult).then_inc(sem("br_evac"), 1)
                else:
                    if n:
                        dve.wait_ge(sem("mixed"), n)
                    nc.vector.tensor_tensor(mix2, src, g, ALU.mult).then_inc(sem("br_evac"), 1)
                    dve.wait_ge(sem("br_evac"), i + 1)
                    nc.vector.tensor_tensor(m, m, mix2, ALU.add).then_inc(sem("mixed"), 1)
                    dve.wait_ge(sem("mixed_hi"), n + 1)
                    nc.vector.tensor_tensor(h_lo[:, 4 * n:4 * n + 4, 0:T], m.rearrange("p (k n) -> p k n", n=T),
                                            h_hi[:, 4 * n:4 * n + 4, 0:T].bitcast(F32),
                                            ALU.subtract).then_inc(sem("mixed_lo"), 1)
            for i in range(4):
                split(LIN_OUT + i + 2)
                dve.wait_ge(sem("lin_done"), LIN_OUT + i + 1)
                for t in range(2):
                    k = 2 * i + t
                    nc.vector.scalar_tensor_tensor(xs[:, k, 0:T], bank[i % 2][:, t * T:(t + 1) * T], shift_col(ADA_GT_M, k),
                                                   xs[:, k, 0:T], ALU.mult, ALU.add).then_inc(sem("out_evac"), 1)
            norm("ffn", 1, 8, norm_tmp, 2)

            def conv_taps(which, dst, c, first):
                dve.wait_ge(sem("tap2"), 4 * c + 2 * which + 2)
                for t in range(2):
                    tile = 2 * c + t + (22 if which else 0)
                    me.mark(nc.vector.scalar_tensor_tensor(dst[:, t, 1:T], bank[which][:, t * T:(t + 1) * T - 1],
                                                           col("w_conv", 44 + tile), dst[:, t, 1:T], ALU.mult, ALU.add))
                me.wait()
                for t in range(2):
                    tile = 2 * c + t + (22 if which else 0)
                    ins = nc.vector.scalar_tensor_tensor(dst[:, t, 2:T], bank[which][:, t * T:(t + 1) * T - 2],
                                                         col("w_conv", tile), dst[:, t, 2:T], ALU.mult, ALU.add)
                    if t == 0:
                        me.mark(ins)
                ins.then_inc(sem("gate_conv" if which else "value_conv"), 1)

            def ffn_product(c):
                dve.wait_ge(sem("gelu_done"), c + 1)
                dve.wait_ge(sem("value_conv"), c + 1)
                nc.vector.tensor_tensor(cv, cv, cg, ALU.mult).then_inc(sem("ffn_mult"), 1)
                dve.wait_ge(sem("g_hi_done"), c + 1)
                nc.vector.tensor_tensor(g_lo[:, :, :], cv, g_hi[:, :, :].bitcast(F32), ALU.subtract).then_inc(sem("g_lo_done"), 1)

            split(LIN_FFN + 2)
            conv_taps(0, cv, 0, True)
            split(LIN_FFN + 3)
            conv_taps(1, cg, 0, True)
            ffn_product(0)
            j0, r0 = LIN_FFN + 2, RAW_OF_LIN[LIN_FFN + 2]
            with dve.Fori(0, FF_STEPS - 1) as i:
                me.enter(i, 6)
                j = 3 * i + j0
                split(j + 2, (j0 + 2) % SPL, (r0 + 3) % RAW)
                conv_taps(0, cv, i + 1, False)
                split(j + 3, (j0 + 3) % SPL, (r0 + 4) % RAW)
                conv_taps(1, cg, i + 1, False)
                split(j + 4, (j0 + 4) % SPL, (r0 + 5) % RAW)
                ffn_product(i + 1)
            me.leave(FF_STEPS - 1)
            mod_evac(24, 48, 48)
            coefficients(16, "e_norm", mod_row(E_SC, 0))
            coefficients(24, "e_norm", mod_row(E_SC, 1))
            coefficients(32, "o_norm", mod_row(O_SC, 0))
            coefficients(40, "o_norm", mod_row(O_SC, 1))
            split(LIN_EIN + 1)
            norm("even_ctx", 2, 16, norm_tmp, 6)
            dve.wait_ge(sem("lin_done"), LIN_EIN)
            for k in range(KT):
                nc.vector.scalar_tensor_tensor(xs[:, k, 0:T], wide[:, k // 2, (k % 2) * T:(k % 2 + 1) * T],
                                               shift_col(ADA_GT_F, k), xs[:, k, 0:T], ALU.mult,
                                               ALU.add).then_inc(sem("ffn_down_evac"), 1)
            dve.wait_ge(sem("rstd_ready"), 4)
            for k in range(KT):
                nc.vector.scalar_tensor_tensor(xs[:, k, 0:T], xs[:, k, 0:T], col("g_final", k), rstd[:, 0:T],
                                               ALU.mult, ALU.mult).then_inc(sem("final_scaled"), 1)
            norm("even_x", 4, 24, norm_tmp, 6)
            def conv_dve(t):
                acc = conv[:, t, :].rearrange("p (s n) -> p s n", s=2)
                me.mark(nc.vector.tensor_scalar(acc, u_pad[:, t, :, 0:T], col("a_conv_w", t), col("a_conv_b", t),
                                                ALU.mult, ALU.add))
                for k in range(1, 31):
                    me.wait()
                    me.mark(nc.vector.scalar_tensor_tensor(acc, u_pad[:, t, :, k:k + T], col("a_conv_w", 4 * k + t), acc,
                                                           ALU.mult, ALU.add))

            for i in range(10):
                split(LIN_EIN + i + 2)
                if i in (3, 5):
                    t = i - 3
                    dve.wait_ge(sem("ein_evac"), i + 1)
                    dst = u_pad[:, t:t + 2, :, 15:15 + T]
                    nc.vector.tensor_tensor(dst, dst, glu.rearrange("p t (s n) -> p t s n", s=2),
                                            ALU.mult).then_inc(sem("glu_done"), 1)
                if i == 6:
                    dve.wait_ge(sem("glu_done"), 2)
                    dve.wait_ge(sem("pads_set"), 2)
                if i in (6, 7, 8):
                    conv_dve(i - 6)
            me.wait()
            nc.vector.tensor_copy(small[:, 61:62], small[:, 63:64]).then_inc(sem("conv_dve"), 1)
            dve.wait_ge(sem("y_b_raw"), 8)
            dve.wait_ge(sem("ein_evac"), 10)
            nc.vector.tensor_tensor(y_b, y_b, sgate[:, 4:8, :], ALU.mult).then_inc(sem("y_b"), 1)
            dve.wait_ge(sem("ln_sum"), 1)
            for t in range(4):
                nc.vector.scalar_tensor_tensor(conv[:, t, :], bank[2][:, :], -1.0 / 512, conv[:, t, :],
                                               ALU.mult, ALU.add).then_inc(sem("centered"), 1)
            dve.wait_ge(sem("ln_rstd"), 1)
            for t in range(4):
                ins = nc.vector.tensor_tensor(conv[:, t, :], conv[:, t, :], rstd[:, :], ALU.mult)
                if t < 3:
                    me.mark(ins)
            ins.then_inc(sem("ln_scaled"), 1)
            for t in range(4):
                dve.wait_ge(sem("u_hi"), t + 1)
                nc.vector.tensor_tensor(h_lo[:, 4 + t, :], conv[:, t, :], h_hi[:, 4 + t, :].bitcast(F32),
                                        ALU.subtract).then_inc(sem("u_lo"), 1)
            split(LIN_PW + 2)
            dve.wait_ge(sem("lin_done"), LIN_PW + 1)
            for t in range(4):
                nc.vector.scalar_tensor_tensor(ln_tmp[:, t, :], wide[:, t, :], col("pw_b", t), sgate[:, t, :],
                                               ALU.add, ALU.mult).then_inc(sem("y_a"), 1)
            for t in range(4):
                dve.wait_ge(sem("y_hi"), t + 1)
                nc.vector.tensor_tensor(h_lo[:, t, :], ln_tmp[:, t, :], h_hi[:, t, :].bitcast(F32),
                                        ALU.subtract).then_inc(sem("y_lo"), 1)
            dve.wait_ge(sem("y_hi"), 5)
            nc.vector.tensor_tensor(h_lo[:, 4:8, :], y_b, h_hi[:, 4:8, :].bitcast(F32), ALU.subtract).then_inc(sem("y_lo"), 1)
            for i in range(4):
                split(LIN_EOUT + i + 2)
                dve.wait_ge(sem("lin_done"), LIN_EOUT + i + 1)
                for t in range(2):
                    for s in range(2):
                        k = 2 * i + t
                        c = slice(s * T, (s + 1) * T)
                        nc.vector.scalar_tensor_tensor(xs[:, k, c], wide[:, 2 * (i % 2) + t, c], shift_col(E_GT, k, s),
                                                       xs[:, k, c], ALU.mult, ALU.add).then_inc(sem("eout_evac"), 1)
            norm("odd_x", 5, 32, norm_tmp, 6)
            norm("odd_ctx", 6, 40, norm_tmp, 6)
            for i in range(3):
                split(LIN_OIN + i + 2)
            neg_sink = small[:, 8:16]
            me.mark(nc.vector.tensor_scalar(neg_sink, vec[:, VEC["sink"]:VEC["sink"] + 8], -1.0, None, ALU.mult))
            me.mark(nc.vector.memset(ccx[:, :, 0:1], 0.0))
            me.mark(nc.vector.memset(ccx[:, :, T + 1:T + 2], 0.0))
            dve.wait_ge(sem("q_raw"), 3)
            dve.wait_ge(sem("rot_done"), 1)
            for half in range(2):
                for n in range(2):
                    a = slice(512 * half + T * n, 512 * half + T * (n + 1))
                    me.mark(nc.vector.tensor_tensor(rot_tmp[:, a], bank[half][:, T * n:T * (n + 1)], rope_sin, ALU.mult))
                    me.mark(nc.vector.tensor_tensor(q_raw[:, a], q_raw[:, a], rope_cos, ALU.mult))
            me.wait()
            nc.vector.tensor_tensor(q_rot.rearrange("p t n -> p (t n)"), q_raw, rot_tmp, ALU.add).then_inc(sem("roped"), 1)
            me.mark(nc.vector.tensor_tensor(k_raw, k_raw, rope_cos, ALU.mult))
            dve.wait_ge(sem("roped"), 1)
            me.mark(nc.vector.tensor_tensor(rot_tmp[:, 0:T], bank[2][:, 0:T], rope_sin, ALU.mult))
            me.wait()
            nc.vector.tensor_tensor(k_all[:, 0:T], k_raw, rot_tmp[:, 0:T], ALU.add).then_inc(sem("roped"), 1)
            for u in range(16):
                if u < 10:
                    split(LIN_OIN + 3 + u + 2)
                h = (u // 2) % 4 + 4 * (u // 8)
                dve.wait_ge(sem("ws_done"), u + 1)
                me.mark(nc.vector.reduce_max(small[:, 60:61], bank[u % 2][:, :], AX_X, negate=True))
                me.wait()
                nc.vector.tensor_scalar(small[:, 16 + u:17 + u], small[:, 60:61], QK, neg_sink[:, h:h + 1],
                                        ALU.mult, ALU.min).then_inc(sem("wneg_max"), 1)
                if u < 4 and u % 2:
                    t = 2 * (u // 2)
                    dve.wait_ge(sem("lin_done"), LIN_OIN + 3 + u + 1)
                    dve.wait_ge(sem("oin_evac"), u // 2 + 1)
                    dst = ccx[:, t:t + 2, 1:1 + T]
                    nc.vector.tensor_tensor(dst, dst, wide[:, 1, :].rearrange("p (t n) -> p t n", n=T),
                                            ALU.mult).then_inc(sem("ccx_done"), 1)
                dve.wait_ge(sem("wexp"), 2 * u + 2)
                s2 = small[:, 32 + 2 * (u % 2):34 + 2 * (u % 2)]
                den = small[:, 36:37]
                me.mark(nc.vector.tensor_tensor(den, s2[:, 0:1], s2[:, 1:2], ALU.add))
                me.wait()
                me.mark(nc.vector.reciprocal(small[:, 37:38], den))
                me.wait()
                nc.vector.tensor_scalar(w_prob[u % 2], w_prob[u % 2], small[:, 37:38], None,
                                        ALU.mult).then_inc(sem("wprob_ready"), 1)
                if u == 12:
                    dve.wait_ge(sem("ccx_done"), 2)
                    for t in range(4):
                        me.mark(nc.vector.tensor_scalar(y_c[:, t, :], ccx[:, t, 0:T], col("o_conv", t), None, ALU.mult))
                    me.wait()
                    for k in (1, 2):
                        for t in range(4):
                            me.mark(nc.vector.scalar_tensor_tensor(y_c[:, t, :], ccx[:, t, k:k + T], col("o_conv", 4 * k + t),
                                                                   y_c[:, t, :], ALU.mult, ALU.add))
                        me.wait()
                    dve.wait_ge(sem("oin_evac"), 4)
                    me.mark(nc.vector.tensor_tensor(y_c, y_c, cb, ALU.mult))
            dve.wait_ge(sem("silu_gates"), 1)
            me.wait()
            nc.vector.tensor_tensor(y_c, y_c, cg_ag[:, 0:4, :], ALU.mult).then_inc(sem("y_c"), 1)
            dve.wait_ge(sem("wpv_done"), 16)
            nc.vector.tensor_tensor(rot_tmp, wide[:, 2:4, :].rearrange("p b n -> p (b n)"),
                                    cg_ag[:, 4:8, :].rearrange("p t n -> p (t n)"), ALU.mult).then_inc(sem("y_d"), 1)
            for half, src in ((0, y_c), (1, rot_tmp.rearrange("p (t n) -> p t n", n=T))):
                dve.wait_ge(sem("yo_hi"), half + 1)
                nc.vector.tensor_tensor(h_lo[:, 4 * half:4 * half + 4, 0:T], src,
                                        h_hi[:, 4 * half:4 * half + 4, 0:T].bitcast(F32), ALU.subtract).then_inc(sem("yo_lo"), 1)
            for i in range(4):
                split(LIN_OOUT + i + 2)
                dve.wait_ge(sem("lin_done"), LIN_OOUT + i + 1)
                for t in range(2):
                    k = 2 * i + t
                    nc.vector.scalar_tensor_tensor(xs[:, k, 0:T], bank[i % 2][:, t * T:(t + 1) * T], shift_col(O_GT, k),
                                                   xs[:, k, 0:T], ALU.mult, ALU.add).then_inc(sem("oout_evac"), 1)
            dve.wait_ge(sem("rstd_ready"), 8)
            for k in range(KT):
                nc.vector.scalar_tensor_tensor(xs[:, k, 0:T], xs[:, k, 0:T], col("final_norm", k), rstd[:, 0:T],
                                               ALU.mult, ALU.mult).then_inc(sem("last_done"), 1)

        @block.tensor
        def _(pe):
            mm = nc.tensor.matmul
            ident, ones = c0[:, 0:P], c0[:, P:2 * P]
            cact = vec[:, VEC["cact"]:VEC["cact"] + 32].rearrange("p (k v) -> p k v", v=4)

            def mod_chunk(m, slot, arrived, vecs, start=None):
                pe.wait_ge(sem(f"arrived{slot}"), arrived)
                for t in range(2):
                    for k in range(KT):
                        c = 4 * m + 2 * t
                        last = mm(bank[3][:, bass.ds(c, 2)], raw[:, slot, k * 256 + t * P:k * 256 + (t + 1) * P],
                                  cact[:, k, vecs:vecs + 2], start=(k == 0), stop=(k == KT - 1))
                last.then_inc(sem("mod_done"), 1)

            def mod(m):
                r = RAW_OF_MOD[m]
                mod_chunk(m, r % RAW, 16 * (r // RAW + 1), 0 if m < 24 else 2)

            def triple(out, w, x, start, stop, skip=False):
                for n, (a, b) in enumerate(((0, 0), (0, 1), (1, 0))):
                    last = mm(out, w[a], x[b], start=start and n == 0, stop=stop and n == 2, skip_group_check=skip)
                return last

            def whl(slot, a, n):
                return w_hi[:, slot, a:a + n], w_lo[:, slot, a:a + n]

            def hhl(k, a, n):
                return h_hi[:, k, a:a + n], h_lo[:, k, a:a + n]

            def features(j, slot, outs, a, n):
                pe.wait_ge(sem("lo_done"), j + 1)
                for m in range(2):
                    for k in range(KT):
                        last = triple(outs[m], whl(slot, 256 * k + P * m, P), hhl(k, a, n), k == 0, k == KT - 1)
                last.then_inc(sem("lin_done"), 1)

            def tokens(j, slot, outs, a):
                pe.wait_ge(sem("lo_done"), j + 1)
                for m in range(2):
                    for k in range(KT):
                        last = triple(outs[m], hhl(k, a + P * m, P), whl(slot, 256 * k, 256), k == 0, k == KT - 1)
                last.then_inc(sem("lin_done"), 1)

            def halves(b):
                return b[:, 0:T], b[:, T:2 * T]

            def sum_squares(n, src, s):
                pe.wait_ge(sem("squares"), n + 1)
                if n:
                    pe.wait_ge(sem("rstd_ready"), n)
                for k in range(KT):
                    last = mm(bank[2][:, s * T:(s + 1) * T], ones, src[:, k, :], start=(k == 0), stop=(k == KT - 1))
                last.then_inc(sem("sumsq"), 1)

            pe.wait_ge(sem("rel_loaded"), 16)
            pe.wait_ge(sem("rel_one"), 1)
            pe.wait_ge(sem("c1_loaded"), 16)
            mm(bank[0][0:8, 0:384], rel[:, :], onehot, start=True, stop=True).then_inc(sem("bias_row"), 1)
            pe.wait_ge(sem("cact_ready"), 1)
            for m in range(3):
                mod(m)
            pe.wait_ge(sem("c0_loaded"), 16)
            sum_squares(0, norm_tmp, 0)
            for m in range(3, 8):
                mod(m)
            pe.wait_ge(sem("mod_read"), 1)
            mod(8)
            pe.wait_ge(sem("norm_lo"), KT)
            pe.wait_ge(sem("bias_row_out"), 1)
            def qkv_step(i, n):
                j = 6 * i + n
                r = MOD_FIRST + 2 * n
                mod_chunk(j + MOD_FIRST, r % RAW, 48 * i + 16 * (r // RAW + 1), 0)
                if not isinstance(i, int) or j >= 2:
                    pe.wait_ge(sem("proj_evac"), j - 1)
                (features if n < 4 else tokens)(*((j, n % SPL, halves(bank[n % 2])) + ((0, T) if n < 4 else (0,))))

            for n in range(6):
                qkv_step(0, n)
            for n in range(6):
                qkv_step(1, n)

            def q_of(h, branch, a, b):
                t, p0 = h // 2, HD * (h % 2)
                return proj[p0:p0 + HD, 6 * branch + t // 2, (t % 2) * T + a:(t % 2) * T + b]

            def k_of(h, branch, a, b):
                t, p0 = h // 2, HD * (h % 2)
                return proj[p0:p0 + HD, 6 * branch + 2 + t // 2, (t % 2) * T + a:(t % 2) * T + b]

            def v_of(h, branch, m):
                return proj[:, 6 * branch + 4 + h // 4, m * T + (h % 4) * HD:m * T + (h % 4 + 1) * HD]

            def weighted_values(h):
                pe.wait_ge(sem("pt_ready"), h + 1)
                pe.wait_ge(sem("aw_ready"), h + 1)
                if h >= 2 and h % 2 == 0:
                    pe.wait_ge(sem("att_lo"), h // 2)
                p0 = HD * (h % 2)
                for branch, w in ((0, pt[h % 2]), (1, aw)):
                    c = branch * T
                    mm(wide[p0:p0 + HD, 3, c:c + T], v_of(h, branch, 0), w[:, 0:T], start=True, stop=False)
                    last = mm(wide[p0:p0 + HD, 3, c + P:c + T], v_of(h, branch, 1), w[:, T:T + P], start=False, stop=True)
                last.then_inc(sem("pv_done"), 1)

            pe.wait_ge(sem("proj_evac"), 12)
            pe.wait_ge(sem("trev_loaded"), 16)
            for h in range(NH):
                if h:
                    pe.wait_ge(sem("exp_done"), 2 * h)
                    pe.wait_ge(sem("sb_relu"), h)
                mm(wide[:, 0, 0:128], q_of(h, 0, 0, 128), k_of(h, 0, 0, 128), start=True, stop=False)
                mm(wide[:, 0, 0:128], anti8, trev[:, h, 128:256], start=False, stop=True)
                mm(wide[:, 0, 128:384], q_of(h, 0, 128, 256), k_of(h, 0, 0, 256), start=True, stop=False)
                mm(wide[:, 0, 128:384], anti8, trev[:, h, :], start=False, stop=True)
                mm(wide[:, 2, 0:256], k_of(h, 1, 0, 128), q_of(h, 1, 0, 256), start=True, stop=True)
                mm(wide[:, 2, 256:384], k_of(h, 1, 128, 256), q_of(h, 1, 128, 256), start=True,
                   stop=True).then_inc(sem("qk_done"), 1)
                if h:
                    weighted_values(h - 1)
                mod(MOD_FIRST + 12 + h)
                if h >= 2:
                    pe.wait_ge(sem("gate_evac"), h - 1)
                j = LIN_GATE + h
                features(j, j % SPL, halves(bank[j % 2]), 0, T)
                pe.wait_ge(sem("prob_ready"), h + 1)
                if h:
                    pe.wait_ge(sem("pt_ready"), h)
                nc.tensor.transpose(wide[:, 1, 0:128], prob[:, 0:128], ident)
                nc.tensor.transpose(wide[:, 1, 128:256], prob[:, 128:256], ident)
                nc.tensor.transpose(wide[:, 1, 256:384], prob[:, 256:384], ident).then_inc(sem("pt_done"), 1)
                pe.wait_ge(sem("sb_kept"), h + 1)
                if h:
                    pe.wait_ge(sem("sb_min"), h)
                e = bank[2]
                mm(e[:, 0:256], k_of(h, 1, 0, 128), q_of(h, 1, 0, 256), start=True, stop=False)
                mm(e[:, 0:256], tri8, sb_r[:, 0:256], start=False, stop=False)
                mm(e[:, 128:256], all8, sb_r[:, 256:384], start=False, stop=True)
                mm(e[:, 256:384], k_of(h, 1, 128, 256), q_of(h, 1, 128, 256), start=True, stop=False)
                mm(e[:, 256:384], tri8, sb_r[:, 256:384], start=False, stop=True).then_inc(sem("e_done"), 1)
            weighted_values(NH - 1)
            pe.wait_ge(sem("mod_read"), 2)
            for i in range(4):
                j = LIN_BR + i
                mod(MOD_FIRST + 20 + i)
                pe.wait_ge(sem("lo_done"), j + 1)
                if i == 0:
                    pe.wait_ge(sem("att_lo"), 4)
                if i >= 2:
                    pe.wait_ge(sem("br_evac"), i - 1)
                for m in range(4):
                    out = wide[:, 2 * (i % 2) + m // 2, (m % 2) * T:(m % 2 + 1) * T]
                    for k in range(4):
                        last = triple(out, whl(j % SPL, 512 * k + P * m, P), hhl(4 * (i % 2) + k, T, T), k == 0, k == 3)
                last.then_inc(sem("lin_done"), 1)
            pe.wait_ge(sem("mixed_lo"), 2)
            pe.wait_ge(sem("gate_evac"), 8)
            for i in range(4):
                j = LIN_OUT + i
                mod(MOD_FIRST + 24 + i)
                if i >= 2:
                    pe.wait_ge(sem("out_evac"), 2 * (i - 1))
                features(j, j % SPL, halves(bank[i % 2]), 0, T)
            sum_squares(1, norm_tmp, 0)
            pe.wait_ge(sem("zeros_set"), 1)
            for b in range(4):
                mm(wide[:, b, :], zeros[:, 0:P], zeros[:, :], start=True, stop=False, skip_group_check=True)

            def down(j, slot, c):
                pe.wait_ge(sem("lo_done"), j + 1)
                pe.wait_ge(sem("g_lo_done"), c + 1)
                for k in range(2):
                    for m in range(KT):
                        last = triple(wide[:, m // 2, (m % 2) * T:(m % 2 + 1) * T], whl(slot, 1024 * k + P * m, P),
                                      (g_hi[:, k, :], g_lo[:, k, :]), False, True, skip=True)
                last.then_inc(sem("lin_done"), 1)

            pe.wait_ge(sem("norm_lo"), 2 * KT)
            features(LIN_FFN, LIN_FFN % SPL, halves(bank[0]), 0, T)
            mod(MOD_FIRST + 28)
            features(LIN_FFN + 1, (LIN_FFN + 1) % SPL, halves(bank[1]), 0, T)
            j0, r0 = LIN_FFN + 2, RAW_OF_LIN[LIN_FFN + 2]
            with pe.Fori(0, FF_STEPS - 1) as i:
                j = 3 * i + j0
                pe.wait_ge(sem("value_conv"), i + 1)
                features(j, j0 % SPL, halves(bank[0]), 0, T)
                pe.wait_ge(sem("gate_conv"), i + 1)
                features(j + 1, (j0 + 1) % SPL, halves(bank[1]), 0, T)
                mod_chunk(i + MOD_FIRST + 29, (r0 + 2) % RAW, 16 * i + 16 * ((r0 + 2) // RAW + 1), 2)
                down(j + 2, (j0 + 2) % SPL, i)
            sum_squares(2, norm_tmp, 1)
            down(LIN_EIN - 1, (LIN_EIN - 1) % SPL, FF_STEPS - 1)
            sum_squares(3, norm_tmp, 0)
            sum_squares(4, norm_tmp, 0)
            pe.wait_ge(sem("c2_loaded"), 32)
            mm(bank[0][:, :], dft_d[:, 0:P], fw, start=True, stop=True)
            mm(bank[1][:, :], dft_d[:, P:2 * P], fw, start=True, stop=True).then_inc(sem("fold_done"), 1)
            pe.wait_ge(sem("norm_lo"), 4 * KT)

            def fourier_a(n):
                g, s = n // 2, n % 2
                if n:
                    pe.wait_ge(sem("four_ready"), n)
                else:
                    pe.wait_ge(sem("fold_ready"), 2)
                    pe.wait_ge(sem("ein_evac"), 2)
                for lt in range(2):
                    last = mm(bank[0][:, lt * T:(lt + 1) * T], b_val[:, g, s * T + lt * P:s * T + (lt + 1) * P],
                              fold[:, g, :, :].rearrange("p c n -> p (c n)"), start=True, stop=True)
                last.then_inc(sem("four_a"), 1)

            def fourier_b(n):
                pe.wait_ge(sem("four_ready"), n + 1)
                if n:
                    pe.wait_ge(sem("y_b_raw"), n)
                for q, (part, table) in enumerate(((0, cos_l), (1, sin_l))):
                    for lt in range(2):
                        last = mm(bank[1][:, 0:T], four[n % 2][:, lt * T + part * P:lt * T + (part + 1) * P],
                                  table[:, lt, :], start=(q == 0 and lt == 0), stop=(q == 1 and lt == 1))
                last.then_inc(sem("four_b"), 1)

            for i in range(10):
                j = LIN_EIN + i
                b = 2 * (i % 2)
                if i >= 2:
                    pe.wait_ge(sem("ein_evac"), i - 1)
                features(j, j % SPL, (wide[:, b, :], wide[:, b + 1, :]), 0, 2 * T)
                if i >= 2:
                    fourier_a(i - 2)
                if i >= 3:
                    fourier_b(i - 3)
            fourier_b(7)
            pe.wait_ge(sem("conv_dve"), 1)
            pe.wait_ge(sem("conv_pool"), 1)
            pe.wait_ge(sem("rstd_ready"), 5)
            for t in range(4):
                last = mm(bank[2][:, :], ones, conv[:, t, :], start=(t == 0), stop=(t == 3))
            last.then_inc(sem("ln_sum"), 1)
            pe.wait_ge(sem("ln_squares"), 1)
            for t in range(4):
                last = mm(bank[3][:, :], ones, ln_tmp[:, t, :], start=(t == 0), stop=(t == 3))
            last.then_inc(sem("ln_sumsq"), 1)
            pe.wait_ge(sem("u_lo"), 4)
            pe.wait_ge(sem("lo_done"), LIN_PW + 1)
            pe.wait_ge(sem("ein_evac"), 10)
            for m in range(4):
                for k in range(4):
                    last = triple(wide[:, m, :], whl(LIN_PW % SPL, 512 * k + P * m, P), hhl(4 + k, 0, 2 * T), k == 0, k == 3)
            last.then_inc(sem("lin_done"), 1)
            pe.wait_ge(sem("y_lo"), 5)
            for i in range(4):
                j = LIN_EOUT + i
                b = 2 * (i % 2)
                if i >= 2:
                    pe.wait_ge(sem("eout_evac"), 4 * (i - 1))
                features(j, j % SPL, (wide[:, b, :], wide[:, b + 1, :]), 0, 2 * T)
            sum_squares(5, norm_tmp, 0)
            sum_squares(6, norm_tmp, 1)
            pe.wait_ge(sem("norm_lo"), 5 * KT)
            pe.wait_ge(sem("eout_evac"), 16)
            for i in range(2):
                features(LIN_OIN + i, (LIN_OIN + i) % SPL, halves(wide[:, i, :]), 0, T)
            j = LIN_OIN + 2
            pe.wait_ge(sem("norm_lo"), 6 * KT)
            pe.wait_ge(sem("lo_done"), j + 1)
            for k in range(KT):
                triple(wide[:, 2, :], whl(j % SPL, 256 * k, P), hhl(k, 0, 2 * T), k == 0, k == KT - 1)
            for tt in range(4):
                for k in range(KT):
                    last = triple(wide[:, 3, tt * P:(tt + 1) * P], hhl(k, tt * P, P), whl(j % SPL, 256 * k + P, P),
                                  k == 0, k == KT - 1)
            last.then_inc(sem("lin_done"), 1)
            pe.wait_ge(sem("q_raw"), 3)
            pe.wait_ge(sem("rstd_ready"), 7)
            mm(bank[0][:, :], swap, q_raw[:, 0:512], start=True, stop=True)
            mm(bank[1][:, :], swap, q_raw[:, 512:1024], start=True, stop=True)
            mm(bank[2][:, 0:T], swap, k_raw, start=True, stop=True).then_inc(sem("rot_done"), 1)
            pe.wait_ge(sem("roped"), 2)
            pe.wait_ge(sem("kv_evac"), 2)

            def unit(u):
                return (u // 2) % 4, u // 8, u % 2

            for u in range(18):
                if u < 16:
                    t, b, qt = unit(u)
                    p0 = HD * b
                    if u >= 2:
                        pe.wait_ge(sem("wexp"), 2 * (u - 1) - 1)
                    keys = slice(P, 2 * P) if qt == 0 else slice(0, P)
                    mm(bank[u % 2][:, :], q_rot[p0:p0 + HD, t, qt * P:(qt + 1) * P], k_all[p0:p0 + HD, :],
                       start=True, stop=False)
                    mm(bank[u % 2][:, keys], ident, band[:, qt * P:(qt + 1) * P], start=False,
                       stop=True).then_inc(sem("ws_done"), 1)
                if u < 10:
                    j = LIN_OIN + 3 + u
                    if u >= 2:
                        n = u - 2
                        if n < 4 and n % 2:
                            pe.wait_ge(sem("ccx_done"), n // 2 + 1)
                        else:
                            pe.wait_ge(sem("oin_evac"), n // 2 + 1 if n < 4 else n - 1)
                    features(j, j % SPL, halves(wide[:, u % 2, :]), 0, T)
                if 1 <= u < 17:
                    v = u - 1
                    pe.wait_ge(sem("wprob_ready"), v + 1)
                    if v >= 2:
                        pe.wait_ge(sem("wpt_ready"), v - 1)
                    for k in range(4):
                        last = nc.tensor.transpose(bank[2 + v % 2][:, k * P:(k + 1) * P],
                                                   w_prob[v % 2][:, k * P:(k + 1) * P], ident)
                    last.then_inc(sem("wt_done"), 1)
                if u >= 2:
                    v = u - 2
                    t, b, qt = unit(v)
                    pe.wait_ge(sem("wpt_ready"), v + 1)
                    out = wide[HD * b:HD * (b + 1), 2 + t // 2, (t % 2) * T + qt * P:(t % 2) * T + (qt + 1) * P]
                    for k in range(4):
                        last = mm(out, v_tok[:, k, HD * b:HD * (b + 1)], w_pt[v % 2][:, k * P:(k + 1) * P],
                                  start=(k == 0), stop=(k == 3))
                    last.then_inc(sem("wpv_done"), 1)
            pe.wait_ge(sem("yo_lo"), 2)
            for i in range(4):
                j = LIN_OOUT + i
                if i >= 2:
                    pe.wait_ge(sem("oout_evac"), 2 * (i - 1))
                features(j, j % SPL, halves(bank[i % 2]), 0, T)
            sum_squares(7, norm_tmp, 0)


def shape_constants():
    f = np.float32
    i, j = np.meshgrid(np.arange(P), np.arange(P), indexing="ij")
    c0 = np.concatenate([np.eye(P), np.ones((P, P))], 1).astype(f)
    c1 = np.zeros((P, N_C1), f)
    c1[:, 0:128] = 8.0 * (i + j == P - 1)
    c1[:, 128:256] = -8.0 * (i >= j)
    c1[:, 256:384] = -8.0
    past = np.concatenate([i < j, np.ones((P, P), bool), i < j], 1)
    c1[:, 384:768] = past
    c1[:, 768:1152] = np.where(past, BIG, NEG)
    dist = 255 - np.arange(383)
    n = np.maximum(dist, 0)
    n_f = np.maximum(n, 16).astype(f)
    large = 16 + (np.log(n_f / f(16)) / f(np.log(128 / 16)) * f(16)).astype(np.int32)
    bucket = np.where(n < 16, n, np.minimum(large, 31))
    hot = np.zeros((33, 384), f)
    hot[:32, :383] = (np.arange(32)[:, None] == bucket[None, :]) & (dist >= 0)[None, :]
    hot[32, :383] = np.where(dist >= 0, 0.0, NEG)
    c1[0:33, 1152:1536] = hot
    l = np.arange(T)
    ang = 2 * np.pi * (np.outer(l, l) % T) / T
    scale = 1.0 / np.sqrt(T * P)
    cos_l = (np.cos(ang) * scale).reshape(2, P, T).transpose(1, 0, 2).reshape(P, 512)
    sin_l = (-np.sin(ang) * scale).reshape(2, P, T).transpose(1, 0, 2).reshape(P, 512)
    d = np.arange(P)
    ang = 2 * np.pi * (np.outer(d, d) % P) / P
    pos = np.arange(T)
    row, cl = (pos // 64).astype(f), (pos % 64).astype(f)
    inv = np.power(f(10000.0), -np.arange(16, dtype=f) / f(16)).astype(f)
    r = np.arange(P) % HD
    coord = np.where((r // 32 == 0)[:, None], row[None, :], cl[None, :])
    a = (coord * inv[r % 16][:, None]).astype(f)
    sign = np.where((r % 32) // 16 == 0, -1.0, 1.0)[:, None]
    partner = np.where((np.arange(P) % 32) // 16 == 0, np.arange(P) + 16, np.arange(P) - 16)
    swap = (np.arange(P)[:, None] == partner[None, :]).astype(f)
    band = np.concatenate([np.where(j <= i, 0.0, 8 * NEG), np.where(j >= i, 0.0, 8 * NEG)], 1)
    c2 = np.concatenate([cos_l, sin_l, np.cos(ang), np.sin(ang), np.cos(a), np.sin(a) * sign, swap, band], 1).astype(f)
    return c0, c1, c2


def k8(w):
    n = w.shape[1] // 256
    return list(w.reshape(8, P, n, 256).transpose(2, 1, 0, 3).reshape(n, P, CHUNK))


def k4(w):
    n = w.shape[1] // 512
    return list(w.reshape(4, P, n, 512).transpose(2, 1, 0, 3).reshape(n, P, CHUNK))


def k2(w):
    n = w.shape[0] // 256
    return list(w.reshape(n, 2, P, 1024).transpose(0, 2, 1, 3).reshape(n, P, CHUNK))


def tiles(v):
    return v.reshape(-1, P).T


def rows(m):
    return np.concatenate([tiles(r) for r in m], 1)


def kernel(**inputs):
    import concourse.bacc as bacc
    from concourse.bass_utils import run_bass_kernel_spmd as run

    a = {k: np.asarray(v) for k, v in inputs.items()}
    x, cx = a["x"][0], a["ctx_2"][0]
    xs = np.concatenate([x.T.reshape(8, P, T), cx.T.reshape(8, P, T)], 2).transpose(1, 0, 2)

    wi = a["w_in"][0]
    part = [wi[:, 512 * i:512 * (i + 1)] for i in range(6)] + [wi[:, 3072:]]
    lin = []
    for b in (0, 3):
        for n in range(3):
            lin += k8(part[b + n])
    lin += k8(part[6])
    bm, bs = k4(a["w_br_moba"][0]), k4(a["w_br_sb"][0])
    lin += [bm[0], bs[0], bm[1], bs[1]]
    lin += k8(a["w_out"][0])
    up = a["w_up"][0]
    uv, ug, dn = k8(up[:, :2816]), k8(up[:, 2816:]), k2(a["w_down"][0])
    lin += [uv[0], ug[0]]
    for i in range(10):
        lin += [uv[i + 1], ug[i + 1], dn[i]]
    lin += [dn[10]]
    ei = a["e_w_in_2"][0]
    av, ag, at, bv, bg = (k8(ei[:, 512 * i:512 * (i + 1)]) for i in range(5))
    lin += bv + [av[0], ag[0], av[1], ag[1]] + at + bg
    lin += k4(a["e_a_pw_w_2"][0])
    lin += k8(a["e_w_out_2"][0])
    oi = a["o_w_in_2"][0]
    heads = [0, 4, 1, 5, 2, 6, 3, 7]
    hperm = np.concatenate([np.arange(HD * h, HD * (h + 1)) for h in heads])
    cb, cc, cxx, cg = (k8(oi[:, 512 * i:512 * (i + 1)]) for i in range(4))
    q, kv, og = oi[:, 2048:2560][:, hperm], oi[:, 2560:2816], oi[:, 2816:3328][:, hperm]
    lin += k8(q) + k8(kv) + [cc[0], cxx[0], cc[1], cxx[1]] + cb + cg + k8(og)
    oo = a["o_w_out_2"][0]
    lin += k8(np.concatenate([oo[:512], oo[512:][hperm]], 0))
    assert len(lin) == N_LIN
    ada = a["w_ada"][0]
    sh_m, sc_m, gt_m, sh_f, sc_f, gt_f = (k8(ada[:, D * i:D * (i + 1)]) for i in range(6))
    mod = sc_m + sh_m + gt_m + sh_f + sc_f + gt_f
    for w in (a["e_w_mod_2"][0], a["o_w_mod_2"][0]):
        sh, sc, gt = (k8(w[:, D * i:D * (i + 1)]) for i in range(3))
        mod += sc + sh + gt
    assert len(mod) == N_MOD
    w = np.stack([(lin if kind == "lin" else mod)[n] for kind, n in ORDER])

    c = tiles(a["c"][0])
    cact = np.stack([c, c, tiles(a["c_2"][0]), tiles(a["c_ctx_2"])], 2).reshape(P, 32)
    ba = a["b_ada"][0]
    bias = [ba[D:2 * D], ba[:D], ba[2 * D:3 * D], ba[3 * D:4 * D], ba[4 * D:5 * D], ba[5 * D:]]
    for b in (a["e_b_mod_2"][0], a["o_b_mod_2"][0]):
        bias += [b[D:2 * D], b[:D], b[2 * D:]]
    bias = np.repeat(tiles(np.concatenate(bias)), 2, axis=1)
    sink = np.broadcast_to(a["o_sink_2"][0][None, :], (P, 8))
    vec = np.concatenate([cact, bias, tiles(a["g_mix"][0]), tiles(a["g_ffn"][0]), tiles(a["g_final"]),
                          tiles(a["e_norm_2"][0]), tiles(a["o_norm_2"][0]), tiles(a["final_norm_2"]),
                          rows(a["w_conv"][0]), tiles(a["b_conv"][0]), rows(a["e_a_conv_w_2"][0]),
                          tiles(a["e_a_conv_b_2"][0]), tiles(a["e_a_ln_g_2"][0]), tiles(a["e_a_ln_b_2"][0]),
                          tiles(a["e_a_pw_b_2"][0]), rows(a["o_c_conv_w_2"][0]), sink], 1)
    assert vec.shape == (P, N_VEC)
    fw = a["e_b_fw_2"][0].transpose(1, 0, 2).reshape(P, 512)
    c0, c1, c2 = shape_constants()
    arrays = {"xs": xs, "vec": vec, "rel": a["rel_bias"].T, "w": w, "fw": fw, "c0": c0, "c1": c1, "c2": c2}
    arrays = {k: np.ascontiguousarray(v) for k, v in arrays.items()}

    nc = bacc.Bacc("TRN2", target_bir_lowering=False, num_devices=1)
    aps = [nc.dram_tensor("in_" + k, v.shape, F32, kind="ExternalInput").ap() for k, v in arrays.items()]
    diff = nc.dram_tensor("diff", (8, 384), F32).ap()
    out = nc.dram_tensor("out", (P, KT, T), F32, kind="ExternalOutput").ap()
    build(nc, *aps, diff, out)
    r = run(nc, [{"in_" + k: v for k, v in arrays.items()}], core_ids=[0])
    return r.results[0]["out"].transpose(2, 1, 0).reshape(1, T, D)
```

```python
import numpy as np
from contextlib import ExitStack

import concourse.bass as bass
from concourse import mybir

F32 = mybir.dt.float32
F32R = mybir.dt.float32r
BF16 = mybir.dt.bfloat16
ALU = mybir.AluOpType
ACT = mybir.ActivationFunctionType
AX_X = mybir.AxisListType.X

P = 128
T = 256
D = 1024
KT = D // P
HD = 64
NH = 8
FF_STEPS = 11
CHUNK = 2048
RAW = 4
SPL = 3
EPS = 1e-6
NEG = -1e30
BIG = 3.0e38
QK = 0.125

LIN_QKV, LIN_GATE, LIN_BR, LIN_OUT, LIN_FFN = 0, 12, 20, 24, 28
LIN_EIN = LIN_FFN + 3 * FF_STEPS
LIN_PW = LIN_EIN + 10
LIN_EOUT = LIN_PW + 1
LIN_OIN = LIN_EOUT + 4
LIN_OOUT = LIN_OIN + 13
N_LIN = LIN_OOUT + 4
MOD_FIRST = 8
N_MOD = 48
LIN_OPEN = 1
ADA_SC_M, ADA_SH_M, ADA_GT_M, ADA_SH_F, ADA_SC_F, ADA_GT_F = 0, 4, 8, 12, 16, 20
E_SC, E_SH, E_GT, O_SC, O_SH, O_GT = 24, 28, 32, 36, 40, 44

CONV_W = 31
CONV_VECTOR = {2: [(0, 0, 13)], 3: [(0, 13, 25)], 4: [(0, 25, 31), (2, 0, 4)], 5: [(2, 4, 16)], 6: [(2, 16, 28)],
               7: [(2, 28, 31), (3, 0, 14)], 8: [(3, 14, 31)]}
CONV_SCALAR = {2: [(1, 0, 7)], 3: [(1, 7, 14)], 4: [(1, 14, 21)], 5: [(1, 21, 28)], 6: [(1, 28, 31), (3, 0, 6)],
               7: [(3, 6, 17)], 8: [(3, 17, 28)], 9: [(3, 28, 31)]}
PRODS = 3


def stream_order():
    order = [("mod", m) for m in range(MOD_FIRST)]
    m = MOD_FIRST
    for j in range(LIN_BR + 2):
        order += [("lin", j)]
        n = int(j % 3 == 2) if j < LIN_GATE else 0 if j == LIN_GATE else 2 if j < LIN_BR else 1
        order += [("mod", m + k) for k in range(n)]
        m += n
    order += [("lin", j) for j in range(LIN_BR + 2, LIN_FFN + 1)]
    order += [("mod", m), ("lin", LIN_FFN + 1)]
    m += 1
    for i in range(FF_STEPS - 1):
        j = LIN_FFN + 2 + 3 * i
        order += [("lin", j), ("lin", j + 1), ("mod", m), ("lin", j + 2)]
        m += 1
    order += [("lin", LIN_EIN - 1)]
    for j in range(LIN_EIN, N_LIN):
        n = 2 if j == LIN_EOUT + 1 else 1 if LIN_EOUT + 1 < j < LIN_EOUT + 5 or LIN_OIN + 4 <= j < LIN_OIN + 8 else 0
        order += [("mod", m + k) for k in range(n)]
        m += n
        order += [("lin", j)]
    assert m == N_MOD
    return order


ORDER = stream_order()
RAW_OF_LIN = [0] * N_LIN
RAW_OF_MOD = [0] * N_MOD
for _r, (_kind, _n) in enumerate(ORDER):
    (RAW_OF_LIN if _kind == "lin" else RAW_OF_MOD)[_n] = _r

VEC_SIZES = [("mod_bias", 4 * N_MOD), ("g_mix", 8), ("g_ffn", 8), ("g_final", 8),
             ("e_norm", 8), ("o_norm", 8), ("final_norm", 8), ("w_conv", 132), ("b_conv", 44),
             ("a_conv_w", 124), ("a_conv_b", 4), ("ln_g", 4), ("ln_b", 4), ("pw_b", 4),
             ("o_conv", 12), ("sink", 8)]
VEC = {}
_at = 0
for _n, _s in VEC_SIZES:
    VEC[_n] = _at
    _at += _s
N_VEC = _at

C0 = {"ident": 0, "ones": 128}
N_C0 = 256
N_C1 = 1536
N_C2 = 1280
N_C3 = 896


def mod_col(m, t, v):
    return 4 * m + 2 * t + v


def build(nc, xs_d, cond_d, vec_d, rel_d, w_d, fw_d, c0_d, c1_d, c2_d, c3_d, diff_d, out_d):
    ctx = ExitStack()
    with ctx:
        def sb(name, shape, dt=F32):
            return ctx.enter_context(nc.sbuf_tensor(name, shape, dt))

        sems = {}

        def sem(name):
            if name not in sems:
                sems[name] = ctx.enter_context(nc.semaphore(name))
            return sems[name]

        raw = sb("raw", [P, RAW, CHUNK])
        w_hi = sb("w_hi", [P, SPL, CHUNK], F32R)
        w_lo = sb("w_lo", [P, SPL, CHUNK], F32R)
        h_hi = sb("h_hi", [P, KT, 2 * T], F32R)
        h_lo = sb("h_lo", [P, KT, 2 * T], F32R)
        g_hi = sb("g_hi", [P, 2, T], F32R)
        g_lo = sb("g_lo", [P, 2, T], F32R)
        xs = sb("xs", [P, KT, 2 * T])
        vec = sb("vec", [P, N_VEC])
        c0 = sb("c0", [P, N_C0])
        modv = sb("modv", [P, 4 * N_MOD])
        coef = sb("coef", [P, 48])
        small = sb("small", [P, 64])
        zeros = sb("zeros", [P, 512], BF16)
        rel = sb("rel", [33, 8])
        consts = sb("consts", [P, 2048])
        cond = sb("cond", [P, 2, D])
        arena = sb("arena", [P, 10496])
        att = sb("att", [P, 7 * 384])
        rstd = sb("rstd", [P, 2 * T])
        bank = [ctx.enter_context(nc.psum_tensor(f"bank{i}", [P, 512], F32)) for i in range(4)]
        wide = ctx.enter_context(nc.psum_tensor("wide", [P, 4, 512], F32))

        proj = arena[:, 0:6144].rearrange("p (c n) -> p c n", n=512)
        gate = arena[:, 6144:10240]
        cond_ada = gate[:, 3072:4096]
        onehot = gate[0:33, 2048:2432]
        urow = gate[0:8, 2432:2816]
        norm_tmp = att[:, 0:2048].rearrange("p (k n) -> p k n", n=T)
        TREV = 3
        trev = consts[:, 1152:1152 + TREV * T].rearrange("p (h n) -> p h n", n=T)
        anti8, tri8, all8 = (consts[:, P * i:P * (i + 1)] for i in range(3))
        past, bound = consts[:, 384:768], consts[:, 768:1152]
        prob, sb_t, sb_r, sb_e = (att[:, 384 * i:384 * (i + 1)] for i in range(4))
        pt = [att[:, 384 * 4:384 * 5], att[:, 384 * 5:384 * 6]]
        aw = att[:, 384 * 6:384 * 7]
        mix = arena[:, 0:2048]
        mix2 = arena[:, 2048:3072]
        cv = arena[:, 3072:3584].rearrange("p (t n) -> p t n", n=T)
        cg = arena[:, 3584:4096].rearrange("p (t n) -> p t n", n=T)
        cos_l = consts[:, 0:512].rearrange("p (l n) -> p l n", n=T)
        sin_l = consts[:, 512:1024].rearrange("p (l n) -> p l n", n=T)
        dft_d = att[:, 2048:2304]
        fw = consts[:, 1024:1536]
        fold = consts[:, 1024:2048].rearrange("p (g c n) -> p g c n", g=4, c=2)
        UW = T + 30
        u_pad = arena[:, 0:4 * 2 * UW].rearrange("p (t s n) -> p t s n", t=4, s=2)
        b_val = arena[:, 2304:4352].rearrange("p (t n) -> p t n", n=512)
        sgate = arena[:, 4352:8448].rearrange("p (t n) -> p t n", n=512)
        conv = arena[:, 8448:10496].rearrange("p (t n) -> p t n", n=512)
        ln_tmp = arena[:, 0:2048].rearrange("p (t n) -> p t n", n=512)
        glu = arena[:, 4352:5376].rearrange("p (t n) -> p t n", n=512)
        y_b = b_val
        four = [att[:, 0:512], att[:, 512:1024]]
        conv_prod = [att[:, 1024 + 512 * n:1536 + 512 * n] for n in range(PRODS)]
        q_raw = arena[:, 0:1024]
        q_rot = arena[:, 1024:2048].rearrange("p (t n) -> p t n", n=T)
        k_all = arena[:, 2048:2560]
        k_raw = arena[:, 2560:2816]
        v_tok = arena[:, 3072:3584].rearrange("p (t n) -> p t n", n=P)
        rot_tmp = arena[:, 3584:4608]
        ccx = arena[:, 4608:4608 + 4 * 258].rearrange("p (t n) -> p t n", n=258)
        cb = arena[:, 5696:6720].rearrange("p (t n) -> p t n", n=T)
        cg_ag = arena[:, 6720:8768].rearrange("p (t n) -> p t n", n=T)
        y_c = arena[:, 0:1024].rearrange("p (t n) -> p t n", n=T)
        c3 = arena[:, 9472:9472 + N_C3]
        rope_cos, rope_sin, swap, band = c3[:, 0:256], c3[:, 256:512], c3[:, 512:640], c3[:, 640:896]
        w_prob = [att[:, 0:512], att[:, 512:1024]]
        w_pt = [att[:, 1024:1536], att[:, 1536:2048]]

        def col(name, i):
            return vec[:, bass.ds(VEC[name] + i, 1)]

        def modc(m, t, v=0):
            return modv[:, mod_col(m, t, v):mod_col(m, t, v) + 1]

        def shift_col(base, k, v=0):
            return modc(base + k // 2, k % 2, v)

        def conv_part(t, k, engine):
            acc, src = conv[:, t, :].rearrange("p (s n) -> p s n", s=2), u_pad[:, t, :, k:k + T]
            if t == 3:
                s = 0 if engine == "vector" else 1
                acc, src = acc[:, s, :], src[:, s, :]
            return acc, src

        def mod_row(base, v):
            return modv[:, 4 * base:4 * base + 16].rearrange("p (k v) -> p k v", v=2)[:, :, v]

        class Steps:

            def __init__(self, eng, name):
                self.eng, self.sem, self.base, self.off = eng, sem(name), 0, 0

            def mark(self, ins):
                self.base += 1
                ins.then_inc(self.sem, 1)

            def value(self):
                return self.off + self.base

            def wait(self):
                self.eng.wait_ge(self.sem, self.value())

            def enter(self, i, per):
                self.off, self.per, self.start = i * per, per, self.base

            def leave(self, count):
                assert self.base - self.start == self.per, (self.base, self.start, self.per)
                self.base = self.start + self.per * count
                self.off = 0

        NORMS = {"mix": (0, 0, (ADA_SH_M, 0)), "ffn": (0, 8, (ADA_SH_F, 0)),
                 "even_ctx": (1, 24, (E_SH, 1)), "even_x": (0, 16, (E_SH, 0)),
                 "odd_x": (0, 32, (O_SH, 0)), "odd_ctx": (1, 40, (O_SH, 1)),
                 "final": (0, None, None), "last": (0, None, None)}

        block = ctx.enter_context(nc.Block())

        @block.sync
        def _(sp):
            def load(r, slot, freed=None):
                if freed is not None:
                    sp.wait_ge(sem("lo_done" if freed[0] == "lin" else "mod_done"), freed[1] + 1)
                src = w_d[bass.ds(r, 1), :, :].rearrange("a p n -> (a p) n")
                sp.dma_start(raw[:, slot, :], src).then_inc(sem(f"arrived{slot}"), 16)

            for r in range(MOD_FIRST + 4):
                load(r, r % RAW, ORDER[r - RAW] if r >= RAW else None)
            with sp.Fori(0, LIN_GATE // 3) as i:
                for n in range(4):
                    load(4 * i + MOD_FIRST + 4 + n, n, ("lin", 3 * i + n) if n < 3 else ("mod", i + MOD_FIRST))
            r0 = RAW_OF_LIN[LIN_FFN]
            for r in range(RAW_OF_LIN[LIN_GATE] + 4, r0 + 3):
                load(r, r % RAW, ORDER[r - RAW])
            with sp.Fori(0, FF_STEPS - 1) as i:
                for n, (kind, first, step) in enumerate((("lin", LIN_FFN - 1, 3), ("lin", LIN_FFN, 3),
                                                         ("mod", E_SH, 1), ("lin", LIN_FFN + 1, 3))):
                    load(4 * i + r0 + 3 + n, (r0 + 3 + n) % RAW, (kind, step * i + first))
            r1 = r0 + 3 + 4 * (FF_STEPS - 1)
            for r in range(r1, len(ORDER)):
                load(r, r % RAW, ORDER[r - RAW])
            for half in range(2):
                sp.wait_ge(sem("last_done"), 4 * (half + 1))
                sp.dma_start(out_d[:, 4 * half:4 * half + 4, :], xs[:, 4 * half:4 * half + 4, 0:T]).then_inc(sem("stored"), 16)
            sp.wait_ge(sem("stored"), 32)

        @block.gpsimd
        def _(pool):
            pool.memset(zeros[:, :], 0.0).then_inc(sem("zeros_set"), 1)
            for h in range(NH):
                pool.wait_ge(sem("sb_ln"), h + 1)
                pool.wait_ge(sem("sb_relu"), h + 1)
                nc.gpsimd.tensor_tensor(sb_r, sb_r, sb_t, ALU.add).then_inc(sem("sb_sum"), 1)
                pool.wait_ge(sem("sb_sum"), h + 1)
                nc.gpsimd.tensor_tensor(sb_r, sb_r, past, ALU.mult).then_inc(sem("sb_kept"), 1)
            def product(c):
                pool.wait_ge(sem("gelu_done"), c + 1)
                pool.wait_ge(sem("value_conv"), c + 1)
                nc.gpsimd.tensor_tensor(cv, cv, cg, ALU.mult).then_inc(sem("ffn_mult"), 1)

            product(0)
            with pool.Fori(0, FF_STEPS - 1) as i:
                product(i + 1)
            pool.wait_ge(sem("ffn_down_evac"), 8)
            pool.memset(u_pad[:, :, :, 0:15], 0.0).then_inc(sem("pads_set"), 1)
            pool.memset(u_pad[:, :, :, 15 + T:UW], 0.0).then_inc(sem("pads_set"), 1)
            n = 0
            for t in (1, 3):
                pool.wait_ge(sem("conv_opened"), 1 if t == 1 else 2)
                for k in range(1, CONV_W):
                    acc, _ = conv_part(t, k, "scalar")
                    pool.wait_ge(sem("prod_ready"), n + 1)
                    if n:
                        pool.wait_ge(sem("prod_used"), n)
                    prod = conv_prod[n % PRODS]
                    prod = prod.rearrange("p (s n) -> p s n", s=2) if t == 1 else prod[:, 0:T]
                    nc.gpsimd.tensor_tensor(acc, acc, prod, ALU.add).then_inc(sem("prod_used"), 1)
                    n += 1
            for g in range(4):
                pool.wait_ge(sem("y_b_raw"), g + 1)
                pool.wait_ge(sem("ein_evac"), 10)
                nc.gpsimd.tensor_tensor(y_b[:, g, :], y_b[:, g, :], sgate[:, 4 + g, :], ALU.mult).then_inc(sem("y_b"), 1)

        @block.scalar
        def _(act):
            me = Steps(act, "act_steps")
            act.dma_start(cond_ada, bass.AP(cond_d.tensor, 0, [[0, P], [1, D]])).then_inc(sem("cond_ada_loaded"), 16)
            act.dma_start(xs[:, :, 0:T], xs_d[:, :, 0:T]).then_inc(sem("x_loaded"), 16)
            act.dma_start(c0[:, :], c0_d).then_inc(sem("c0_loaded"), 16)
            act.dma_start(vec[:, :], vec_d).then_inc(sem("vec_loaded"), 16)
            act.dma_start(rel[0:32, :], rel_d).then_inc(sem("rel_loaded"), 16)
            act.dma_start(onehot, c1_d[0:33, 1152:1536]).then_inc(sem("rel_loaded"), 16)

            def split(j, slot=None, rslot=None, arrived=None):
                if isinstance(j, int):
                    if j >= N_LIN:
                        return
                    r = RAW_OF_LIN[j]
                    slot, rslot, arrived = j % SPL, r % RAW, 16 * (r // RAW + 1)
                act.wait_ge(sem(f"arrived{rslot}"), arrived)
                if not isinstance(j, int) or j >= SPL:
                    act.wait_ge(sem("lin_done"), LIN_OPEN + j - (SPL - 1))
                nc.scalar.copy(w_hi[:, slot, :], raw[:, rslot, :]).then_inc(sem("hi_done"), 1)

            def rms(name, n_before, ready, tmp):
                s = NORMS[name][0]
                for (sname, v) in ready:
                    act.wait_ge(sem(sname), v)
                nc.scalar.activation(tmp, xs[:, :, s * T:(s + 1) * T], ACT.Square).then_inc(sem("squares"), 1)
                act.wait_ge(sem("sumsq"), n_before + 1)
                out = rstd[:, s * T:(s + 1) * T]
                me.mark(nc.scalar.activation(out, bank[2][:, s * T:(s + 1) * T], ACT.Ln, bias=EPS_AP, scale=1.0 / D))
                me.wait()
                nc.scalar.activation(out, out, ACT.Exp, scale=-0.5).then_inc(sem("rstd_ready"), 1)

            def shift_hi(name, tiles_before, tmp):
                s, _, (sh, v) = NORMS[name]
                for k in range(KT):
                    act.wait_ge(sem("normed"), tiles_before + k + 1)
                    nc.scalar.activation(h_hi[:, k, s * T:(s + 1) * T], tmp[:, k, :], ACT.Identity,
                                         bias=shift_col(sh, k, v), scale=1.0).then_inc(sem("norm_hi"), 1)

            eps_col = small[:, 63:64]
            EPS_AP = eps_col
            act.wait_ge(sem("cond_ada_loaded"), 16)
            nc.scalar.activation(cond_ada, cond_ada, ACT.Silu).then_inc(sem("cond_ada_ready"), 1)
            act.wait_ge(sem("eps_set"), 1)
            rms("mix", 0, [("x_loaded", 16)], norm_tmp)
            shift_hi("mix", 0, norm_tmp)
            act.dma_start(consts[:, 0:1152], c1_d[:, 0:1152]).then_inc(sem("c1_loaded"), 16)
            act.dma_start(cond.rearrange("p v n -> p (v n)"),
                          bass.AP(cond_d.tensor, D, [[0, P], [1, 2 * D]])).then_inc(sem("cond_loaded"), 16)
            act.dma_start(xs[:, :, T:2 * T], xs_d[:, :, T:2 * T]).then_inc(sem("ctx_loaded"), 16)
            split(0)
            split(1)
            act.wait_ge(sem("bias_row"), 1)
            nc.scalar.copy(urow, bank[0][0:8, 0:384]).then_inc(sem("bias_row_out"), 1)
            act.wait_ge(sem("bias_row_out"), 1)
            act.dma_start(diff_d, urow).then_inc(sem("bias_stored"), 16)
            act.wait_ge(sem("bias_stored"), 16)

            def load_trev(h):
                act.dma_start(trev[:, h % TREV, :], bass.AP(diff_d.tensor, 384 * h, [[1, P], [1, T]])
                              ).then_inc(sem(f"trev_loaded{h % TREV}"), 16)

            for h in range(TREV):
                load_trev(h)
            with act.Fori(0, 2) as i:
                for n in range(6):
                    j = 6 * i + n
                    r_ahead = MOD_FIRST + 4 * ((n + 2) // 3) + (n + 2) % 3
                    split(j + 2, (n + 2) % SPL, r_ahead % RAW, 32 * i + 16 * (r_ahead // RAW + 1))
                    act.wait_ge(sem("lin_done"), LIN_OPEN + j + 1)
                    nc.scalar.copy(proj[:, bass.ds(j, 1), :].rearrange("p a n -> p (a n)"),
                                   bank[n % 2][:, :]).then_inc(sem("proj_evac"), 1)
            act.wait_ge(sem("cond_loaded"), 16)
            nc.scalar.activation(cond[:, :, :], cond[:, :, :], ACT.Silu).then_inc(sem("cond_ready"), 1)
            for h in range(NH + 1):
                j = LIN_GATE + h
                if h < NH:
                    act.wait_ge(sem("qk_done"), h + 1)
                    if h + TREV < NH:
                        load_trev(h + TREV)
                    if h:
                        act.wait_ge(sem("sb_sum"), h)
                    me.mark(nc.scalar.activation(sb_t, wide[:, 2, 0:384], ACT.Abs))
                    abs_done = me.value()
                if h:
                    act.wait_ge(sem("pt_done"), h)
                    if h >= 3:
                        act.wait_ge(sem("pv_done"), h - 2)
                    nc.scalar.copy(pt[(h - 1) % 2], wide[:, 1, 0:384]).then_inc(sem("pt_ready"), 1)
                if h >= 3 and h % 2:
                    pair_hi = (h - 3) // 2
                    act.wait_ge(sem("pv_done"), h - 1)
                    nc.scalar.copy(h_hi[:, pair_hi::4, T:2 * T],
                                   wide[:, 3, :].rearrange("p (a n) -> p a n", a=2)).then_inc(sem("att_hi"), 1)
                if h < NH:
                    act.wait_ge(sem("neg_max"), h + 1)
                    for qt, (a, b) in enumerate(((0, 128), (128, 384))):
                        nc.scalar.activation(prob[:, a:b], wide[:, 0, a:b], ACT.Exp, bias=small[:, 2 + qt:3 + qt], scale=QK,
                                             accum_out=small[:, 4 + qt:5 + qt]).then_inc(sem("exp_done"), 1)
                    act.wait_ge(me.sem, abs_done)
                    me.mark(nc.scalar.activation(sb_t, sb_t, ACT.Exp, scale=-QK))
                if h:
                    act.wait_ge(sem("sb_min"), h)
                    if h >= 2:
                        act.wait_ge(sem("pv_done"), h - 1)
                    nc.scalar.activation(aw, sb_e, ACT.Exp, scale=QK).then_inc(sem("aw_ready"), 1)
                if h < NH:
                    me.wait()
                    nc.scalar.activation(sb_t, sb_t, ACT.Ln, bias=1.0).then_inc(sem("sb_ln"), 1)
                    if h:
                        act.wait_ge(sem("e_done"), h)
                    nc.scalar.activation(sb_r, wide[:, 2, 0:384], ACT.Relu, scale=QK).then_inc(sem("sb_relu"), 1)
                    split(j + 2)
                if h < NH:
                    act.wait_ge(sem("lin_done"), LIN_OPEN + j + 1)
                    nc.scalar.copy(gate[:, 512 * h:512 * (h + 1)], bank[j % 2][:, :]).then_inc(sem("gate_evac"), 1)
            act.wait_ge(sem("pv_done"), NH)
            nc.scalar.copy(h_hi[:, 3::4, T:2 * T], wide[:, 3, :].rearrange("p (a n) -> p a n", a=2)).then_inc(sem("att_hi"), 1)
            act.wait_ge(sem("gate_evac"), NH)
            nc.scalar.activation(gate, gate, ACT.Sigmoid).then_inc(sem("gates_ready"), 1)
            act.wait_ge(sem("e_done"), NH)
            act.wait_ge(sem("qk_done"), NH)
            act.wait_ge(sem("sb_kept"), NH)
            act.wait_ge(sem("sb_min"), NH)
            act.dma_start(consts[:, 0:1024], c2_d[:, 0:1024]).then_inc(sem("c2_loaded"), 16)
            act.dma_start(dft_d, c2_d[:, 1024:1280]).then_inc(sem("c2_loaded"), 16)
            act.dma_start(fw, fw_d).then_inc(sem("c2_loaded"), 16)
            for i in range(4):
                split(LIN_BR + i + 2)
                if i % 2:
                    n = i // 2
                    act.wait_ge(sem("mixed"), n + 1)
                    nc.scalar.copy(h_hi[:, 4 * n:4 * n + 4, 0:T],
                                   mix[:, 1024 * n:1024 * (n + 1)].rearrange("p (k n) -> p k n", n=T)).then_inc(sem("mixed_hi"), 1)
            for i in range(4):
                split(LIN_OUT + i + 2)
            rms("ffn", 1, [("out_evac", 8)], norm_tmp)
            shift_hi("ffn", 8, norm_tmp)

            def conv_first(which, dst, c):
                for t in range(2):
                    tile = 2 * c + t + (22 if which else 0)
                    nc.scalar.activation(dst[:, t, :], bank[which][:, t * T:(t + 1) * T], ACT.Identity,
                                         bias=col("b_conv", tile), scale=col("w_conv", 88 + tile)).then_inc(sem("tap2"), 1)

            split(LIN_FFN + 2)
            act.wait_ge(sem("lin_done"), LIN_OPEN + LIN_FFN + 1)
            conv_first(0, cv, 0)
            split(LIN_FFN + 3)
            act.wait_ge(sem("lin_done"), LIN_OPEN + LIN_FFN + 2)
            conv_first(1, cg, 0)
            act.wait_ge(sem("gate_conv"), 1)
            nc.scalar.activation(cg, cg, ACT.Gelu_apprx_tanh).then_inc(sem("gelu_done"), 1)
            act.wait_ge(sem("ffn_mult"), 1)
            nc.scalar.copy(g_hi[:, :, :], cv).then_inc(sem("g_hi_done"), 1)
            j0, r0 = LIN_FFN + 2, RAW_OF_LIN[LIN_FFN + 2]
            with act.Fori(0, FF_STEPS - 1) as i:
                j = 3 * i + j0
                split(j + 2, (j0 + 2) % SPL, (r0 + 3) % RAW, 16 * i + 16 * ((r0 + 3) // RAW + 1))
                act.wait_ge(sem("lin_done"), LIN_OPEN + j + 1)
                act.wait_ge(sem("g_lo_done"), i + 1)
                conv_first(0, cv, i + 1)
                split(j + 3, (j0 + 3) % SPL, (r0 + 4) % RAW, 16 * i + 16 * ((r0 + 4) // RAW + 1))
                act.wait_ge(sem("lin_done"), LIN_OPEN + j + 2)
                conv_first(1, cg, i + 1)
                act.wait_ge(sem("gate_conv"), i + 2)
                nc.scalar.activation(cg, cg, ACT.Gelu_apprx_tanh).then_inc(sem("gelu_done"), 1)
                split(j + 4, (j0 + 4) % SPL, (r0 + 5) % RAW, 16 * i + 16 * ((r0 + 5) // RAW + 1))
                act.wait_ge(sem("ffn_mult"), i + 2)
                act.wait_ge(sem("lin_done"), LIN_OPEN + j + 3)
                nc.scalar.copy(g_hi[:, :, :], cv).then_inc(sem("g_hi_done"), 1)
            split(LIN_EIN + 1)
            rms("even_ctx", 2, [("ctx_loaded", 16)], norm_tmp)
            shift_hi("even_ctx", 16, norm_tmp)
            rms("final", 3, [("ffn_down_evac", 8)], norm_tmp)
            rms("even_x", 4, [("final_scaled", 8)], norm_tmp)
            shift_hi("even_x", 24, norm_tmp)

            act.wait_ge(sem("fold_done"), 1)
            nc.scalar.copy(fold[:, :, 0, :], bank[0][:, :].rearrange("p (g n) -> p g n", g=4)).then_inc(sem("fold_ready"), 1)
            nc.scalar.copy(fold[:, :, 1, :], bank[1][:, :].rearrange("p (g n) -> p g n", g=4)).then_inc(sem("fold_ready"), 1)

            def chunk_banks(i):
                b = 2 * (i % 2)
                return wide[:, b:b + 2, :]

            def fourier_evac(g):
                for s in range(2):
                    act.wait_ge(sem("four_a"), 2 * g + s + 1)
                    if g:
                        act.wait_ge(sem("four_b"), g)
                    nc.scalar.copy(four[s], bank[2 * s][:, :]).then_inc(sem("four_ready"), 1)

            def fourier_out(g):
                act.wait_ge(sem("four_b"), g + 1)
                nc.scalar.copy(y_b[:, g, :], bank[1][:, :]).then_inc(sem("y_b_raw"), 1)

            n_prod = 0
            for i in range(10):
                split(LIN_EIN + i + 2)
                for t, k0, k1 in CONV_SCALAR.get(i, ()):
                    act.wait_ge(sem("glu_done"), 1 if t == 1 else 2)
                    act.wait_ge(sem("pads_set"), 2)
                    for k in range(k0, k1):
                        acc, src = conv_part(t, k, "scalar")
                        if k == 0:
                            nc.scalar.activation(acc, src, ACT.Identity, bias=col("a_conv_b", t),
                                                 scale=col("a_conv_w", t)).then_inc(sem("conv_opened"), 1)
                            continue
                        if n_prod >= PRODS:
                            act.wait_ge(sem("prod_used"), n_prod - PRODS + 1)
                        prod = conv_prod[n_prod % PRODS]
                        prod = prod.rearrange("p (s n) -> p s n", s=2) if t == 1 else prod[:, 0:T]
                        nc.scalar.activation(prod, src, ACT.Copy,
                                             scale=col("a_conv_w", 4 * k + t)).then_inc(sem("prod_ready"), 1)
                        n_prod += 1
                act.wait_ge(sem("lin_done"), LIN_OPEN + LIN_EIN + i + 1)
                src = chunk_banks(i)
                if i < 4 and i % 2 == 0:
                    ins = nc.scalar.copy(u_pad[:, i:i + 2, :, 15:15 + T], src.rearrange("p t (s n) -> p t s n", s=2))
                elif i < 4:
                    if i == 3:
                        act.wait_ge(sem("glu_done"), 1)
                    ins = nc.scalar.activation(glu, src, ACT.Sigmoid)
                elif i < 6:
                    ins = nc.scalar.copy(b_val[:, 2 * (i - 4):2 * (i - 4) + 2, :], src)
                else:
                    t = 2 * (i - 6)
                    ins = nc.scalar.activation(sgate[:, t:t + 2, :], src, ACT.Silu)
                ins.then_inc(sem("ein_evac"), 1)
                if i >= 7:
                    fourier_out(i - 7)
                if i >= 6:
                    fourier_evac(i - 6)
            fourier_out(3)
            me.mark(nc.scalar.activation(small[:, 62:63], eps_col, ACT.Sqrt))
            for t in range(4):
                act.wait_ge(sem("centered"), t + 1)
                nc.scalar.activation(ln_tmp[:, t, :], conv[:, t, :], ACT.Square).then_inc(sem("ln_squares"), 1)
            act.wait_ge(sem("ln_sumsq"), 1)
            nc.scalar.activation(rstd[:, :], bank[3][:, :], ACT.Sqrt, bias=EPS_AP, scale=1.0 / 512).then_inc(sem("ln_std"), 1)
            me.wait()
            me.mark(nc.scalar.activation(small[:, 62:63], eps_col, ACT.Silu))
            silu_at = []
            for t in range(5):
                if t < 4:
                    act.wait_ge(sem("ln_scaled"), t + 1)
                    me.mark(nc.scalar.activation(conv[:, t, :], conv[:, t, :], ACT.Silu, bias=col("ln_b", t),
                                                 scale=col("ln_g", t)))
                    silu_at.append(me.value())
                if t:
                    act.wait_ge(me.sem, silu_at[t - 1])
                    nc.scalar.copy(h_hi[:, t - 1, :], conv[:, t - 1, :]).then_inc(sem("u_hi"), 1)
            split(LIN_PW + 2)
            for t in range(4):
                act.wait_ge(sem("y_a"), t + 1)
                nc.scalar.copy(h_hi[:, 4 + t, :], ln_tmp[:, t, :]).then_inc(sem("y_hi"), 1)
            act.wait_ge(sem("lin_done"), LIN_OPEN + LIN_PW + 1)
            for t in range(4):
                act.wait_ge(sem("y_b"), t + 1)
                nc.scalar.copy(h_hi[:, t, :], y_b[:, t, :]).then_inc(sem("y_hi"), 1)
            act.wait_ge(sem("u_lo"), 4)
            act.dma_start(c3, c3_d).then_inc(sem("c3_loaded"), 16)
            for i in range(4):
                split(LIN_EOUT + i + 2)
            rms("odd_x", 5, [("eout_evac", 16)], norm_tmp)
            shift_hi("odd_x", 32, norm_tmp)
            rms("odd_ctx", 6, [("norm_lo", 5 * KT)], norm_tmp)
            shift_hi("odd_ctx", 40, norm_tmp)
            for i in range(3):
                j = LIN_OIN + i
                split(j + 2)
                act.wait_ge(sem("lin_done"), LIN_OPEN + j + 1)
                if i < 2:
                    nc.scalar.copy(q_raw[:, 512 * i:512 * (i + 1)], wide[:, i, :]).then_inc(sem("q_raw"), 1)
                else:
                    nc.scalar.copy(k_raw, wide[:, 2, 0:T]).then_inc(sem("q_raw"), 1)
                    nc.scalar.copy(k_all[:, T:2 * T], wide[:, 2, T:2 * T]).then_inc(sem("kv_evac"), 1)
                    nc.scalar.copy(v_tok, wide[:, 3, :].rearrange("p (t n) -> p t n", n=P)).then_inc(sem("kv_evac"), 1)

            def window_pt(u):
                act.wait_ge(sem("wt_done"), u + 1)
                if u >= 2:
                    act.wait_ge(sem("wpv_done"), u - 1)
                nc.scalar.copy(w_pt[u % 2], bank[2 + u % 2][:, :]).then_inc(sem("wpt_ready"), 1)

            for u in range(18):
                if u < 10:
                    split(LIN_OIN + 3 + u + 2)
                if u < 16:
                    act.wait_ge(sem("wneg_max"), u + 1)
                    if u >= 2:
                        act.wait_ge(sem("wt_done"), u - 1)
                    nb = small[:, 16 + u:17 + u]
                    nc.scalar.activation(w_prob[u % 2], bank[u % 2][:, :], ACT.Exp, bias=nb, scale=QK,
                                         accum_out=small[:, 32 + 2 * (u % 2):33 + 2 * (u % 2)]).then_inc(sem("wexp"), 1)
                    t, b = (u // 2) % 4, u // 8
                    nc.scalar.activation(small[:, 33 + 2 * (u % 2):34 + 2 * (u % 2)], nb, ACT.Exp, scale=1.0,
                                         bias=col("sink", t + 4 * b)).then_inc(sem("wexp"), 1)
                if u < 10:
                    act.wait_ge(sem("lin_done"), LIN_OPEN + LIN_OIN + 3 + u + 1)
                    src = wide[:, u % 2, :].rearrange("p (t n) -> p t n", n=T)
                    t = 2 * ((u // 2) % 2) if u < 4 else 2 * (u % 2)
                    if u < 4 and u % 2 == 0:
                        nc.scalar.copy(ccx[:, t:t + 2, 1:1 + T], src).then_inc(sem("oin_evac"), 1)
                    elif u in (4, 5):
                        nc.scalar.copy(cb[:, t:t + 2, :], src).then_inc(sem("oin_evac"), 1)
                    elif u >= 6:
                        nc.scalar.copy(cg_ag[:, 2 * (u - 6):2 * (u - 6) + 2, :], src).then_inc(sem("oin_evac"), 1)
                if 1 <= u < 17:
                    window_pt(u - 1)
            me.mark(nc.scalar.activation(cg_ag, cg_ag, ACT.Silu))
            me.wait()
            nc.scalar.copy(small[:, 62:63], small[:, 63:64]).then_inc(sem("silu_gates"), 1)
            act.wait_ge(sem("y_c"), 1)
            nc.scalar.copy(h_hi[:, 0:4, 0:T], y_c).then_inc(sem("yo_hi"), 1)
            act.wait_ge(sem("y_d"), 1)
            nc.scalar.copy(h_hi[:, 4:8, 0:T], rot_tmp.rearrange("p (t n) -> p t n", n=T)).then_inc(sem("yo_hi"), 1)
            for i in range(4):
                split(LIN_OOUT + i + 2)
            rms("last", 7, [("oout_evac", 8)], norm_tmp)

        @block.vector
        def _(dve):
            me = Steps(dve, "dve_steps")

            def mod(m, rslot, arrived, j, slot, both=None):
                if both is None:
                    both = E_SC <= m < O_GT
                    vecs = ((0, cond_ada),) if m < E_SC else ((0, cond[:, 0, :]), (1, cond[:, 1, :]))[:1 + both]
                else:
                    vecs = ((0, cond[:, 0, :]), (1, cond[:, 1, :])) if both else ((0, cond_ada),)
                dve.wait_ge(sem(f"arrived{rslot}"), arrived)
                if not isinstance(j, int) or j >= SPL:
                    dve.wait_ge(sem("lin_done"), LIN_OPEN + j - (SPL - 1))
                if not isinstance(m, int) or m:
                    dve.wait_ge(sem("mod_done"), m)
                for v, c in vecs:
                    if v:
                        me.mark(last)
                        me.wait()
                    for t in range(2):
                        last = nc.vector.scalar_tensor_tensor(
                            w_lo[:, slot, D * t:D * (t + 1)], raw[:, rslot, D * t:D * (t + 1)], 1.0, c, ALU.mult, ALU.mult,
                            accum_out=modv[:, bass.ds(4 * m + 2 * t + v, 1)])
                last.then_inc(sem("mod_done"), 1)

            def mods_before(j):
                r, mods = RAW_OF_LIN[j] - 1, []
                while r >= MOD_FIRST and ORDER[r][0] == "mod":
                    mods.insert(0, ORDER[r][1])
                    r -= 1
                return mods

            def mod_static(m, j):
                r = RAW_OF_MOD[m]
                mod(m, r % RAW, 16 * (r // RAW + 1), j, j % SPL)

            def split(j, slot=None, rslot=None, mod_before=None, done=0):
                if isinstance(j, int):
                    if j >= N_LIN:
                        return
                    slot, rslot = j % SPL, RAW_OF_LIN[j] % RAW
                if isinstance(j, int):
                    for mod_before in mods_before(j)[done:]:
                        mod_static(mod_before, j)
                    mod_before = (mods_before(j) or [None])[-1]
                if mod_before is not None:
                    dve.wait_ge(sem("mod_done"), mod_before + 1)
                dve.wait_ge(sem("hi_done"), j + 1)
                nc.vector.tensor_tensor(w_lo[:, slot, :], raw[:, rslot, :], w_hi[:, slot, :].bitcast(F32),
                                        ALU.subtract).then_inc(sem("lo_done"), 1)

            def coefficients(at, gain, scale_cols):
                nc.vector.scalar_tensor_tensor(coef[:, at:at + 8], scale_cols, 1.0, vec[:, VEC[gain]:VEC[gain] + 8],
                                               ALU.add, ALU.mult).then_inc(sem("coef_ready"), 1)

            batches = []

            def mod_bias(m0, m1):
                one = m0 < E_SC or m0 >= O_GT
                dve.wait_ge(sem("mod_done"), m1)
                a, b = 4 * m0, 4 * m1
                dst, bias = modv[:, a:b], vec[:, VEC["mod_bias"] + a:VEC["mod_bias"] + b]
                if one:
                    dst, bias = (z.rearrange("p (c v) -> p c v", v=2)[:, :, 0] for z in (dst, bias))
                nc.vector.tensor_tensor(dst, dst, bias, ALU.add).then_inc(sem("mod_biased"), 1)
                batches.append(m1)
                dve.wait_ge(sem("mod_biased"), len(batches))

            def norm(name, n_before, tiles_before, tmp, coefs_before):
                s, at, (sh, v) = NORMS[name]
                dve.wait_ge(sem("rstd_ready"), n_before + 1)
                dve.wait_ge(sem("coef_ready"), coefs_before)
                for k in range(KT):
                    nc.vector.scalar_tensor_tensor(tmp[:, k, :], xs[:, k, s * T:(s + 1) * T], coef[:, at + k:at + k + 1],
                                                   rstd[:, s * T:(s + 1) * T], ALU.mult, ALU.mult).then_inc(sem("normed"), 1)
                for k in range(KT):
                    dve.wait_ge(sem("norm_hi"), tiles_before + k + 1)
                    nc.vector.scalar_tensor_tensor(h_lo[:, k, s * T:(s + 1) * T], tmp[:, k, :], shift_col(sh, k, v),
                                                   h_hi[:, k, s * T:(s + 1) * T].bitcast(F32),
                                                   ALU.add, ALU.subtract).then_inc(sem("norm_lo"), 1)

            nc.vector.memset(rel[32:33, :], 1.0).then_inc(sem("rel_one"), 1)
            nc.vector.memset(small[:, 63:64], EPS).then_inc(sem("eps_set"), 1)
            dve.wait_ge(sem("cond_ada_ready"), 1)
            for m in range(MOD_FIRST):
                mod(m, RAW_OF_MOD[m] % RAW, 16 * (RAW_OF_MOD[m] // RAW + 1), 0, 0)
            dve.wait_ge(sem("vec_loaded"), 16)
            mod_bias(0, 8)
            coefficients(0, "g_mix", mod_row(ADA_SC_M, 0))
            norm("mix", 0, 0, norm_tmp, 1)
            split(0)
            split(1)
            with dve.Fori(0, 2) as i:
                for n in range(6):
                    j = 6 * i + n + 2
                    r = MOD_FIRST + 4 * ((n + 2) // 3) + (n + 2) % 3
                    m = None
                    if (n + 2) % 3 == 0:
                        m = 2 * i + MOD_FIRST + (n + 2) // 3 - 1
                        mod(m, (r - 1) % RAW, 32 * i + 16 * ((r - 1) // RAW + 1), j, (n + 2) % SPL, False)
                    split(j, (n + 2) % SPL, r % RAW, m)
            dve.wait_ge(sem("cond_ready"), 1)
            for h in range(NH + 1):
                j = LIN_GATE + h
                if h < NH:
                    dve.wait_ge(sem("qk_done"), h + 1)
                    me.mark(nc.vector.reduce_max(small[:, 0:1], wide[:, 0, 0:128], AX_X, negate=True))
                    me.mark(nc.vector.reduce_max(small[:, 1:2], wide[:, 0, 128:384], AX_X, negate=True))
                    me.wait()
                    nc.vector.tensor_scalar(small[:, 2:4], small[:, 0:2], QK, None, ALU.mult).then_inc(sem("neg_max"), 1)
                if h:
                    dve.wait_ge(sem("e_done"), h)
                    if h >= 2:
                        dve.wait_ge(sem("aw_ready"), h - 1)
                    nc.vector.tensor_tensor(sb_e, bank[2][:, 0:384], bound, ALU.min).then_inc(sem("sb_min"), 1)
                if h >= 3 and h % 2:
                    pair = (h - 3) // 2
                    dve.wait_ge(sem("att_hi"), pair + 1)
                    nc.vector.tensor_tensor(h_lo[:, pair::4, T:2 * T], wide[:, 3, :].rearrange("p (a n) -> p a n", a=2),
                                            h_hi[:, pair::4, T:2 * T].bitcast(F32), ALU.subtract).then_inc(sem("att_lo"), 1)
                if h == NH:
                    break
                mods = mods_before(j + 2)
                for m in mods[:1]:
                    mod_static(m, j + 2)
                dve.wait_ge(sem("exp_done"), 2 * h + 2)
                me.mark(nc.vector.reciprocal(small[:, 6:8], small[:, 4:6]))
                me.wait()
                me.mark(nc.vector.tensor_scalar(prob[:, 0:128], prob[:, 0:128], small[:, 6:7], None, ALU.mult))
                nc.vector.tensor_scalar(prob[:, 128:384], prob[:, 128:384], small[:, 7:8], None,
                                        ALU.mult).then_inc(sem("prob_ready"), 1)
                split(j + 2, done=1)
            dve.wait_ge(sem("att_hi"), 4)
            nc.vector.tensor_tensor(h_lo[:, 3::4, T:2 * T], wide[:, 3, :].rearrange("p (a n) -> p a n", a=2),
                                    h_hi[:, 3::4, T:2 * T].bitcast(F32), ALU.subtract).then_inc(sem("att_lo"), 1)
            mod_bias(8, 20)
            coefficients(8, "g_ffn", mod_row(ADA_SC_F, 0))
            for i in range(4):
                split(LIN_BR + i + 2)
                n, two = i // 2, i % 2
                dve.wait_ge(sem("lin_done"), LIN_OPEN + LIN_BR + i + 1)
                if i == 0:
                    dve.wait_ge(sem("gates_ready"), 1)
                src = wide[:, 2 * two:2 * two + 2, :].rearrange("p b n -> p (b n)")
                g = gate[:, 2048 * two + 1024 * n:2048 * two + 1024 * (n + 1)]
                m = mix[:, 1024 * n:1024 * (n + 1)]
                if not two:
                    nc.vector.tensor_tensor(m, src, g, ALU.mult).then_inc(sem("br_evac"), 1)
                else:
                    if n:
                        dve.wait_ge(sem("mixed"), n)
                    nc.vector.tensor_tensor(mix2, src, g, ALU.mult).then_inc(sem("br_evac"), 1)
                    dve.wait_ge(sem("br_evac"), i + 1)
                    nc.vector.tensor_tensor(m, m, mix2, ALU.add).then_inc(sem("mixed"), 1)
                    dve.wait_ge(sem("mixed_hi"), n + 1)
                    nc.vector.tensor_tensor(h_lo[:, 4 * n:4 * n + 4, 0:T], m.rearrange("p (k n) -> p k n", n=T),
                                            h_hi[:, 4 * n:4 * n + 4, 0:T].bitcast(F32),
                                            ALU.subtract).then_inc(sem("mixed_lo"), 1)
            for i in range(4):
                split(LIN_OUT + i + 2)
                dve.wait_ge(sem("lin_done"), LIN_OPEN + LIN_OUT + i + 1)
                for t in range(2):
                    k = 2 * i + t
                    nc.vector.scalar_tensor_tensor(xs[:, k, 0:T], bank[i % 2][:, t * T:(t + 1) * T], shift_col(ADA_GT_M, k),
                                                   xs[:, k, 0:T], ALU.mult, ALU.add).then_inc(sem("out_evac"), 1)
            norm("ffn", 1, 8, norm_tmp, 2)

            def conv_taps(which, dst, c, first):
                dve.wait_ge(sem("tap2"), 4 * c + 2 * which + 2)
                for t in range(2):
                    tile = 2 * c + t + (22 if which else 0)
                    me.mark(nc.vector.scalar_tensor_tensor(dst[:, t, 1:T], bank[which][:, t * T:(t + 1) * T - 1],
                                                           col("w_conv", 44 + tile), dst[:, t, 1:T], ALU.mult, ALU.add))
                me.wait()
                for t in range(2):
                    tile = 2 * c + t + (22 if which else 0)
                    ins = nc.vector.scalar_tensor_tensor(dst[:, t, 2:T], bank[which][:, t * T:(t + 1) * T - 2],
                                                         col("w_conv", tile), dst[:, t, 2:T], ALU.mult, ALU.add)
                    if t == 0:
                        me.mark(ins)
                ins.then_inc(sem("gate_conv" if which else "value_conv"), 1)

            def product_lo(c):
                dve.wait_ge(sem("g_hi_done"), c + 1)
                nc.vector.tensor_tensor(g_lo[:, :, :], cv, g_hi[:, :, :].bitcast(F32), ALU.subtract).then_inc(sem("g_lo_done"), 1)

            split(LIN_FFN + 2)
            conv_taps(0, cv, 0, True)
            split(LIN_FFN + 3)
            conv_taps(1, cg, 0, True)
            product_lo(0)
            j0, r0 = LIN_FFN + 2, RAW_OF_LIN[LIN_FFN + 2]
            with dve.Fori(0, FF_STEPS - 1) as i:
                me.enter(i, 7)
                j = 3 * i + j0
                mod(i + E_SH + 1, (r0 + 2) % RAW, 16 * i + 16 * ((r0 + 2) // RAW + 1), j + 2, (j0 + 2) % SPL, True)
                split(j + 2, (j0 + 2) % SPL, (r0 + 3) % RAW, i + E_SH + 1)
                conv_taps(0, cv, i + 1, False)
                split(j + 3, (j0 + 3) % SPL, (r0 + 4) % RAW)
                conv_taps(1, cg, i + 1, False)
                split(j + 4, (j0 + 4) % SPL, (r0 + 5) % RAW)
                product_lo(i + 1)
            me.leave(FF_STEPS - 1)
            mod_bias(20, 24)
            mod_bias(24, 36)
            coefficients(16, "e_norm", mod_row(E_SC, 0))
            coefficients(24, "e_norm", mod_row(E_SC, 1))
            split(LIN_EIN + 1)
            norm("even_ctx", 2, 16, norm_tmp, 4)
            dve.wait_ge(sem("lin_done"), LIN_OPEN + LIN_EIN)
            for k in range(KT):
                nc.vector.scalar_tensor_tensor(xs[:, k, 0:T], wide[:, k // 2, (k % 2) * T:(k % 2 + 1) * T],
                                               shift_col(ADA_GT_F, k), xs[:, k, 0:T], ALU.mult,
                                               ALU.add).then_inc(sem("ffn_down_evac"), 1)
            dve.wait_ge(sem("rstd_ready"), 4)
            for k in range(KT):
                nc.vector.scalar_tensor_tensor(xs[:, k, 0:T], xs[:, k, 0:T], col("g_final", k), rstd[:, 0:T],
                                               ALU.mult, ALU.mult).then_inc(sem("final_scaled"), 1)
            norm("even_x", 4, 24, norm_tmp, 4)
            taps = 0
            for i in range(10):
                split(LIN_EIN + i + 2)
                if i in (2, 4):
                    dve.wait_ge(sem("ein_evac"), i)
                    dst = u_pad[:, i - 2:i, :, 15:15 + T]
                    nc.vector.tensor_tensor(dst, dst, glu.rearrange("p t (s n) -> p t s n", s=2),
                                            ALU.mult).then_inc(sem("glu_done"), 1)
                for t, k0, k1 in CONV_VECTOR.get(i, ()):
                    dve.wait_ge(sem("glu_done"), 1 if t == 0 else 2)
                    dve.wait_ge(sem("pads_set"), 2)
                    for k in range(k0, k1):
                        acc, src = conv_part(t, k, "vector")
                        if k == 0:
                            ins = nc.vector.tensor_scalar(acc, src, col("a_conv_w", t), col("a_conv_b", t), ALU.mult, ALU.add)
                        else:
                            dve.wait_ge(sem("conv_tap"), taps)
                            ins = nc.vector.scalar_tensor_tensor(acc, src, col("a_conv_w", 4 * k + t), acc, ALU.mult, ALU.add)
                        ins.then_inc(sem("conv_tap"), 1)
                        taps += 1
            dve.wait_ge(sem("ln_sum"), 1)
            for t in range(4):
                nc.vector.scalar_tensor_tensor(conv[:, t, :], bank[2][:, :], -1.0 / 512, conv[:, t, :],
                                               ALU.mult, ALU.add).then_inc(sem("centered"), 1)
            dve.wait_ge(sem("ln_std"), 1)
            me.mark(nc.vector.reciprocal(rstd[:, :], rstd[:, :]))
            me.wait()
            for t in range(6):
                if t < 4:
                    nc.vector.tensor_tensor(conv[:, t, :], conv[:, t, :], rstd[:, :], ALU.mult).then_inc(sem("ln_scaled"), 1)
                if t >= 2:
                    dve.wait_ge(sem("u_hi"), t - 1)
                    nc.vector.tensor_tensor(h_lo[:, t - 2, :], conv[:, t - 2, :], h_hi[:, t - 2, :].bitcast(F32),
                                            ALU.subtract).then_inc(sem("u_lo"), 1)
            split(LIN_PW + 2)
            for t in range(4):
                if t < 3:
                    dve.wait_ge(sem("pw_tile"), t + 1)
                else:
                    dve.wait_ge(sem("lin_done"), LIN_OPEN + LIN_PW + 1)
                nc.vector.scalar_tensor_tensor(ln_tmp[:, t, :], wide[:, t, :], col("pw_b", t), sgate[:, t, :],
                                               ALU.add, ALU.mult).then_inc(sem("y_a"), 1)
                dve.wait_ge(sem("y_hi"), t + 1)
                nc.vector.tensor_tensor(h_lo[:, 4 + t, :], ln_tmp[:, t, :], h_hi[:, 4 + t, :].bitcast(F32),
                                        ALU.subtract).then_inc(sem("y_lo"), 1)
            for t in range(4):
                dve.wait_ge(sem("y_hi"), 5 + t)
                nc.vector.tensor_tensor(h_lo[:, t, :], y_b[:, t, :], h_hi[:, t, :].bitcast(F32),
                                        ALU.subtract).then_inc(sem("y_lo"), 1)
            for i in range(4):
                split(LIN_EOUT + i + 2)
                dve.wait_ge(sem("lin_done"), LIN_OPEN + LIN_EOUT + i + 1)
                for t in range(2):
                    for s in range(2):
                        k = 2 * i + t
                        c = slice(s * T, (s + 1) * T)
                        nc.vector.scalar_tensor_tensor(xs[:, k, c], wide[:, 2 * (i % 2) + t, c], shift_col(E_GT, k, s),
                                                       xs[:, k, c], ALU.mult, ALU.add).then_inc(sem("eout_evac"), 1)
            mod_bias(36, 44)
            coefficients(32, "o_norm", mod_row(O_SC, 0))
            coefficients(40, "o_norm", mod_row(O_SC, 1))
            norm("odd_x", 5, 32, norm_tmp, 6)
            norm("odd_ctx", 6, 40, norm_tmp, 6)
            for i in range(3):
                split(LIN_OIN + i + 2)
            neg_sink = small[:, 8:16]
            me.mark(nc.vector.tensor_scalar(neg_sink, vec[:, VEC["sink"]:VEC["sink"] + 8], -1.0, None, ALU.mult))
            me.mark(nc.vector.memset(ccx[:, :, 0:1], 0.0))
            me.mark(nc.vector.memset(ccx[:, :, T + 1:T + 2], 0.0))
            dve.wait_ge(sem("q_raw"), 3)
            dve.wait_ge(sem("rot_done"), 1)
            for half in range(2):
                for n in range(2):
                    a = slice(512 * half + T * n, 512 * half + T * (n + 1))
                    me.mark(nc.vector.tensor_tensor(rot_tmp[:, a], bank[half][:, T * n:T * (n + 1)], rope_sin, ALU.mult))
                    me.mark(nc.vector.tensor_tensor(q_raw[:, a], q_raw[:, a], rope_cos, ALU.mult))
            me.wait()
            nc.vector.tensor_tensor(q_rot.rearrange("p t n -> p (t n)"), q_raw, rot_tmp, ALU.add).then_inc(sem("roped"), 1)
            me.mark(nc.vector.tensor_tensor(k_raw, k_raw, rope_cos, ALU.mult))
            dve.wait_ge(sem("roped"), 1)
            me.mark(nc.vector.tensor_tensor(rot_tmp[:, 0:T], bank[2][:, 0:T], rope_sin, ALU.mult))
            me.wait()
            nc.vector.tensor_tensor(k_all[:, 0:T], k_raw, rot_tmp[:, 0:T], ALU.add).then_inc(sem("roped"), 1)
            for u in range(16):
                if u < 10:
                    split(LIN_OIN + 3 + u + 2)
                h = (u // 2) % 4 + 4 * (u // 8)
                dve.wait_ge(sem("ws_done"), u + 1)
                me.mark(nc.vector.reduce_max(small[:, 60:61], bank[u % 2][:, :], AX_X, negate=True))
                me.wait()
                nc.vector.tensor_scalar(small[:, 16 + u:17 + u], small[:, 60:61], QK, neg_sink[:, h:h + 1],
                                        ALU.mult, ALU.min).then_inc(sem("wneg_max"), 1)
                if u < 4 and u % 2:
                    t = 2 * (u // 2)
                    dve.wait_ge(sem("lin_done"), LIN_OPEN + LIN_OIN + 3 + u + 1)
                    dve.wait_ge(sem("oin_evac"), u // 2 + 1)
                    dst = ccx[:, t:t + 2, 1:1 + T]
                    nc.vector.tensor_tensor(dst, dst, wide[:, 1, :].rearrange("p (t n) -> p t n", n=T),
                                            ALU.mult).then_inc(sem("ccx_done"), 1)
                dve.wait_ge(sem("wexp"), 2 * u + 2)
                s2 = small[:, 32 + 2 * (u % 2):34 + 2 * (u % 2)]
                den = small[:, 36:37]
                me.mark(nc.vector.tensor_tensor(den, s2[:, 0:1], s2[:, 1:2], ALU.add))
                me.wait()
                me.mark(nc.vector.reciprocal(small[:, 37:38], den))
                me.wait()
                nc.vector.tensor_scalar(w_prob[u % 2], w_prob[u % 2], small[:, 37:38], None,
                                        ALU.mult).then_inc(sem("wprob_ready"), 1)
                if u == 12:
                    dve.wait_ge(sem("ccx_done"), 2)
                    for t in range(4):
                        me.mark(nc.vector.tensor_scalar(y_c[:, t, :], ccx[:, t, 0:T], col("o_conv", t), None, ALU.mult))
                    me.wait()
                    for k in (1, 2):
                        for t in range(4):
                            me.mark(nc.vector.scalar_tensor_tensor(y_c[:, t, :], ccx[:, t, k:k + T], col("o_conv", 4 * k + t),
                                                                   y_c[:, t, :], ALU.mult, ALU.add))
                        me.wait()
                    dve.wait_ge(sem("oin_evac"), 4)
                    me.mark(nc.vector.tensor_tensor(y_c, y_c, cb, ALU.mult))
            dve.wait_ge(sem("silu_gates"), 1)
            me.wait()
            nc.vector.tensor_tensor(y_c, y_c, cg_ag[:, 0:4, :], ALU.mult).then_inc(sem("y_c"), 1)
            dve.wait_ge(sem("wpv_done"), 16)
            nc.vector.tensor_tensor(rot_tmp, wide[:, 2:4, :].rearrange("p b n -> p (b n)"),
                                    cg_ag[:, 4:8, :].rearrange("p t n -> p (t n)"), ALU.mult).then_inc(sem("y_d"), 1)
            for half, src in ((0, y_c), (1, rot_tmp.rearrange("p (t n) -> p t n", n=T))):
                dve.wait_ge(sem("yo_hi"), half + 1)
                nc.vector.tensor_tensor(h_lo[:, 4 * half:4 * half + 4, 0:T], src,
                                        h_hi[:, 4 * half:4 * half + 4, 0:T].bitcast(F32), ALU.subtract).then_inc(sem("yo_lo"), 1)
            mod_bias(44, 48)
            for i in range(4):
                split(LIN_OOUT + i + 2)
                dve.wait_ge(sem("lin_done"), LIN_OPEN + LIN_OOUT + i + 1)
                for t in range(2):
                    k = 2 * i + t
                    nc.vector.scalar_tensor_tensor(xs[:, k, 0:T], bank[i % 2][:, t * T:(t + 1) * T], shift_col(O_GT, k),
                                                   xs[:, k, 0:T], ALU.mult, ALU.add).then_inc(sem("oout_evac"), 1)
            dve.wait_ge(sem("rstd_ready"), 8)
            for k in range(KT):
                nc.vector.scalar_tensor_tensor(xs[:, k, 0:T], xs[:, k, 0:T], col("final_norm", k), rstd[:, 0:T],
                                               ALU.mult, ALU.mult).then_inc(sem("last_done"), 1)

        @block.tensor
        def _(pe):
            mm = nc.tensor.matmul
            ident, ones = c0[:, 0:P], c0[:, P:2 * P]

            def triple(out, w, x, start, stop, skip=False):
                for n, (a, b) in enumerate(((0, 0), (0, 1), (1, 0))):
                    last = mm(out, w[a], x[b], start=start and n == 0, stop=stop and n == 2, skip_group_check=skip)
                return last

            def whl(slot, a, n):
                return w_hi[:, slot, a:a + n], w_lo[:, slot, a:a + n]

            def hhl(k, a, n):
                return h_hi[:, k, a:a + n], h_lo[:, k, a:a + n]

            def features(j, slot, outs, a, n, order=None, ready=None):
                pe.wait_ge(sem("lo_done"), j + 1)
                order = order or [(k, k) for k in range(KT)]
                for m in range(2):
                    for i, (k, hk) in enumerate(order):
                        if ready and m == 0:
                            ready(hk)
                        last = triple(outs[m], whl(slot, 256 * k + P * m, P), hhl(hk, a, n), i == 0, i == KT - 1)
                last.then_inc(sem("lin_done"), 1)

            def tokens(j, slot, outs, a):
                pe.wait_ge(sem("lo_done"), j + 1)
                for m in range(2):
                    for k in range(KT):
                        last = triple(outs[m], hhl(k, a + P * m, P), whl(slot, 256 * k, 256), k == 0, k == KT - 1)
                last.then_inc(sem("lin_done"), 1)

            def halves(b):
                return b[:, 0:T], b[:, T:2 * T]

            def sum_squares(n, src, s):
                pe.wait_ge(sem("squares"), n + 1)
                if n:
                    pe.wait_ge(sem("rstd_ready"), n)
                for k in range(KT):
                    last = mm(bank[2][:, s * T:(s + 1) * T], ones, src[:, k, :], start=(k == 0), stop=(k == KT - 1))
                    if n == 0 and k == 0:
                        last.then_inc(sem("lin_done"), LIN_OPEN)
                last.then_inc(sem("sumsq"), 1)

            pe.wait_ge(sem("rel_loaded"), 32)
            pe.wait_ge(sem("rel_one"), 1)
            mm(bank[0][0:8, 0:384], rel[:, :], onehot, start=True, stop=True).then_inc(sem("bias_row"), 1)
            pe.wait_ge(sem("c0_loaded"), 16)
            sum_squares(0, norm_tmp, 0)
            pe.wait_ge(sem("norm_lo"), KT)
            pe.wait_ge(sem("bias_row_out"), 1)
            def qkv_step(i, n):
                j = 6 * i + n
                if not isinstance(i, int) or j >= 2:
                    pe.wait_ge(sem("proj_evac"), j - 1)
                (features if n < 4 else tokens)(*((j, n % SPL, halves(bank[n % 2])) + ((0, T) if n < 4 else (0,))))

            for i in range(2):
                for n in range(6):
                    qkv_step(i, n)

            def q_of(h, branch, a, b):
                t, p0 = h // 2, HD * (h % 2)
                return proj[p0:p0 + HD, 6 * branch + t // 2, (t % 2) * T + a:(t % 2) * T + b]

            def k_of(h, branch, a, b):
                t, p0 = h // 2, HD * (h % 2)
                return proj[p0:p0 + HD, 6 * branch + 2 + t // 2, (t % 2) * T + a:(t % 2) * T + b]

            def v_of(h, branch, m):
                return proj[:, 6 * branch + 4 + h // 4, m * T + (h % 4) * HD:m * T + (h % 4 + 1) * HD]

            def weighted_values(h):
                pe.wait_ge(sem("pt_ready"), h + 1)
                pe.wait_ge(sem("aw_ready"), h + 1)
                if h >= 2 and h % 2 == 0:
                    pe.wait_ge(sem("att_lo"), h // 2)
                p0 = HD * (h % 2)
                for branch, w in ((0, pt[h % 2]), (1, aw)):
                    c = branch * T
                    mm(wide[p0:p0 + HD, 3, c:c + T], v_of(h, branch, 0), w[:, 0:T], start=True, stop=False)
                    last = mm(wide[p0:p0 + HD, 3, c + P:c + T], v_of(h, branch, 1), w[:, T:T + P], start=False, stop=True)
                last.then_inc(sem("pv_done"), 1)

            pe.wait_ge(sem("proj_evac"), 12)
            pe.wait_ge(sem("c1_loaded"), 16)
            def transposed_probs(h):
                pe.wait_ge(sem("prob_ready"), h + 1)
                if h:
                    pe.wait_ge(sem("pt_ready"), h)
                nc.tensor.transpose(wide[:, 1, 0:128], prob[:, 0:128], ident)
                nc.tensor.transpose(wide[:, 1, 128:256], prob[:, 128:256], ident)
                nc.tensor.transpose(wide[:, 1, 256:384], prob[:, 256:384], ident).then_inc(sem("pt_done"), 1)

            def stick_exponents(h):
                pe.wait_ge(sem("sb_kept"), h + 1)
                if h:
                    pe.wait_ge(sem("sb_min"), h)
                e = bank[2]
                mm(e[:, 0:256], k_of(h, 1, 0, 128), q_of(h, 1, 0, 256), start=True, stop=False)
                mm(e[:, 0:256], tri8, sb_r[:, 0:256], start=False, stop=False)
                mm(e[:, 128:256], all8, sb_r[:, 256:384], start=False, stop=True)
                mm(e[:, 256:384], k_of(h, 1, 128, 256), q_of(h, 1, 128, 256), start=True, stop=False)
                mm(e[:, 256:384], tri8, sb_r[:, 256:384], start=False, stop=True).then_inc(sem("e_done"), 1)

            for h in range(NH + 1):
                if h < NH:
                    pe.wait_ge(sem(f"trev_loaded{h % TREV}"), 16 * (h // TREV + 1))
                    if h:
                        pe.wait_ge(sem("exp_done"), 2 * h)
                        pe.wait_ge(sem("sb_relu"), h)
                    mm(wide[:, 0, 0:128], q_of(h, 0, 0, 128), k_of(h, 0, 0, 128), start=True, stop=False)
                    mm(wide[:, 0, 0:128], anti8, trev[:, h % TREV, 128:256], start=False, stop=True)
                    mm(wide[:, 0, 128:384], q_of(h, 0, 128, 256), k_of(h, 0, 0, 256), start=True, stop=False)
                    mm(wide[:, 0, 128:384], anti8, trev[:, h % TREV, :], start=False, stop=True)
                    mm(wide[:, 2, 0:256], k_of(h, 1, 0, 128), q_of(h, 1, 0, 256), start=True, stop=True)
                    mm(wide[:, 2, 256:384], k_of(h, 1, 128, 256), q_of(h, 1, 128, 256), start=True,
                       stop=True).then_inc(sem("qk_done"), 1)
                if h:
                    transposed_probs(h - 1)
                    stick_exponents(h - 1)
                if h < NH:
                    if h >= 2:
                        pe.wait_ge(sem("gate_evac"), h - 1)
                    j = LIN_GATE + h
                    features(j, j % SPL, halves(bank[j % 2]), 0, T)
                if h:
                    weighted_values(h - 1)
            for i in range(4):
                j = LIN_BR + i
                pe.wait_ge(sem("lo_done"), j + 1)
                if i == 0:
                    pe.wait_ge(sem("att_lo"), 4)
                if i >= 2:
                    pe.wait_ge(sem("br_evac"), i - 1)
                for m in range(4):
                    out = wide[:, 2 * (i % 2) + m // 2, (m % 2) * T:(m % 2 + 1) * T]
                    for k in range(4):
                        last = triple(out, whl(j % SPL, 512 * k + P * m, P), hhl(4 * (i % 2) + k, T, T), k == 0, k == 3)
                last.then_inc(sem("lin_done"), 1)
            pe.wait_ge(sem("mixed_lo"), 2)
            pe.wait_ge(sem("gate_evac"), 8)
            for i in range(4):
                j = LIN_OUT + i
                if i >= 2:
                    pe.wait_ge(sem("out_evac"), 2 * (i - 1))
                features(j, j % SPL, halves(bank[i % 2]), 0, T)
            sum_squares(1, norm_tmp, 0)
            pe.wait_ge(sem("zeros_set"), 1)
            for b in range(4):
                mm(wide[:, b, :], zeros[:, 0:P], zeros[:, :], start=True, stop=False, skip_group_check=True)

            def down(j, slot, c):
                pe.wait_ge(sem("lo_done"), j + 1)
                pe.wait_ge(sem("g_lo_done"), c + 1)
                for k in range(2):
                    for m in range(KT):
                        last = triple(wide[:, m // 2, (m % 2) * T:(m % 2 + 1) * T], whl(slot, 1024 * k + P * m, P),
                                      (g_hi[:, k, :], g_lo[:, k, :]), False, True, skip=True)
                last.then_inc(sem("lin_done"), 1)

            pe.wait_ge(sem("norm_lo"), 2 * KT)
            features(LIN_FFN, LIN_FFN % SPL, halves(bank[0]), 0, T)
            features(LIN_FFN + 1, (LIN_FFN + 1) % SPL, halves(bank[1]), 0, T)
            j0, r0 = LIN_FFN + 2, RAW_OF_LIN[LIN_FFN + 2]
            with pe.Fori(0, FF_STEPS - 1) as i:
                j = 3 * i + j0
                pe.wait_ge(sem("value_conv"), i + 1)
                features(j, j0 % SPL, halves(bank[0]), 0, T)
                pe.wait_ge(sem("gate_conv"), i + 1)
                features(j + 1, (j0 + 1) % SPL, halves(bank[1]), 0, T)
                down(j + 2, (j0 + 2) % SPL, i)
            sum_squares(2, norm_tmp, 1)
            down(LIN_EIN - 1, (LIN_EIN - 1) % SPL, FF_STEPS - 1)
            sum_squares(3, norm_tmp, 0)
            sum_squares(4, norm_tmp, 0)
            pe.wait_ge(sem("c2_loaded"), 48)
            mm(bank[0][:, :], dft_d[:, 0:P], fw, start=True, stop=True)
            mm(bank[1][:, :], dft_d[:, P:2 * P], fw, start=True, stop=True).then_inc(sem("fold_done"), 1)
            pe.wait_ge(sem("norm_lo"), 4 * KT)

            def fourier_a(g):
                if g:
                    pe.wait_ge(sem("four_ready"), 2 * g)
                else:
                    pe.wait_ge(sem("fold_ready"), 2)
                    pe.wait_ge(sem("ein_evac"), 6)
                for s in range(2):
                    for lt in range(2):
                        last = mm(bank[2 * s][:, lt * T:(lt + 1) * T], b_val[:, g, s * T + lt * P:s * T + (lt + 1) * P],
                                  fold[:, g, :, :].rearrange("p c n -> p (c n)"), start=True, stop=True)
                    last.then_inc(sem("four_a"), 1)

            def fourier_b(g):
                pe.wait_ge(sem("four_ready"), 2 * g + 2)
                if g:
                    pe.wait_ge(sem("y_b_raw"), g)
                for s in range(2):
                    for q, (part, table) in enumerate(((0, cos_l), (1, sin_l))):
                        for lt in range(2):
                            last = mm(bank[1][:, s * T:(s + 1) * T], four[s][:, lt * T + part * P:lt * T + (part + 1) * P],
                                      table[:, lt, :], start=(q == 0 and lt == 0), stop=(q == 1 and lt == 1))
                last.then_inc(sem("four_b"), 1)

            for i in range(10):
                j = LIN_EIN + i
                b = 2 * (i % 2)
                if i >= 2:
                    pe.wait_ge(sem("ein_evac"), i - 1)
                features(j, j % SPL, (wide[:, b, :], wide[:, b + 1, :]), 0, 2 * T)
                if i >= 7:
                    fourier_b(i - 7)
                if i >= 6:
                    fourier_a(i - 6)
            fourier_b(3)
            pe.wait_ge(sem("four_ready"), 8)
            for n, t in enumerate((0, 2, 1, 3)):
                if t != 1:
                    pe.wait_ge(sem("conv_tap"), CONV_W * {0: 1, 2: 2, 3: 3}[t])
                if t in (1, 3):
                    pe.wait_ge(sem("prod_used"), (CONV_W - 1) * (1 if t == 1 else 2))
                last = mm(bank[2][:, :], ones, conv[:, t, :], start=(n == 0), stop=(n == 3))
            last.then_inc(sem("ln_sum"), 1)
            for t in range(4):
                pe.wait_ge(sem("ln_squares"), t + 1)
                last = mm(bank[3][:, :], ones, ln_tmp[:, t, :], start=(t == 0), stop=(t == 3))
            last.then_inc(sem("ln_sumsq"), 1)
            pe.wait_ge(sem("lo_done"), LIN_PW + 1)
            pe.wait_ge(sem("ein_evac"), 10)
            for m in range(4):
                for k in range(4):
                    if m == 0:
                        pe.wait_ge(sem("u_lo"), k + 1)
                    last = triple(wide[:, m, :], whl(LIN_PW % SPL, 512 * k + P * m, P), hhl(k, 0, 2 * T), k == 0, k == 3)
                last.then_inc(sem("pw_tile" if m < 3 else "lin_done"), 1)
            for i in range(4):
                j = LIN_EOUT + i
                b = 2 * (i % 2)
                if i >= 2:
                    pe.wait_ge(sem("eout_evac"), 4 * (i - 1))
                features(j, j % SPL, (wide[:, b, :], wide[:, b + 1, :]), 0, 2 * T, [(k, (k + 4) % KT) for k in range(KT)],
                         None if i else lambda hk: pe.wait_ge(sem("y_lo"), (hk + 4) % KT + 1))
            sum_squares(5, norm_tmp, 0)
            sum_squares(6, norm_tmp, 1)
            pe.wait_ge(sem("norm_lo"), 5 * KT)
            pe.wait_ge(sem("eout_evac"), 16)
            for i in range(2):
                features(LIN_OIN + i, (LIN_OIN + i) % SPL, halves(wide[:, i, :]), 0, T)
            j = LIN_OIN + 2
            pe.wait_ge(sem("norm_lo"), 6 * KT)
            pe.wait_ge(sem("lo_done"), j + 1)
            for k in range(KT):
                triple(wide[:, 2, :], whl(j % SPL, 256 * k, P), hhl(k, 0, 2 * T), k == 0, k == KT - 1)
            for tt in range(4):
                for k in range(KT):
                    last = triple(wide[:, 3, tt * P:(tt + 1) * P], hhl(k, tt * P, P), whl(j % SPL, 256 * k + P, P),
                                  k == 0, k == KT - 1)
            last.then_inc(sem("lin_done"), 1)
            pe.wait_ge(sem("q_raw"), 3)
            pe.wait_ge(sem("rstd_ready"), 7)
            pe.wait_ge(sem("c3_loaded"), 16)
            mm(bank[0][:, :], swap, q_raw[:, 0:512], start=True, stop=True)
            mm(bank[1][:, :], swap, q_raw[:, 512:1024], start=True, stop=True)
            mm(bank[2][:, 0:T], swap, k_raw, start=True, stop=True).then_inc(sem("rot_done"), 1)
            pe.wait_ge(sem("roped"), 2)
            pe.wait_ge(sem("kv_evac"), 2)

            def unit(u):
                return (u // 2) % 4, u // 8, u % 2

            for u in range(18):
                if u < 16:
                    t, b, qt = unit(u)
                    p0 = HD * b
                    if u >= 2:
                        pe.wait_ge(sem("wexp"), 2 * (u - 1) - 1)
                    keys = slice(P, 2 * P) if qt == 0 else slice(0, P)
                    mm(bank[u % 2][:, :], q_rot[p0:p0 + HD, t, qt * P:(qt + 1) * P], k_all[p0:p0 + HD, :],
                       start=True, stop=False)
                    mm(bank[u % 2][:, keys], ident, band[:, qt * P:(qt + 1) * P], start=False,
                       stop=True).then_inc(sem("ws_done"), 1)
                if u < 10:
                    j = LIN_OIN + 3 + u
                    if u >= 2:
                        n = u - 2
                        if n < 4 and n % 2:
                            pe.wait_ge(sem("ccx_done"), n // 2 + 1)
                        else:
                            pe.wait_ge(sem("oin_evac"), n // 2 + 1 if n < 4 else n - 1)
                    features(j, j % SPL, halves(wide[:, u % 2, :]), 0, T)
                if 1 <= u < 17:
                    v = u - 1
                    pe.wait_ge(sem("wprob_ready"), v + 1)
                    if v >= 2:
                        pe.wait_ge(sem("wpt_ready"), v - 1)
                    for k in range(4):
                        last = nc.tensor.transpose(bank[2 + v % 2][:, k * P:(k + 1) * P],
                                                   w_prob[v % 2][:, k * P:(k + 1) * P], ident)
                    last.then_inc(sem("wt_done"), 1)
                if u >= 2:
                    v = u - 2
                    t, b, qt = unit(v)
                    pe.wait_ge(sem("wpt_ready"), v + 1)
                    out = wide[HD * b:HD * (b + 1), 2 + t // 2, (t % 2) * T + qt * P:(t % 2) * T + (qt + 1) * P]
                    for k in range(4):
                        last = mm(out, v_tok[:, k, HD * b:HD * (b + 1)], w_pt[v % 2][:, k * P:(k + 1) * P],
                                  start=(k == 0), stop=(k == 3))
                    last.then_inc(sem("wpv_done"), 1)
            pe.wait_ge(sem("yo_lo"), 2)
            for i in range(4):
                j = LIN_OOUT + i
                if i >= 2:
                    pe.wait_ge(sem("oout_evac"), 2 * (i - 1))
                features(j, j % SPL, halves(bank[i % 2]), 0, T)
            sum_squares(7, norm_tmp, 0)


def shape_constants():
    f = np.float32
    i, j = np.meshgrid(np.arange(P), np.arange(P), indexing="ij")
    c0 = np.concatenate([np.eye(P), np.ones((P, P))], 1).astype(f)
    c1 = np.zeros((P, N_C1), f)
    c1[:, 0:128] = 8.0 * (i + j == P - 1)
    c1[:, 128:256] = -8.0 * (i >= j)
    c1[:, 256:384] = -8.0
    past = np.concatenate([i < j, np.ones((P, P), bool), i < j], 1)
    c1[:, 384:768] = past
    c1[:, 768:1152] = np.where(past, BIG, NEG)
    dist = 255 - np.arange(383)
    n = np.maximum(dist, 0)
    n_f = np.maximum(n, 16).astype(f)
    large = 16 + (np.log(n_f / f(16)) / f(np.log(128 / 16)) * f(16)).astype(np.int32)
    bucket = np.where(n < 16, n, np.minimum(large, 31))
    hot = np.zeros((33, 384), f)
    hot[:32, :383] = (np.arange(32)[:, None] == bucket[None, :]) & (dist >= 0)[None, :]
    hot[32, :383] = np.where(dist >= 0, 0.0, NEG)
    c1[0:33, 1152:1536] = hot
    l = np.arange(T)
    ang = 2 * np.pi * (np.outer(l, l) % T) / T
    scale = 1.0 / np.sqrt(T * P)
    cos_l = (np.cos(ang) * scale).reshape(2, P, T).transpose(1, 0, 2).reshape(P, 512)
    sin_l = (-np.sin(ang) * scale).reshape(2, P, T).transpose(1, 0, 2).reshape(P, 512)
    d = np.arange(P)
    ang = 2 * np.pi * (np.outer(d, d) % P) / P
    pos = np.arange(T)
    row, cl = (pos // 64).astype(f), (pos % 64).astype(f)
    inv = np.power(f(10000.0), -np.arange(16, dtype=f) / f(16)).astype(f)
    r = np.arange(P) % HD
    coord = np.where((r // 32 == 0)[:, None], row[None, :], cl[None, :])
    a = (coord * inv[r % 16][:, None]).astype(f)
    sign = np.where((r % 32) // 16 == 0, -1.0, 1.0)[:, None]
    partner = np.where((np.arange(P) % 32) // 16 == 0, np.arange(P) + 16, np.arange(P) - 16)
    swap = (np.arange(P)[:, None] == partner[None, :]).astype(f)
    band = np.concatenate([np.where(j <= i, 0.0, 8 * NEG), np.where(j >= i, 0.0, 8 * NEG)], 1)
    c2 = np.concatenate([cos_l, sin_l, np.cos(ang), np.sin(ang)], 1).astype(f)
    c3 = np.concatenate([np.cos(a), np.sin(a) * sign, swap, band], 1).astype(f)
    assert c2.shape == (P, N_C2) and c3.shape == (P, N_C3)
    return c0, c1, c2, c3


def k8(w):
    n = w.shape[1] // 256
    return list(w.reshape(8, P, n, 256).transpose(2, 1, 0, 3).reshape(n, P, CHUNK))


def transposed(w):
    n = w.shape[1] // 256
    return list(w.T.reshape(n, 2, P, 1024).transpose(0, 2, 1, 3).reshape(n, P, CHUNK))


def k4(w):
    n = w.shape[1] // 512
    return list(w.reshape(4, P, n, 512).transpose(2, 1, 0, 3).reshape(n, P, CHUNK))


def k2(w):
    n = w.shape[0] // 256
    return list(w.reshape(n, 2, P, 1024).transpose(0, 2, 1, 3).reshape(n, P, CHUNK))


def tiles(v):
    return v.reshape(-1, P).T


def rows(m):
    return np.concatenate([tiles(r) for r in m], 1)


def kernel(**inputs):
    import concourse.bacc as bacc
    from concourse.bass_utils import run_bass_kernel_spmd as run

    a = {k: np.asarray(v) for k, v in inputs.items()}
    x, cx = a["x"][0], a["ctx_2"][0]
    xs = np.concatenate([x.T.reshape(8, P, T), cx.T.reshape(8, P, T)], 2).transpose(1, 0, 2)

    wi = a["w_in"][0]
    part = [wi[:, 512 * i:512 * (i + 1)] for i in range(6)] + [wi[:, 3072:]]
    lin = []
    for b in (0, 3):
        for n in range(3):
            lin += k8(part[b + n])
    lin += k8(part[6])
    bm, bs = k4(a["w_br_moba"][0]), k4(a["w_br_sb"][0])
    lin += [bm[0], bs[0], bm[1], bs[1]]
    lin += k8(a["w_out"][0])
    up = a["w_up"][0]
    uv, ug, dn = k8(up[:, :2816]), k8(up[:, 2816:]), k2(a["w_down"][0])
    lin += [uv[0], ug[0]]
    for i in range(10):
        lin += [uv[i + 1], ug[i + 1], dn[i]]
    lin += [dn[10]]
    ei = a["e_w_in_2"][0]
    av, ag, at, bv, bg = (k8(ei[:, 512 * i:512 * (i + 1)]) for i in range(5))
    lin += [av[0], ag[0], av[1], ag[1]] + bv + at + bg
    lin += k4(a["e_a_pw_w_2"][0])
    lin += k8(a["e_w_out_2"][0])
    oi = a["o_w_in_2"][0]
    heads = [0, 4, 1, 5, 2, 6, 3, 7]
    hperm = np.concatenate([np.arange(HD * h, HD * (h + 1)) for h in heads])
    cb, cc, cxx, cg = (k8(oi[:, 512 * i:512 * (i + 1)]) for i in range(4))
    q, kv, og = oi[:, 2048:2560][:, hperm], oi[:, 2560:2816], oi[:, 2816:3328][:, hperm]
    lin += k8(q) + k8(kv) + [cc[0], cxx[0], cc[1], cxx[1]] + cb + cg + k8(og)
    oo = a["o_w_out_2"][0]
    lin += k8(np.concatenate([oo[:512], oo[512:][hperm]], 0))
    assert len(lin) == N_LIN
    ada = a["w_ada"][0]
    sh_m, sc_m, gt_m, sh_f, sc_f, gt_f = (transposed(ada[:, D * i:D * (i + 1)]) for i in range(6))
    mod = sc_m + sh_m + gt_m + sh_f + sc_f + gt_f
    for w in (a["e_w_mod_2"][0], a["o_w_mod_2"][0]):
        sh, sc, gt = (transposed(w[:, D * i:D * (i + 1)]) for i in range(3))
        mod += sc + sh + gt
    assert len(mod) == N_MOD
    w = np.stack([(lin if kind == "lin" else mod)[n] for kind, n in ORDER])

    cond = np.stack([a["c"][0], a["c_2"][0], a["c_ctx_2"]])
    ba = a["b_ada"][0]
    bias = [ba[D:2 * D], ba[:D], ba[2 * D:3 * D], ba[3 * D:4 * D], ba[4 * D:5 * D], ba[5 * D:]]
    for b in (a["e_b_mod_2"][0], a["o_b_mod_2"][0]):
        bias += [b[D:2 * D], b[:D], b[2 * D:]]
    bias = np.repeat(tiles(np.concatenate(bias)), 2, axis=1)
    sink = np.broadcast_to(a["o_sink_2"][0][None, :], (P, 8))
    vec = np.concatenate([bias, tiles(a["g_mix"][0]), tiles(a["g_ffn"][0]), tiles(a["g_final"]),
                          tiles(a["e_norm_2"][0]), tiles(a["o_norm_2"][0]), tiles(a["final_norm_2"]),
                          rows(a["w_conv"][0]), tiles(a["b_conv"][0]), rows(a["e_a_conv_w_2"][0]),
                          tiles(a["e_a_conv_b_2"][0]), tiles(a["e_a_ln_g_2"][0]), tiles(a["e_a_ln_b_2"][0]),
                          tiles(a["e_a_pw_b_2"][0]), rows(a["o_c_conv_w_2"][0]), sink], 1)
    assert vec.shape == (P, N_VEC)
    fw = a["e_b_fw_2"][0].transpose(1, 0, 2).reshape(P, 512)
    c0, c1, c2, c3 = shape_constants()
    arrays = {"xs": xs, "cond": cond, "vec": vec, "rel": a["rel_bias"].T, "w": w, "fw": fw, "c0": c0, "c1": c1,
              "c2": c2, "c3": c3}
    arrays = {k: np.ascontiguousarray(v) for k, v in arrays.items()}

    nc = bacc.Bacc("TRN2", target_bir_lowering=False, num_devices=1)
    aps = [nc.dram_tensor("in_" + k, v.shape, F32, kind="ExternalInput").ap() for k, v in arrays.items()]
    diff = nc.dram_tensor("diff", (8, 384), F32).ap()
    out = nc.dram_tensor("out", (P, KT, T), F32, kind="ExternalOutput").ap()
    build(nc, *aps, diff, out)
    r = run(nc, [{"in_" + k: v for k, v in arrays.items()}], core_ids=[0])
    return r.results[0]["out"].transpose(2, 1, 0).reshape(1, T, D)
```

```python
import numpy as np
from contextlib import ExitStack

import concourse.bass as bass
from concourse import mybir

F32 = mybir.dt.float32
F32R = mybir.dt.float32r
BF16 = mybir.dt.bfloat16
ALU = mybir.AluOpType
ACT = mybir.ActivationFunctionType
AX_X = mybir.AxisListType.X

P = 128
T = 256
D = 1024
KT = D // P
HD = 64
NH = 8
FF_STEPS = 11
CHUNK = 2048
RAW = 4
SPL = 3
EPS = 1e-6
NEG = -1e30
BIG = 3.0e38
QK = 0.125

LIN_QKV, LIN_GATE, LIN_BR, LIN_OUT, LIN_FFN = 0, 12, 20, 24, 28
LIN_EIN = LIN_FFN + 3 * FF_STEPS
LIN_PW = LIN_EIN + 10
LIN_EOUT = LIN_PW + 1
LIN_OIN = LIN_EOUT + 4
LIN_OOUT = LIN_OIN + 13
N_LIN = LIN_OOUT + 4
OIN_PARTS = {u: [(u, 0), (u, 1)] if u < 4 else [(4 + (u - 4) // 2, u % 2)] for u in range(16)}
OIN_CHUNK = {u: parts[-1][0] for u, parts in OIN_PARTS.items() if parts[-1][1] == 1}
MOD_FIRST = 8
N_MOD = 48
LIN_OPEN = 1
ADA_SC_M, ADA_SH_M, ADA_GT_M, ADA_SH_F, ADA_SC_F, ADA_GT_F = 0, 4, 8, 12, 16, 20
E_SC, E_SH, E_GT, O_SC, O_SH, O_GT = 24, 28, 32, 36, 40, 44

CONV_W = 31
CONV_VECTOR = {2: [(0, 0, 13)], 3: [(0, 13, 25)], 4: [(0, 25, 31), (2, 0, 4)], 5: [(2, 4, 16)], 6: [(2, 16, 28)],
               7: [(2, 28, 31), (3, 0, 14)], 8: [(3, 14, 31)]}
CONV_SCALAR = {2: [(1, 0, 7)], 3: [(1, 7, 14)], 4: [(1, 14, 21)], 5: [(1, 21, 28)], 6: [(1, 28, 31), (3, 0, 6)],
               7: [(3, 6, 17)], 8: [(3, 17, 28)], 9: [(3, 28, 31)]}
PRODS = 3


def stream_order():
    order = [("lin", 0)] + [("mod", m) for m in range(MOD_FIRST)]
    m = MOD_FIRST
    for j in range(LIN_BR + 3):
        order += [("lin", j)] if j else []
        n = int(j % 3 == 2) if j < LIN_GATE else 0 if j == LIN_GATE else 2 if j < LIN_BR - 1 else 1
        order += [("mod", m + k) for k in range(n)]
        m += n
    order += [("lin", j) for j in range(LIN_BR + 3, LIN_FFN + 1)]
    order += [("mod", m), ("lin", LIN_FFN + 1)]
    m += 1
    for i in range(FF_STEPS - 1):
        j = LIN_FFN + 2 + 3 * i
        order += [("lin", j), ("lin", j + 1), ("mod", m), ("lin", j + 2)]
        m += 1
    order += [("lin", LIN_EIN - 1)]
    for j in range(LIN_EIN, N_LIN):
        n = int(LIN_EIN + 2 <= j < LIN_EIN + 4 or LIN_EOUT < j < LIN_EOUT + 4 or LIN_OIN + 4 <= j < LIN_OIN + 8)
        order += [("mod", m + k) for k in range(n)]
        m += n
        order += [("lin", j)]
    assert m == N_MOD
    return order


ORDER = stream_order()
RAW_OF_LIN = [0] * N_LIN
RAW_OF_MOD = [0] * N_MOD
for _r, (_kind, _n) in enumerate(ORDER):
    (RAW_OF_LIN if _kind == "lin" else RAW_OF_MOD)[_n] = _r

VEC_SIZES = [("mod_bias", 4 * N_MOD), ("g_mix", 8), ("g_ffn", 8), ("g_final", 8),
             ("e_norm", 8), ("o_norm", 8), ("final_norm", 8), ("w_conv", 132), ("b_conv", 44),
             ("a_conv_w", 124), ("a_conv_b", 4), ("ln_g", 4), ("ln_b", 4), ("pw_b", 4),
             ("o_conv", 12), ("sink", 8)]
VEC = {}
_at = 0
for _n, _s in VEC_SIZES:
    VEC[_n] = _at
    _at += _s
N_VEC = _at

C0 = {"ident": 0, "ones": 128}
N_C0 = 256
N_C1 = 1536
N_C2 = 1280
N_C3 = 896


def mod_col(m, t, v):
    return 4 * m + 2 * t + v


def build(nc, xs_d, cond_d, vec_d, rel_d, w_d, fw_d, c0_d, c1_d, c2_d, c3_d, diff_d, out_d):
    ctx = ExitStack()
    with ctx:
        def sb(name, shape, dt=F32):
            return ctx.enter_context(nc.sbuf_tensor(name, shape, dt))

        sems = {}

        def sem(name):
            if name not in sems:
                sems[name] = ctx.enter_context(nc.semaphore(name))
            return sems[name]

        raw = sb("raw", [P, RAW, CHUNK])
        w_hi = sb("w_hi", [P, SPL, CHUNK], F32R)
        w_lo = sb("w_lo", [P, SPL, CHUNK], F32R)
        h_hi = sb("h_hi", [P, KT, 2 * T], F32R)
        h_lo = sb("h_lo", [P, KT, 2 * T], F32R)
        g_hi = sb("g_hi", [P, 2, T], F32R)
        g_lo = sb("g_lo", [P, 2, T], F32R)
        xs = sb("xs", [P, KT, 2 * T])
        vec = sb("vec", [P, N_VEC])
        c0 = sb("c0", [P, N_C0])
        modv = sb("modv", [P, 4 * N_MOD])
        coef = sb("coef", [P, 48])
        small = sb("small", [P, 64])
        zeros = sb("zeros", [P, 512], BF16)
        rel = sb("rel", [33, 8])
        consts = sb("consts", [P, 2048])
        cond = sb("cond", [P, 2, D])
        arena = sb("arena", [P, 10496])
        att = sb("att", [P, 7 * 384])
        rstd = sb("rstd", [P, 2 * T])
        bank = [ctx.enter_context(nc.psum_tensor(f"bank{i}", [P, 512], F32)) for i in range(4)]
        wide = ctx.enter_context(nc.psum_tensor("wide", [P, 4, 512], F32))

        proj = arena[:, 0:6144].rearrange("p (c n) -> p c n", n=512)
        gate = arena[:, 6144:10240]
        cond_ada = gate[:, 3072:4096]
        onehot = gate[0:33, 2048:2432]
        urow = gate[0:8, 2432:2816]
        norm_tmp = att[:, 0:2048].rearrange("p (k n) -> p k n", n=T)
        gain_sq = arena[:, 4096:6144].rearrange("p (k n) -> p k n", n=T)
        rstd2 = arena[:, 6144:6400]
        TREV = 3
        trev = consts[:, 1152:1152 + TREV * T].rearrange("p (h n) -> p h n", n=T)
        anti8, tri8, all8 = (consts[:, P * i:P * (i + 1)] for i in range(3))
        past, bound = consts[:, 384:768], consts[:, 768:1152]
        prob, sb_t, sb_r, sb_e = (att[:, 384 * i:384 * (i + 1)] for i in range(4))
        pt = [att[:, 384 * 4:384 * 5], att[:, 384 * 5:384 * 6]]
        aw = att[:, 384 * 6:384 * 7]
        mix = arena[:, 0:2048]
        mix2 = arena[:, 2048:3072]
        cv = arena[:, 3072:3584].rearrange("p (t n) -> p t n", n=T)
        cg = arena[:, 3584:4096].rearrange("p (t n) -> p t n", n=T)
        cos_l = consts[:, 0:512].rearrange("p (l n) -> p l n", n=T)
        sin_l = consts[:, 512:1024].rearrange("p (l n) -> p l n", n=T)
        dft_d = att[:, 2048:2304]
        fw = consts[:, 1024:1536]
        fold = consts[:, 1024:2048].rearrange("p (g c n) -> p g c n", g=4, c=2)
        UW = T + 30
        u_pad = arena[:, 0:4 * 2 * UW].rearrange("p (t s n) -> p t s n", t=4, s=2)
        b_val = arena[:, 2304:4352].rearrange("p (t n) -> p t n", n=512)
        sgate = arena[:, 4352:8448].rearrange("p (t n) -> p t n", n=512)
        conv = arena[:, 8448:10496].rearrange("p (t n) -> p t n", n=512)
        ln_tmp = arena[:, 0:2048].rearrange("p (t n) -> p t n", n=512)
        glu = arena[:, 4352:5376].rearrange("p (t n) -> p t n", n=512)
        y_b = b_val
        four = [att[:, 0:512], att[:, 512:1024]]
        conv_prod = [att[:, 1024 + 512 * n:1536 + 512 * n] for n in range(PRODS)]
        q_raw = arena[:, 0:1024]
        q_rot = arena[:, 1024:2048].rearrange("p (t n) -> p t n", n=T)
        k_all = arena[:, 2048:2560]
        k_raw = arena[:, 2560:2816]
        v_tok = arena[:, 3072:3584].rearrange("p (t n) -> p t n", n=P)
        rot_tmp = arena[:, 3584:4608]
        ccx = arena[:, 4608:4608 + 4 * 258].rearrange("p (t n) -> p t n", n=258)
        cb = arena[:, 5696:6720].rearrange("p (t n) -> p t n", n=T)
        cg_ag = arena[:, 6720:8768].rearrange("p (t n) -> p t n", n=T)
        y_c = arena[:, 0:1024].rearrange("p (t n) -> p t n", n=T)
        c3 = arena[:, 9472:9472 + N_C3]
        rope_cos, rope_sin, swap, band = c3[:, 0:256], c3[:, 256:512], c3[:, 512:640], c3[:, 640:896]
        w_prob = [att[:, 0:512], att[:, 512:1024]]
        w_pt = [att[:, 1024:1536], att[:, 1536:2048]]

        def col(name, i):
            return vec[:, bass.ds(VEC[name] + i, 1)]

        def modc(m, t, v=0):
            return modv[:, mod_col(m, t, v):mod_col(m, t, v) + 1]

        def shift_col(base, k, v=0):
            return modc(base + k // 2, k % 2, v)

        def conv_part(t, k, engine):
            acc, src = conv[:, t, :].rearrange("p (s n) -> p s n", s=2), u_pad[:, t, :, k:k + T]
            if t == 3:
                s = 0 if engine == "vector" else 1
                acc, src = acc[:, s, :], src[:, s, :]
            return acc, src

        def mod_row(base, v):
            return modv[:, 4 * base:4 * base + 16].rearrange("p (k v) -> p k v", v=2)[:, :, v]

        class Steps:

            def __init__(self, eng, name):
                self.eng, self.sem, self.base, self.off = eng, sem(name), 0, 0

            def mark(self, ins):
                self.base += 1
                ins.then_inc(self.sem, 1)

            def value(self):
                return self.off + self.base

            def wait(self):
                self.eng.wait_ge(self.sem, self.value())

            def enter(self, i, per):
                self.off, self.per, self.start = i * per, per, self.base

            def leave(self, count):
                assert self.base - self.start == self.per, (self.base, self.start, self.per)
                self.base = self.start + self.per * count
                self.off = 0

        NORMS = {"mix": (0, 0, 0, (ADA_SH_M, 0), 0), "even_ctx": (1, 1, 24, (E_SH, 1), 24),
                 "ffn": (2, 0, 8, (ADA_SH_F, 0), 8), "even_x": (3, 0, 16, (E_SH, 0), 16),
                 "odd_x": (4, 0, 32, (O_SH, 0), 32), "odd_ctx": (5, 1, 40, (O_SH, 1), 40),
                 "last": (6, 0, None, None, None)}

        def square_tmp(name):
            return gain_sq if name == "odd_ctx" else norm_tmp

        def squares_before(n):
            return KT * (n + (n > 3))

        block = ctx.enter_context(nc.Block())

        @block.sync
        def _(sp):
            def load(r, slot, freed=None):
                if freed is not None:
                    sp.wait_ge(sem("lo_done" if freed[0] == "lin" else "mod_done"), freed[1] + 1)
                src = w_d[bass.ds(r, 1), :, :].rearrange("a p n -> (a p) n")
                sp.dma_start(raw[:, slot, :], src).then_inc(sem(f"arrived{slot}"), 16)

            for r in range(MOD_FIRST + 4):
                load(r, r % RAW, ORDER[r - RAW] if r >= RAW else None)
            sp.wait_ge(sem("mod_done"), MOD_FIRST)
            with sp.Fori(0, LIN_GATE // 3) as i:
                for n in range(4):
                    load(4 * i + MOD_FIRST + 4 + n, n, ("lin", 3 * i + n) if n < 3 else ("mod", i + MOD_FIRST))
            r0 = RAW_OF_LIN[LIN_FFN]
            for r in range(RAW_OF_LIN[LIN_GATE] + 4, r0 + 3):
                load(r, r % RAW, ORDER[r - RAW])
            with sp.Fori(0, FF_STEPS - 1) as i:
                for n, (kind, first, step) in enumerate((("lin", LIN_FFN - 1, 3), ("lin", LIN_FFN, 3),
                                                         ("mod", E_SH, 1), ("lin", LIN_FFN + 1, 3))):
                    load(4 * i + r0 + 3 + n, (r0 + 3 + n) % RAW, (kind, step * i + first))
            r1 = r0 + 3 + 4 * (FF_STEPS - 1)
            for r in range(r1, len(ORDER)):
                load(r, r % RAW, ORDER[r - RAW])
            for half in range(2):
                sp.wait_ge(sem("last_done"), 4 * (half + 1))
                sp.dma_start(out_d[:, 4 * half:4 * half + 4, :], xs[:, 4 * half:4 * half + 4, 0:T]).then_inc(sem("stored"), 16)
            sp.wait_ge(sem("stored"), 32)

        @block.gpsimd
        def _(pool):
            pool.memset(zeros[:, :], 0.0).then_inc(sem("zeros_set"), 1)
            for h in range(NH):
                pool.wait_ge(sem("sb_ln"), h + 1)
                pool.wait_ge(sem("sb_relu"), h + 1)
                nc.gpsimd.tensor_tensor(sb_r, sb_r, sb_t, ALU.add).then_inc(sem("sb_sum"), 1)
                pool.wait_ge(sem("sb_sum"), h + 1)
                nc.gpsimd.tensor_tensor(sb_r, sb_r, past, ALU.mult).then_inc(sem("sb_kept"), 1)
            def product(c):
                pool.wait_ge(sem("gelu_done"), c + 1)
                pool.wait_ge(sem("value_conv"), c + 1)
                nc.gpsimd.tensor_tensor(cv, cv, cg, ALU.mult).then_inc(sem("ffn_mult"), 1)
                pool.wait_ge(sem("g_hi_done"), c + 1)
                nc.gpsimd.tensor_tensor(g_lo[:, :, :], cv, g_hi[:, :, :].bitcast(F32), ALU.subtract).then_inc(sem("g_lo_done"), 1)

            product(0)
            with pool.Fori(0, FF_STEPS - 1) as i:
                product(i + 1)
            pool.wait_ge(sem("ffn_down_evac"), 8)
            pool.memset(u_pad[:, :, :, 0:15], 0.0).then_inc(sem("pads_set"), 1)
            pool.memset(u_pad[:, :, :, 15 + T:UW], 0.0).then_inc(sem("pads_set"), 1)
            n = 0
            for t in (1, 3):
                pool.wait_ge(sem("conv_opened"), 1 if t == 1 else 2)
                for k in range(1, CONV_W):
                    acc, _ = conv_part(t, k, "scalar")
                    pool.wait_ge(sem("prod_ready"), n + 1)
                    if n:
                        pool.wait_ge(sem("prod_used"), n)
                    prod = conv_prod[n % PRODS]
                    prod = prod.rearrange("p (s n) -> p s n", s=2) if t == 1 else prod[:, 0:T]
                    nc.gpsimd.tensor_tensor(acc, acc, prod, ALU.add).then_inc(sem("prod_used"), 1)
                    n += 1
            for g in range(4):
                pool.wait_ge(sem("y_b_raw"), g + 1)
                pool.wait_ge(sem("ein_evac"), 10)
                nc.gpsimd.tensor_tensor(y_b[:, g, :], y_b[:, g, :], sgate[:, 4 + g, :], ALU.mult).then_inc(sem("y_b"), 1)

        @block.scalar
        def _(act):
            me = Steps(act, "act_steps")
            act.dma_start(cond_ada, bass.AP(cond_d.tensor, 0, [[0, P], [1, D]])).then_inc(sem("cond_ada_loaded"), 16)
            act.dma_start(rel[0:32, :], rel_d).then_inc(sem("rel_loaded"), 16)
            act.dma_start(onehot, c1_d[0:33, 1152:1536]).then_inc(sem("rel_loaded"), 16)
            act.dma_start(xs[:, :, 0:T], xs_d[:, :, 0:T]).then_inc(sem("x_loaded"), 16)
            act.dma_start(c0[:, :], c0_d).then_inc(sem("c0_loaded"), 16)
            act.dma_start(vec[:, :], vec_d).then_inc(sem("vec_loaded"), 16)

            def split(j, slot=None, rslot=None, arrived=None):
                if isinstance(j, int):
                    if j >= N_LIN:
                        return
                    r = RAW_OF_LIN[j]
                    slot, rslot, arrived = j % SPL, r % RAW, 16 * (r // RAW + 1)
                act.wait_ge(sem(f"arrived{rslot}"), arrived)
                if not isinstance(j, int) or j >= SPL:
                    act.wait_ge(sem("lin_done"), LIN_OPEN + j - (SPL - 1))
                nc.scalar.copy(w_hi[:, slot, :], raw[:, rslot, :]).then_inc(sem("hi_done"), 1)

            preloads = []

            def preload(func):
                preloads.append(func)
                c = 39 + len(preloads)
                me.mark(nc.scalar.activation(small[:, c:c + 1], eps_col, func))

            def squares(name, ready):
                n, s = NORMS[name][:2]
                preload(ACT.Ln)
                for k in range(KT):
                    for sname, v in ready(k):
                        act.wait_ge(sem(sname), v)
                    nc.scalar.activation(square_tmp(name)[:, k, :], xs[:, k, s * T:(s + 1) * T],
                                         ACT.Square).then_inc(sem("squares"), 1)

            def rstd_of(name):
                n, s = NORMS[name][:2]
                act.wait_ge(sem("sumsq"), n + 1)
                out = rstd[:, s * T:(s + 1) * T]
                me.mark(nc.scalar.activation(out, bank[2 + s][:, s * T:(s + 1) * T], ACT.Ln, bias=EPS_AP, scale=1.0 / D))
                me.wait()
                nc.scalar.activation(out, out, ACT.Exp, scale=-0.5).then_inc(sem("rstd_ready"), 1)

            def shift_hi(name):
                n, s, _, (sh, v), before = NORMS[name]
                for k in range(KT):
                    act.wait_ge(sem("normed"), before + k + 1)
                    nc.scalar.activation(h_hi[:, k, s * T:(s + 1) * T], norm_tmp[:, k, :], ACT.Identity,
                                         bias=shift_col(sh, k, v), scale=1.0).then_inc(sem("norm_hi"), 1)

            eps_col = small[:, 63:64]
            eps2_col = small[:, 59:60]
            EPS_AP = eps_col
            act.wait_ge(sem("cond_ada_loaded"), 16)
            nc.scalar.activation(cond_ada, cond_ada, ACT.Silu).then_inc(sem("cond_ada_ready"), 1)
            split(0)
            act.wait_ge(sem("bias_row"), 1)
            nc.scalar.copy(urow, bank[3][0:8, 0:384]).then_inc(sem("bias_row_out"), 1)
            act.wait_ge(sem("bias_row_out"), 1)
            act.dma_start(diff_d, urow).then_inc(sem("bias_stored"), 16)
            act.wait_ge(sem("bias_stored"), 16)

            def load_trev(h):
                act.dma_start(trev[:, h % TREV, :], bass.AP(diff_d.tensor, 384 * h, [[1, P], [1, T]])
                              ).then_inc(sem(f"trev_loaded{h % TREV}"), 16)

            for h in range(TREV):
                load_trev(h)
            act.wait_ge(sem("eps_set"), 2)
            squares("mix", lambda k: [("x_loaded", 16)] if k == 0 else [])
            rstd_of("mix")
            shift_hi("mix")
            act.dma_start(consts[:, 0:1152], c1_d[:, 0:1152]).then_inc(sem("c1_loaded"), 16)
            split(1)
            with act.Fori(0, 2) as i:
                for n in range(6):
                    j = 6 * i + n
                    r_ahead = MOD_FIRST + 4 * ((n + 2) // 3) + (n + 2) % 3
                    split(j + 2, (n + 2) % SPL, r_ahead % RAW, 32 * i + 16 * (r_ahead // RAW + 1))
                    act.wait_ge(sem("lin_done"), LIN_OPEN + j + 1)
                    nc.scalar.copy(proj[:, bass.ds(j, 1), :].rearrange("p a n -> p (a n)"),
                                   bank[n % 2][:, :]).then_inc(sem("proj_evac"), 1)
            act.dma_start(cond.rearrange("p v n -> p (v n)"),
                          bass.AP(cond_d.tensor, D, [[0, P], [1, 2 * D]])).then_inc(sem("cond_loaded"), 16)
            act.dma_start(xs[:, :, T:2 * T], xs_d[:, :, T:2 * T]).then_inc(sem("ctx_loaded"), 16)
            for h in range(NH + 1):
                j = LIN_GATE + h
                if h == 3:
                    act.wait_ge(sem("cond_loaded"), 16)
                    nc.scalar.activation(cond[:, :, :], cond[:, :, :], ACT.Silu).then_inc(sem("cond_ready"), 1)
                if h < NH:
                    act.wait_ge(sem("qk_done"), h + 1)
                    if h + TREV < NH:
                        load_trev(h + TREV)
                    if h:
                        act.wait_ge(sem("sb_sum"), h)
                    me.mark(nc.scalar.activation(sb_t, wide[:, 2, 0:384], ACT.Abs))
                    abs_done = me.value()
                if h:
                    act.wait_ge(sem("pt_done"), h)
                    if h >= 3:
                        act.wait_ge(sem("pv_done"), h - 2)
                    nc.scalar.copy(pt[(h - 1) % 2], wide[:, 1, 0:384]).then_inc(sem("pt_ready"), 1)
                if h >= 3 and h % 2:
                    pair_hi = (h - 3) // 2
                    act.wait_ge(sem("pv_done"), h - 1)
                    nc.scalar.copy(h_hi[:, pair_hi::4, T:2 * T],
                                   wide[:, 3, :].rearrange("p (a n) -> p a n", a=2)).then_inc(sem("att_hi"), 1)
                if h < NH:
                    act.wait_ge(sem("neg_max"), h + 1)
                    for qt, (a, b) in enumerate(((0, 128), (128, 384))):
                        nc.scalar.activation(prob[:, a:b], wide[:, 0, a:b], ACT.Exp, bias=small[:, 2 + qt:3 + qt], scale=QK,
                                             accum_out=small[:, 4 + qt:5 + qt]).then_inc(sem("exp_done"), 1)
                    act.wait_ge(me.sem, abs_done)
                    me.mark(nc.scalar.activation(sb_t, sb_t, ACT.Exp, scale=-QK))
                if h:
                    act.wait_ge(sem("sb_min"), h)
                    if h >= 2:
                        act.wait_ge(sem("pv_done"), h - 1)
                    nc.scalar.activation(aw, sb_e, ACT.Exp, scale=QK).then_inc(sem("aw_ready"), 1)
                if h < NH:
                    me.wait()
                    nc.scalar.activation(sb_t, sb_t, ACT.Ln, bias=1.0).then_inc(sem("sb_ln"), 1)
                    if h:
                        act.wait_ge(sem("e_done"), h)
                    nc.scalar.activation(sb_r, wide[:, 2, 0:384], ACT.Relu, scale=QK).then_inc(sem("sb_relu"), 1)
                    split(j + 2)
                if h < NH:
                    act.wait_ge(sem("lin_done"), LIN_OPEN + j + 1)
                    nc.scalar.copy(gate[:, 512 * h:512 * (h + 1)], bank[j % 2][:, :]).then_inc(sem("gate_evac"), 1)
            act.wait_ge(sem("pv_done"), NH)
            nc.scalar.copy(h_hi[:, 3::4, T:2 * T], wide[:, 3, :].rearrange("p (a n) -> p a n", a=2)).then_inc(sem("att_hi"), 1)
            act.wait_ge(sem("gate_evac"), NH)
            nc.scalar.activation(gate, gate, ACT.Sigmoid).then_inc(sem("gates_ready"), 1)
            act.wait_ge(sem("e_done"), NH)
            act.wait_ge(sem("qk_done"), NH)
            act.wait_ge(sem("sb_kept"), NH)
            act.wait_ge(sem("sb_min"), NH)
            act.dma_start(consts[:, 0:1024], c2_d[:, 0:1024]).then_inc(sem("c2_loaded"), 16)
            act.dma_start(dft_d, c2_d[:, 1024:1280]).then_inc(sem("c2_loaded"), 16)
            act.dma_start(fw, fw_d).then_inc(sem("c2_loaded"), 16)
            for i in range(4):
                split(LIN_BR + i + 2)
                if i == 0:
                    squares("even_ctx", lambda k: [("ctx_loaded", 16)] if k == 0 else [])
                if i == 2:
                    rstd_of("even_ctx")
                if i % 2:
                    n = i // 2
                    act.wait_ge(sem("mixed"), n + 1)
                    nc.scalar.copy(h_hi[:, 4 * n:4 * n + 4, 0:T],
                                   mix[:, 1024 * n:1024 * (n + 1)].rearrange("p (k n) -> p k n", n=T)).then_inc(sem("mixed_hi"), 1)
            for i in range(4):
                split(LIN_OUT + i + 2)
            squares("ffn", lambda k: [("out_evac", k + 1)])
            rstd_of("ffn")
            shift_hi("ffn")

            def conv_first(which, dst, c):
                for t in range(2):
                    tile = 2 * c + t + (22 if which else 0)
                    nc.scalar.activation(dst[:, t, :], bank[which][:, t * T:(t + 1) * T], ACT.Identity,
                                         bias=col("b_conv", tile), scale=col("w_conv", 88 + tile)).then_inc(sem("tap2"), 1)

            split(LIN_FFN + 2)
            act.wait_ge(sem("lin_done"), LIN_OPEN + LIN_FFN + 1)
            conv_first(0, cv, 0)
            split(LIN_FFN + 3)
            act.wait_ge(sem("lin_done"), LIN_OPEN + LIN_FFN + 2)
            conv_first(1, cg, 0)
            act.wait_ge(sem("gate_conv"), 1)
            nc.scalar.activation(cg, cg, ACT.Gelu_apprx_tanh).then_inc(sem("gelu_done"), 1)
            act.wait_ge(sem("ffn_mult"), 1)
            nc.scalar.copy(g_hi[:, :, :], cv).then_inc(sem("g_hi_done"), 1)
            j0, r0 = LIN_FFN + 2, RAW_OF_LIN[LIN_FFN + 2]
            with act.Fori(0, FF_STEPS - 1) as i:
                j = 3 * i + j0
                split(j + 2, (j0 + 2) % SPL, (r0 + 3) % RAW, 16 * i + 16 * ((r0 + 3) // RAW + 1))
                act.wait_ge(sem("lin_done"), LIN_OPEN + j + 1)
                act.wait_ge(sem("g_lo_done"), i + 1)
                conv_first(0, cv, i + 1)
                split(j + 3, (j0 + 3) % SPL, (r0 + 4) % RAW, 16 * i + 16 * ((r0 + 4) // RAW + 1))
                act.wait_ge(sem("lin_done"), LIN_OPEN + j + 2)
                conv_first(1, cg, i + 1)
                split(j + 4, (j0 + 4) % SPL, (r0 + 5) % RAW, 16 * i + 16 * ((r0 + 5) // RAW + 1))
                act.wait_ge(sem("gate_conv"), i + 2)
                nc.scalar.activation(cg, cg, ACT.Gelu_apprx_tanh).then_inc(sem("gelu_done"), 1)
                act.wait_ge(sem("ffn_mult"), i + 2)
                act.wait_ge(sem("lin_done"), LIN_OPEN + j + 3)
                nc.scalar.copy(g_hi[:, :, :], cv).then_inc(sem("g_hi_done"), 1)
            split(LIN_EIN + 1)
            preload(ACT.Ln)
            for k in range(KT):
                act.wait_ge(sem("ffn_down_evac"), k + 1)
                nc.scalar.activation(norm_tmp[:, k, :], xs[:, k, 0:T], ACT.Square).then_inc(sem("squares"), 1)
                nc.scalar.activation(gain_sq[:, k, :], xs[:, k, 0:T], ACT.Square,
                                     scale=col("g_final", k)).then_inc(sem("squares"), 1)
            act.wait_ge(sem("sumsq"), 4)
            nc.scalar.activation(rstd[:, 0:T], bank[2][:, 0:T], ACT.Ln, bias=EPS_AP,
                                 scale=1.0 / D).then_inc(sem("sumsq_read"), 1)
            act.wait_ge(sem("both_sums"), 1)
            me.mark(nc.scalar.activation(rstd2, rstd2, ACT.Ln, bias=eps2_col, scale=1.0 / D))
            me.wait()
            me.mark(nc.scalar.activation(rstd2, rstd2, ACT.Exp, scale=-0.5))
            nc.scalar.activation(rstd[:, 0:T], rstd[:, 0:T], ACT.Exp, scale=-0.5).then_inc(sem("rstd_ready"), 1)
            shift_hi("even_x")
            shift_hi("even_ctx")

            act.wait_ge(sem("fold_done"), 1)
            nc.scalar.copy(fold[:, :, 0, :], bank[0][:, :].rearrange("p (g n) -> p g n", g=4)).then_inc(sem("fold_ready"), 1)
            nc.scalar.copy(fold[:, :, 1, :], bank[1][:, :].rearrange("p (g n) -> p g n", g=4)).then_inc(sem("fold_ready"), 1)

            def chunk_banks(i):
                b = 2 * (i % 2)
                return wide[:, b:b + 2, :]

            def fourier_evac(g):
                for s in range(2):
                    act.wait_ge(sem("four_a"), 2 * g + s + 1)
                    if g:
                        act.wait_ge(sem("four_b"), g)
                    nc.scalar.copy(four[s], bank[2 * s][:, :]).then_inc(sem("four_ready"), 1)

            def fourier_out(g):
                act.wait_ge(sem("four_b"), g + 1)
                nc.scalar.copy(y_b[:, g, :], bank[1][:, :]).then_inc(sem("y_b_raw"), 1)

            n_prod = 0
            for i in range(10):
                split(LIN_EIN + i + 2)
                for t, k0, k1 in CONV_SCALAR.get(i, ()):
                    act.wait_ge(sem("glu_done"), 1 if t == 1 else 2)
                    act.wait_ge(sem("pads_set"), 2)
                    for k in range(k0, k1):
                        acc, src = conv_part(t, k, "scalar")
                        if k == 0:
                            nc.scalar.activation(acc, src, ACT.Identity, bias=col("a_conv_b", t),
                                                 scale=col("a_conv_w", t)).then_inc(sem("conv_opened"), 1)
                            continue
                        if n_prod >= PRODS:
                            act.wait_ge(sem("prod_used"), n_prod - PRODS + 1)
                        prod = conv_prod[n_prod % PRODS]
                        prod = prod.rearrange("p (s n) -> p s n", s=2) if t == 1 else prod[:, 0:T]
                        nc.scalar.activation(prod, src, ACT.Copy,
                                             scale=col("a_conv_w", 4 * k + t)).then_inc(sem("prod_ready"), 1)
                        n_prod += 1
                act.wait_ge(sem("lin_done"), LIN_OPEN + LIN_EIN + i + 1)
                src = chunk_banks(i)
                if i < 4 and i % 2 == 0:
                    ins = nc.scalar.copy(u_pad[:, i:i + 2, :, 15:15 + T], src.rearrange("p t (s n) -> p t s n", s=2))
                elif i < 4:
                    if i == 3:
                        act.wait_ge(sem("glu_done"), 1)
                    ins = nc.scalar.activation(glu, src, ACT.Sigmoid)
                elif i < 6:
                    ins = nc.scalar.copy(b_val[:, 2 * (i - 4):2 * (i - 4) + 2, :], src)
                else:
                    t = 2 * (i - 6)
                    ins = nc.scalar.activation(sgate[:, t:t + 2, :], src, ACT.Silu)
                ins.then_inc(sem("ein_evac"), 1)
                if i >= 7:
                    fourier_out(i - 7)
                if i >= 6:
                    fourier_evac(i - 6)
            fourier_out(3)
            preload(ACT.Ln)
            for t in range(4):
                act.wait_ge(sem("centered"), t + 1)
                nc.scalar.activation(ln_tmp[:, t, :], conv[:, t, :], ACT.Square).then_inc(sem("ln_squares"), 1)
            act.wait_ge(sem("ln_sumsq"), 1)
            me.mark(nc.scalar.activation(rstd[:, :], bank[3][:, :], ACT.Ln, bias=EPS_AP, scale=1.0 / 512))
            me.wait()
            nc.scalar.activation(rstd[:, :], rstd[:, :], ACT.Exp, scale=-0.5).then_inc(sem("ln_rstd"), 1)
            preload(ACT.Silu)
            silu_at = []
            for t in range(5):
                if t < 4:
                    act.wait_ge(sem("ln_scaled"), t + 1)
                    me.mark(nc.scalar.activation(conv[:, t, :], conv[:, t, :], ACT.Silu, bias=col("ln_b", t),
                                                 scale=col("ln_g", t)))
                    silu_at.append(me.value())
                if t:
                    act.wait_ge(me.sem, silu_at[t - 1])
                    nc.scalar.copy(h_hi[:, t - 1, :], conv[:, t - 1, :]).then_inc(sem("u_hi"), 1)
            split(LIN_PW + 2)
            for t in range(4):
                act.wait_ge(sem("y_a"), t + 1)
                nc.scalar.copy(h_hi[:, 4 + t, :], ln_tmp[:, t, :]).then_inc(sem("y_hi"), 1)
            act.wait_ge(sem("lin_done"), LIN_OPEN + LIN_PW + 1)
            for t in range(4):
                act.wait_ge(sem("y_b"), t + 1)
                nc.scalar.copy(h_hi[:, t, :], y_b[:, t, :]).then_inc(sem("y_hi"), 1)
            act.wait_ge(sem("u_lo"), 4)
            act.dma_start(c3, c3_d).then_inc(sem("c3_loaded"), 16)
            for i in range(4):
                split(LIN_EOUT + i + 2)
            squares("odd_x", lambda k: [("eout_evac", 2 * k + 2)])
            squares("odd_ctx", lambda k: [])
            rstd_of("odd_x")
            rstd_of("odd_ctx")
            shift_hi("odd_x")
            shift_hi("odd_ctx")
            for i in range(3):
                j = LIN_OIN + i
                split(j + 2)
                act.wait_ge(sem("lin_done"), LIN_OPEN + j + 1)
                if i < 2:
                    nc.scalar.copy(q_raw[:, 512 * i:512 * (i + 1)], wide[:, i, :]).then_inc(sem("q_raw"), 1)
                else:
                    nc.scalar.copy(k_raw, wide[:, 2, 0:T]).then_inc(sem("q_raw"), 1)
                    nc.scalar.copy(k_all[:, T:2 * T], wide[:, 2, T:2 * T]).then_inc(sem("kv_evac"), 1)
                    nc.scalar.copy(v_tok, wide[:, 3, :].rearrange("p (t n) -> p t n", n=P)).then_inc(sem("kv_evac"), 1)

            def window_pt(u):
                act.wait_ge(sem("wt_done"), u + 1)
                if u >= 2:
                    act.wait_ge(sem("wpv_done"), u - 1)
                nc.scalar.copy(w_pt[u % 2], bank[2 + u % 2][:, :]).then_inc(sem("wpt_ready"), 1)

            for u in range(18):
                c = OIN_CHUNK.get(u)
                if c is not None:
                    split(LIN_OIN + 3 + c + 2)
                if u < 16:
                    act.wait_ge(sem("wneg_max"), u + 1)
                    if u >= 2:
                        act.wait_ge(sem("wt_done"), u - 1)
                    nb = small[:, 16 + u:17 + u]
                    nc.scalar.activation(w_prob[u % 2], bank[u % 2][:, :], ACT.Exp, bias=nb, scale=QK,
                                         accum_out=small[:, 32 + 2 * (u % 2):33 + 2 * (u % 2)]).then_inc(sem("wexp"), 1)
                    t, b = (u // 2) % 4, u // 8
                    nc.scalar.activation(small[:, 33 + 2 * (u % 2):34 + 2 * (u % 2)], nb, ACT.Exp, scale=1.0,
                                         bias=col("sink", t + 4 * b)).then_inc(sem("wexp"), 1)
                if c is not None:
                    act.wait_ge(sem("lin_done"), LIN_OPEN + LIN_OIN + 3 + c + 1)
                    src = wide[:, c % 2, :].rearrange("p (t n) -> p t n", n=T)
                    if c < 4 and c % 2 == 0:
                        nc.scalar.copy(ccx[:, c:c + 2, 1:1 + T], src).then_inc(sem("oin_evac"), 1)
                    elif c in (4, 5):
                        nc.scalar.copy(cb[:, 2 * c - 8:2 * c - 6, :], src).then_inc(sem("oin_evac"), 1)
                    elif c >= 6:
                        nc.scalar.copy(cg_ag[:, 2 * (c - 6):2 * (c - 6) + 2, :], src).then_inc(sem("oin_evac"), 1)
                if 1 <= u < 17:
                    window_pt(u - 1)
            act.wait_ge(sem("oin_evac"), 8)
            for half in range(2):
                g = cg_ag[:, 4 * half:4 * half + 4, :]
                nc.scalar.activation(g, g, ACT.Silu).then_inc(sem("silu_gates"), 1)
            act.wait_ge(sem("y_c"), 1)
            nc.scalar.copy(h_hi[:, 0:4, 0:T], y_c).then_inc(sem("yo_hi"), 1)
            act.wait_ge(sem("y_d"), 1)
            nc.scalar.copy(h_hi[:, 4:8, 0:T], rot_tmp.rearrange("p (t n) -> p t n", n=T)).then_inc(sem("yo_hi"), 1)
            for i in range(4):
                split(LIN_OOUT + i + 2)
            squares("last", lambda k: [("oout_evac", k + 1)])
            rstd_of("last")

        @block.vector
        def _(dve):
            me = Steps(dve, "dve_steps")

            def mod(m, rslot, arrived, j, slot, both=None):
                if both is None:
                    both = E_SC <= m < O_GT
                    vecs = ((0, cond_ada),) if m < E_SC else ((0, cond[:, 0, :]), (1, cond[:, 1, :]))[:1 + both]
                else:
                    vecs = ((0, cond[:, 0, :]), (1, cond[:, 1, :])) if both else ((0, cond_ada),)
                dve.wait_ge(sem(f"arrived{rslot}"), arrived)
                if not isinstance(j, int) or j >= SPL:
                    dve.wait_ge(sem("lin_done"), LIN_OPEN + j - (SPL - 1))
                if not isinstance(m, int) or m:
                    dve.wait_ge(sem("mod_done"), m)
                for v, c in vecs:
                    if v:
                        me.mark(last)
                        me.wait()
                    for t in range(2):
                        last = nc.vector.scalar_tensor_tensor(
                            w_lo[:, slot, D * t:D * (t + 1)], raw[:, rslot, D * t:D * (t + 1)], 1.0, c, ALU.mult, ALU.mult,
                            accum_out=modv[:, bass.ds(4 * m + 2 * t + v, 1)])
                last.then_inc(sem("mod_done"), 1)

            def mods_before(j):
                r, mods = RAW_OF_LIN[j] - 1, []
                while r > MOD_FIRST and ORDER[r][0] == "mod":
                    mods.insert(0, ORDER[r][1])
                    r -= 1
                return mods

            def mod_static(m, j):
                r = RAW_OF_MOD[m]
                mod(m, r % RAW, 16 * (r // RAW + 1), j, j % SPL)

            def split(j, slot=None, rslot=None, mod_before=None, done=0):
                if isinstance(j, int):
                    if j >= N_LIN:
                        return
                    slot, rslot = j % SPL, RAW_OF_LIN[j] % RAW
                if isinstance(j, int):
                    for mod_before in mods_before(j)[done:]:
                        mod_static(mod_before, j)
                    mod_before = (mods_before(j) or [None])[-1]
                if mod_before is not None:
                    dve.wait_ge(sem("mod_done"), mod_before + 1)
                dve.wait_ge(sem("hi_done"), j + 1)
                nc.vector.tensor_tensor(w_lo[:, slot, :], raw[:, rslot, :], w_hi[:, slot, :].bitcast(F32),
                                        ALU.subtract).then_inc(sem("lo_done"), 1)

            def coefficients(at, gain, scale_cols):
                nc.vector.scalar_tensor_tensor(coef[:, at:at + 8], scale_cols, 1.0, vec[:, VEC[gain]:VEC[gain] + 8],
                                               ALU.add, ALU.mult).then_inc(sem("coef_ready"), 1)

            batches = []

            def mod_bias(m0, m1):
                one = m0 < E_SC or m0 >= O_GT
                dve.wait_ge(sem("mod_done"), m1)
                a, b = 4 * m0, 4 * m1
                dst, bias = modv[:, a:b], vec[:, VEC["mod_bias"] + a:VEC["mod_bias"] + b]
                if one:
                    dst, bias = (z.rearrange("p (c v) -> p c v", v=2)[:, :, 0] for z in (dst, bias))
                nc.vector.tensor_tensor(dst, dst, bias, ALU.add).then_inc(sem("mod_biased"), 1)
                batches.append(m1)
                dve.wait_ge(sem("mod_biased"), len(batches))

            def norm(name, coefs_before, rstd_of=None):
                n, s, at, (sh, v), before = NORMS[name]
                if rstd_of is None:
                    rstd_of = rstd[:, s * T:(s + 1) * T]
                dve.wait_ge(sem("rstd_ready"), n + 1)
                dve.wait_ge(sem("coef_ready"), coefs_before)
                for k in range(KT + 2):
                    if k < KT:
                        nc.vector.scalar_tensor_tensor(norm_tmp[:, k, :], xs[:, k, s * T:(s + 1) * T],
                                                       coef[:, at + k:at + k + 1], rstd_of,
                                                       ALU.mult, ALU.mult).then_inc(sem("normed"), 1)
                    if k >= 2:
                        dve.wait_ge(sem("norm_hi"), before + k - 1)
                        nc.vector.scalar_tensor_tensor(h_lo[:, k - 2, s * T:(s + 1) * T], norm_tmp[:, k - 2, :],
                                                       shift_col(sh, k - 2, v),
                                                       h_hi[:, k - 2, s * T:(s + 1) * T].bitcast(F32),
                                                       ALU.add, ALU.subtract).then_inc(sem("norm_lo"), 1)

            nc.vector.memset(rel[32:33, :], 1.0).then_inc(sem("rel_one"), 1)
            nc.vector.memset(small[:, 59:60], EPS * EPS).then_inc(sem("eps_set"), 1)
            nc.vector.memset(small[:, 63:64], EPS).then_inc(sem("eps_set"), 1)
            split(0)
            dve.wait_ge(sem("cond_ada_ready"), 1)
            for m in range(MOD_FIRST):
                mod(m, RAW_OF_MOD[m] % RAW, 16 * (RAW_OF_MOD[m] // RAW + 1), 1, 1)
            dve.wait_ge(sem("vec_loaded"), 16)
            mod_bias(0, 8)
            coefficients(0, "g_mix", mod_row(ADA_SC_M, 0))
            norm("mix", 1)
            split(1)
            with dve.Fori(0, 2) as i:
                for n in range(6):
                    j = 6 * i + n + 2
                    r = MOD_FIRST + 4 * ((n + 2) // 3) + (n + 2) % 3
                    m = None
                    if (n + 2) % 3 == 0:
                        m = 2 * i + MOD_FIRST + (n + 2) // 3 - 1
                        mod(m, (r - 1) % RAW, 32 * i + 16 * ((r - 1) // RAW + 1), j, (n + 2) % SPL, False)
                    split(j, (n + 2) % SPL, r % RAW, m)
            for h in range(NH + 1):
                j = LIN_GATE + h
                if h == 4:
                    dve.wait_ge(sem("cond_ready"), 1)
                if h < NH:
                    dve.wait_ge(sem("qk_done"), h + 1)
                    me.mark(nc.vector.reduce_max(small[:, 0:1], wide[:, 0, 0:128], AX_X, negate=True))
                    me.mark(nc.vector.reduce_max(small[:, 1:2], wide[:, 0, 128:384], AX_X, negate=True))
                    me.wait()
                    nc.vector.tensor_scalar(small[:, 2:4], small[:, 0:2], QK, None, ALU.mult).then_inc(sem("neg_max"), 1)
                if h:
                    dve.wait_ge(sem("e_done"), h)
                    if h >= 2:
                        dve.wait_ge(sem("aw_ready"), h - 1)
                    nc.vector.tensor_tensor(sb_e, bank[2][:, 0:384], bound, ALU.min).then_inc(sem("sb_min"), 1)
                if h >= 3 and h % 2:
                    pair = (h - 3) // 2
                    dve.wait_ge(sem("att_hi"), pair + 1)
                    nc.vector.tensor_tensor(h_lo[:, pair::4, T:2 * T], wide[:, 3, :].rearrange("p (a n) -> p a n", a=2),
                                            h_hi[:, pair::4, T:2 * T].bitcast(F32), ALU.subtract).then_inc(sem("att_lo"), 1)
                if h == NH:
                    break
                mods = mods_before(j + 2)
                for m in mods[:1]:
                    mod_static(m, j + 2)
                dve.wait_ge(sem("exp_done"), 2 * h + 2)
                me.mark(nc.vector.reciprocal(small[:, 6:8], small[:, 4:6]))
                me.wait()
                me.mark(nc.vector.tensor_scalar(prob[:, 0:128], prob[:, 0:128], small[:, 6:7], None, ALU.mult))
                nc.vector.tensor_scalar(prob[:, 128:384], prob[:, 128:384], small[:, 7:8], None,
                                        ALU.mult).then_inc(sem("prob_ready"), 1)
                split(j + 2, done=1)
            dve.wait_ge(sem("att_hi"), 4)
            nc.vector.tensor_tensor(h_lo[:, 3::4, T:2 * T], wide[:, 3, :].rearrange("p (a n) -> p a n", a=2),
                                    h_hi[:, 3::4, T:2 * T].bitcast(F32), ALU.subtract).then_inc(sem("att_lo"), 1)
            mod_bias(8, 20)
            coefficients(8, "g_ffn", mod_row(ADA_SC_F, 0))
            for i in range(4):
                split(LIN_BR + i + 2)
                n, two = i // 2, i % 2
                dve.wait_ge(sem("lin_done"), LIN_OPEN + LIN_BR + i + 1)
                if i == 0:
                    dve.wait_ge(sem("gates_ready"), 1)
                src = wide[:, 2 * two:2 * two + 2, :].rearrange("p b n -> p (b n)")
                g = gate[:, 2048 * two + 1024 * n:2048 * two + 1024 * (n + 1)]
                m = mix[:, 1024 * n:1024 * (n + 1)]
                if not two:
                    nc.vector.tensor_tensor(m, src, g, ALU.mult).then_inc(sem("br_evac"), 1)
                else:
                    if n:
                        dve.wait_ge(sem("mixed"), n)
                    nc.vector.tensor_tensor(mix2, src, g, ALU.mult).then_inc(sem("br_evac"), 1)
                    dve.wait_ge(sem("br_evac"), i + 1)
                    nc.vector.tensor_tensor(m, m, mix2, ALU.add).then_inc(sem("mixed"), 1)
                    dve.wait_ge(sem("mixed_hi"), n + 1)
                    nc.vector.tensor_tensor(h_lo[:, 4 * n:4 * n + 4, 0:T], m.rearrange("p (k n) -> p k n", n=T),
                                            h_hi[:, 4 * n:4 * n + 4, 0:T].bitcast(F32),
                                            ALU.subtract).then_inc(sem("mixed_lo"), 1)
            for i in range(4):
                split(LIN_OUT + i + 2)
                dve.wait_ge(sem("lin_done"), LIN_OPEN + LIN_OUT + i + 1)
                for t in range(2):
                    k = 2 * i + t
                    nc.vector.scalar_tensor_tensor(xs[:, k, 0:T], bank[i % 2][:, t * T:(t + 1) * T], shift_col(ADA_GT_M, k),
                                                   xs[:, k, 0:T], ALU.mult, ALU.add).then_inc(sem("out_evac"), 1)
            norm("ffn", 2)

            def conv_taps(which, dst, c):
                dve.wait_ge(sem("tap2"), 4 * c + 2 * which + 2)
                for t in range(2):
                    tile = 2 * c + t + (22 if which else 0)
                    me.mark(nc.vector.scalar_tensor_tensor(dst[:, t, 1:T], bank[which][:, t * T:(t + 1) * T - 1],
                                                           col("w_conv", 44 + tile), dst[:, t, 1:T], ALU.mult, ALU.add))
                me.wait()
                for t in range(2):
                    tile = 2 * c + t + (22 if which else 0)
                    ins = nc.vector.scalar_tensor_tensor(dst[:, t, 2:T], bank[which][:, t * T:(t + 1) * T - 2],
                                                         col("w_conv", tile), dst[:, t, 2:T], ALU.mult, ALU.add)
                    if t == 0:
                        me.mark(ins)
                ins.then_inc(sem("gate_conv" if which else "value_conv"), 1)

            split(LIN_FFN + 2)
            conv_taps(0, cv, 0)
            split(LIN_FFN + 3)
            conv_taps(1, cg, 0)
            j0, r0 = LIN_FFN + 2, RAW_OF_LIN[LIN_FFN + 2]
            with dve.Fori(0, FF_STEPS - 1) as i:
                me.enter(i, 7)
                j = 3 * i + j0
                mod(i + E_SH + 1, (r0 + 2) % RAW, 16 * i + 16 * ((r0 + 2) // RAW + 1), j + 2, (j0 + 2) % SPL, True)
                split(j + 2, (j0 + 2) % SPL, (r0 + 3) % RAW, i + E_SH + 1)
                conv_taps(0, cv, i + 1)
                split(j + 3, (j0 + 3) % SPL, (r0 + 4) % RAW)
                conv_taps(1, cg, i + 1)
                split(j + 4, (j0 + 4) % SPL, (r0 + 5) % RAW)
            me.leave(FF_STEPS - 1)
            mod_bias(20, 24)
            mod_bias(24, 36)
            coefficients(16, "e_norm", mod_row(E_SC, 0))
            coefficients(24, "e_norm", mod_row(E_SC, 1))
            split(LIN_EIN + 1)
            dve.wait_ge(sem("coef_ready"), 3)
            nc.vector.tensor_tensor(coef[:, 16:24], coef[:, 16:24], vec[:, VEC["g_final"]:VEC["g_final"] + 8],
                                    ALU.mult).then_inc(sem("coef_ready"), 1)
            for k in range(KT):
                if k % 2 == 0:
                    if k < 6:
                        dve.wait_ge(sem("down_bank"), k // 2 + 1)
                    else:
                        dve.wait_ge(sem("lin_done"), LIN_OPEN + LIN_EIN)
                nc.vector.scalar_tensor_tensor(xs[:, k, 0:T], wide[:, k // 2, (k % 2) * T:(k % 2 + 1) * T],
                                               shift_col(ADA_GT_F, k), xs[:, k, 0:T], ALU.mult,
                                               ALU.add).then_inc(sem("ffn_down_evac"), 1)
            dve.wait_ge(sem("sumsq"), 4)
            me.mark(nc.vector.tensor_copy(rstd2, bank[3][:, 0:T]))
            me.wait()
            dve.wait_ge(sem("sumsq_read"), 1)
            nc.vector.scalar_tensor_tensor(rstd2, bank[2][:, 0:T], EPS, rstd2, ALU.mult, ALU.add).then_inc(sem("both_sums"), 1)
            norm("even_x", 5, rstd_of=rstd2)
            norm("even_ctx", 5)
            taps = 0
            for i in range(10):
                split(LIN_EIN + i + 2)
                if i == 0:
                    for k in range(KT):
                        nc.vector.scalar_tensor_tensor(xs[:, k, 0:T], xs[:, k, 0:T], col("g_final", k), rstd[:, 0:T],
                                                       ALU.mult, ALU.mult).then_inc(sem("final_scaled"), 1)
                if i in (2, 4):
                    dve.wait_ge(sem("ein_evac"), i)
                    dst = u_pad[:, i - 2:i, :, 15:15 + T]
                    nc.vector.tensor_tensor(dst, dst, glu.rearrange("p t (s n) -> p t s n", s=2),
                                            ALU.mult).then_inc(sem("glu_done"), 1)
                for t, k0, k1 in CONV_VECTOR.get(i, ()):
                    dve.wait_ge(sem("glu_done"), 1 if t == 0 else 2)
                    dve.wait_ge(sem("pads_set"), 2)
                    for k in range(k0, k1):
                        acc, src = conv_part(t, k, "vector")
                        if k == 0:
                            ins = nc.vector.tensor_scalar(acc, src, col("a_conv_w", t), col("a_conv_b", t), ALU.mult, ALU.add)
                        else:
                            dve.wait_ge(sem("conv_tap"), taps)
                            ins = nc.vector.scalar_tensor_tensor(acc, src, col("a_conv_w", 4 * k + t), acc, ALU.mult, ALU.add)
                        ins.then_inc(sem("conv_tap"), 1)
                        taps += 1
            dve.wait_ge(sem("ln_sum"), 1)
            for t in range(4):
                nc.vector.scalar_tensor_tensor(conv[:, t, :], bank[2][:, :], -1.0 / 512, conv[:, t, :],
                                               ALU.mult, ALU.add).then_inc(sem("centered"), 1)
            dve.wait_ge(sem("ln_rstd"), 1)
            for t in range(6):
                if t < 4:
                    nc.vector.tensor_tensor(conv[:, t, :], conv[:, t, :], rstd[:, :], ALU.mult).then_inc(sem("ln_scaled"), 1)
                if t >= 2:
                    dve.wait_ge(sem("u_hi"), t - 1)
                    nc.vector.tensor_tensor(h_lo[:, t - 2, :], conv[:, t - 2, :], h_hi[:, t - 2, :].bitcast(F32),
                                            ALU.subtract).then_inc(sem("u_lo"), 1)
            for t in range(4):
                if t < 3:
                    dve.wait_ge(sem("pw_tile"), t + 1)
                else:
                    dve.wait_ge(sem("lin_done"), LIN_OPEN + LIN_PW + 1)
                nc.vector.scalar_tensor_tensor(ln_tmp[:, t, :], wide[:, t, :], col("pw_b", t), sgate[:, t, :],
                                               ALU.add, ALU.mult).then_inc(sem("y_a"), 1)
                dve.wait_ge(sem("y_hi"), t + 1)
                nc.vector.tensor_tensor(h_lo[:, 4 + t, :], ln_tmp[:, t, :], h_hi[:, 4 + t, :].bitcast(F32),
                                        ALU.subtract).then_inc(sem("y_lo"), 1)
            for t in range(4):
                dve.wait_ge(sem("y_hi"), 5 + t)
                nc.vector.tensor_tensor(h_lo[:, t, :], y_b[:, t, :], h_hi[:, t, :].bitcast(F32),
                                        ALU.subtract).then_inc(sem("y_lo"), 1)
            split(LIN_PW + 2)
            for i in range(4):
                split(LIN_EOUT + i + 2)
                dve.wait_ge(sem("lin_done"), LIN_OPEN + LIN_EOUT + i + 1)
                for t in range(2):
                    for s in range(2):
                        k = 2 * i + t
                        c = slice(s * T, (s + 1) * T)
                        if i == 0 and t == 0 and s == 0:
                            dve.wait_ge(sem("final_scaled"), KT)
                        nc.vector.scalar_tensor_tensor(xs[:, k, c], wide[:, 2 * (i % 2) + t, c], shift_col(E_GT, k, s),
                                                       xs[:, k, c], ALU.mult, ALU.add).then_inc(sem("eout_evac"), 1)
            mod_bias(36, 44)
            coefficients(32, "o_norm", mod_row(O_SC, 0))
            coefficients(40, "o_norm", mod_row(O_SC, 1))
            norm("odd_x", 7)
            norm("odd_ctx", 7)
            for i in range(3):
                split(LIN_OIN + i + 2)
            neg_sink = small[:, 8:16]
            me.mark(nc.vector.tensor_scalar(neg_sink, vec[:, VEC["sink"]:VEC["sink"] + 8], -1.0, None, ALU.mult))
            me.mark(nc.vector.memset(ccx[:, :, 0:1], 0.0))
            me.mark(nc.vector.memset(ccx[:, :, T + 1:T + 2], 0.0))
            dve.wait_ge(sem("q_raw"), 3)
            dve.wait_ge(sem("rot_done"), 1)
            for half in range(2):
                for n in range(2):
                    a = slice(512 * half + T * n, 512 * half + T * (n + 1))
                    me.mark(nc.vector.tensor_tensor(rot_tmp[:, a], bank[half][:, T * n:T * (n + 1)], rope_sin, ALU.mult))
                    me.mark(nc.vector.tensor_tensor(q_raw[:, a], q_raw[:, a], rope_cos, ALU.mult))
            me.wait()
            nc.vector.tensor_tensor(q_rot.rearrange("p t n -> p (t n)"), q_raw, rot_tmp, ALU.add).then_inc(sem("roped"), 1)
            me.mark(nc.vector.tensor_tensor(k_raw, k_raw, rope_cos, ALU.mult))
            dve.wait_ge(sem("roped"), 1)
            me.mark(nc.vector.tensor_tensor(rot_tmp[:, 0:T], bank[2][:, 0:T], rope_sin, ALU.mult))
            me.wait()
            nc.vector.tensor_tensor(k_all[:, 0:T], k_raw, rot_tmp[:, 0:T], ALU.add).then_inc(sem("roped"), 1)
            for u in range(16):
                c = OIN_CHUNK.get(u)
                h = (u // 2) % 4 + 4 * (u // 8)
                dve.wait_ge(sem("ws_done"), u + 1)
                me.mark(nc.vector.reduce_max(small[:, 60:61], bank[u % 2][:, :], AX_X, negate=True))
                me.wait()
                nc.vector.tensor_scalar(small[:, 16 + u:17 + u], small[:, 60:61], QK, neg_sink[:, h:h + 1],
                                        ALU.mult, ALU.min).then_inc(sem("wneg_max"), 1)
                if c is not None:
                    split(LIN_OIN + 3 + c + 2)
                if c in (1, 3):
                    dve.wait_ge(sem("lin_done"), LIN_OPEN + LIN_OIN + 3 + c + 1)
                    dve.wait_ge(sem("oin_evac"), c // 2 + 1)
                    dst = ccx[:, c - 1:c + 1, 1:1 + T]
                    nc.vector.tensor_tensor(dst, dst, wide[:, 1, :].rearrange("p (t n) -> p t n", n=T),
                                            ALU.mult).then_inc(sem("ccx_done"), 1)
                dve.wait_ge(sem("wexp"), 2 * u + 2)
                s2 = small[:, 32 + 2 * (u % 2):34 + 2 * (u % 2)]
                den = small[:, 36:37]
                me.mark(nc.vector.tensor_tensor(den, s2[:, 0:1], s2[:, 1:2], ALU.add))
                me.wait()
                me.mark(nc.vector.reciprocal(small[:, 37:38], den))
                me.wait()
                nc.vector.tensor_scalar(w_prob[u % 2], w_prob[u % 2], small[:, 37:38], None,
                                        ALU.mult).then_inc(sem("wprob_ready"), 1)
                if u == 9:
                    dve.wait_ge(sem("ccx_done"), 2)
                    for t in range(4):
                        me.mark(nc.vector.tensor_scalar(y_c[:, t, :], ccx[:, t, 0:T], col("o_conv", t), None, ALU.mult))
                    me.wait()
                    for k in (1, 2):
                        for t in range(4):
                            me.mark(nc.vector.scalar_tensor_tensor(y_c[:, t, :], ccx[:, t, k:k + T], col("o_conv", 4 * k + t),
                                                                   y_c[:, t, :], ALU.mult, ALU.add))
                        me.wait()
                    dve.wait_ge(sem("oin_evac"), 4)
                    me.mark(nc.vector.tensor_tensor(y_c, y_c, cb, ALU.mult))
            dve.wait_ge(sem("silu_gates"), 1)
            me.wait()
            nc.vector.tensor_tensor(y_c, y_c, cg_ag[:, 0:4, :], ALU.mult).then_inc(sem("y_c"), 1)
            dve.wait_ge(sem("silu_gates"), 2)
            dve.wait_ge(sem("wpv_done"), 16)
            nc.vector.tensor_tensor(rot_tmp, wide[:, 2:4, :].rearrange("p b n -> p (b n)"),
                                    cg_ag[:, 4:8, :].rearrange("p t n -> p (t n)"), ALU.mult).then_inc(sem("y_d"), 1)
            for half, src in ((0, y_c), (1, rot_tmp.rearrange("p (t n) -> p t n", n=T))):
                dve.wait_ge(sem("yo_hi"), half + 1)
                nc.vector.tensor_tensor(h_lo[:, 4 * half:4 * half + 4, 0:T], src,
                                        h_hi[:, 4 * half:4 * half + 4, 0:T].bitcast(F32), ALU.subtract).then_inc(sem("yo_lo"), 1)
            mod_bias(44, 48)
            for i in range(4):
                split(LIN_OOUT + i + 2)
                dve.wait_ge(sem("lin_done"), LIN_OPEN + LIN_OOUT + i + 1)
                for t in range(2):
                    k = 2 * i + t
                    nc.vector.scalar_tensor_tensor(xs[:, k, 0:T], bank[i % 2][:, t * T:(t + 1) * T], shift_col(O_GT, k),
                                                   xs[:, k, 0:T], ALU.mult, ALU.add).then_inc(sem("oout_evac"), 1)
            dve.wait_ge(sem("rstd_ready"), 7)
            for k in range(KT):
                nc.vector.scalar_tensor_tensor(xs[:, k, 0:T], xs[:, k, 0:T], col("final_norm", k), rstd[:, 0:T],
                                               ALU.mult, ALU.mult).then_inc(sem("last_done"), 1)

        @block.tensor
        def _(pe):
            mm = nc.tensor.matmul
            ident, ones = c0[:, 0:P], c0[:, P:2 * P]

            def triple(out, w, x, start, stop, skip=False):
                for n, (a, b) in enumerate(((0, 0), (0, 1), (1, 0))):
                    last = mm(out, w[a], x[b], start=start and n == 0, stop=stop and n == 2, skip_group_check=skip)
                return last

            def whl(slot, a, n):
                return w_hi[:, slot, a:a + n], w_lo[:, slot, a:a + n]

            def hhl(k, a, n):
                return h_hi[:, k, a:a + n], h_lo[:, k, a:a + n]

            def features(j, slot, outs, a, n, order=None, ready=None):
                pe.wait_ge(sem("lo_done"), j + 1)
                order = order or [(k, k) for k in range(KT)]
                for m in range(2):
                    for i, (k, hk) in enumerate(order):
                        if ready and m == 0:
                            ready(hk)
                        last = triple(outs[m], whl(slot, 256 * k + P * m, P), hhl(hk, a, n), i == 0, i == KT - 1)
                last.then_inc(sem("lin_done"), 1)

            def tokens(j, slot, outs, a):
                pe.wait_ge(sem("lo_done"), j + 1)
                for m in range(2):
                    for k in range(KT):
                        last = triple(outs[m], hhl(k, a + P * m, P), whl(slot, 256 * k, 256), k == 0, k == KT - 1)
                last.then_inc(sem("lin_done"), 1)

            def halves(b):
                return b[:, 0:T], b[:, T:2 * T]

            def sum_squares(name):
                n, s = NORMS[name][:2]
                if n and s == 0:
                    pe.wait_ge(sem("rstd_ready"), n)
                for k in range(KT):
                    pe.wait_ge(sem("squares"), squares_before(n) + k + 1)
                    last = mm(bank[2 + s][:, s * T:(s + 1) * T], ones, square_tmp(name)[:, k, :], start=(k == 0), stop=(k == KT - 1))
                    if n == 0 and k == 0:
                        last.then_inc(sem("lin_done"), LIN_OPEN)
                last.then_inc(sem("sumsq"), 1)

            def tile_ready(name):
                return lambda k: pe.wait_ge(sem("norm_lo"), NORMS[name][4] + k + 1)

            pe.wait_ge(sem("rel_loaded"), 32)
            pe.wait_ge(sem("rel_one"), 1)
            mm(bank[3][0:8, 0:384], rel[:, :], onehot, start=True, stop=True).then_inc(sem("bias_row"), 1)
            pe.wait_ge(sem("c0_loaded"), 16)
            sum_squares("mix")
            def qkv_step(i, n):
                j = 6 * i + n
                if not isinstance(i, int) or j >= 2:
                    pe.wait_ge(sem("proj_evac"), j - 1)
                if n < 4:
                    features(j, n % SPL, halves(bank[n % 2]), 0, T, ready=tile_ready("mix") if j == 0 else None)
                else:
                    tokens(j, n % SPL, halves(bank[n % 2]), 0)

            for i in range(2):
                for n in range(6):
                    qkv_step(i, n)

            def q_of(h, branch, a, b):
                t, p0 = h // 2, HD * (h % 2)
                return proj[p0:p0 + HD, 6 * branch + t // 2, (t % 2) * T + a:(t % 2) * T + b]

            def k_of(h, branch, a, b):
                t, p0 = h // 2, HD * (h % 2)
                return proj[p0:p0 + HD, 6 * branch + 2 + t // 2, (t % 2) * T + a:(t % 2) * T + b]

            def v_of(h, branch, m):
                return proj[:, 6 * branch + 4 + h // 4, m * T + (h % 4) * HD:m * T + (h % 4 + 1) * HD]

            def weighted_values(h):
                pe.wait_ge(sem("pt_ready"), h + 1)
                pe.wait_ge(sem("aw_ready"), h + 1)
                if h >= 2 and h % 2 == 0:
                    pe.wait_ge(sem("att_lo"), h // 2)
                p0 = HD * (h % 2)
                for branch, w in ((0, pt[h % 2]), (1, aw)):
                    c = branch * T
                    mm(wide[p0:p0 + HD, 3, c:c + T], v_of(h, branch, 0), w[:, 0:T], start=True, stop=False)
                    last = mm(wide[p0:p0 + HD, 3, c + P:c + T], v_of(h, branch, 1), w[:, T:T + P], start=False, stop=True)
                last.then_inc(sem("pv_done"), 1)

            pe.wait_ge(sem("proj_evac"), 12)
            pe.wait_ge(sem("c1_loaded"), 16)
            def transposed_probs(h):
                pe.wait_ge(sem("prob_ready"), h + 1)
                if h:
                    pe.wait_ge(sem("pt_ready"), h)
                nc.tensor.transpose(wide[:, 1, 0:128], prob[:, 0:128], ident)
                nc.tensor.transpose(wide[:, 1, 128:256], prob[:, 128:256], ident)
                nc.tensor.transpose(wide[:, 1, 256:384], prob[:, 256:384], ident).then_inc(sem("pt_done"), 1)

            def stick_exponents(h):
                pe.wait_ge(sem("sb_kept"), h + 1)
                if h:
                    pe.wait_ge(sem("sb_min"), h)
                e = bank[2]
                mm(e[:, 0:256], k_of(h, 1, 0, 128), q_of(h, 1, 0, 256), start=True, stop=False)
                mm(e[:, 0:256], tri8, sb_r[:, 0:256], start=False, stop=False)
                mm(e[:, 128:256], all8, sb_r[:, 256:384], start=False, stop=True)
                mm(e[:, 256:384], k_of(h, 1, 128, 256), q_of(h, 1, 128, 256), start=True, stop=False)
                mm(e[:, 256:384], tri8, sb_r[:, 256:384], start=False, stop=True).then_inc(sem("e_done"), 1)

            for h in range(NH + 1):
                if h < NH:
                    pe.wait_ge(sem(f"trev_loaded{h % TREV}"), 16 * (h // TREV + 1))
                    if h:
                        pe.wait_ge(sem("exp_done"), 2 * h)
                        pe.wait_ge(sem("sb_relu"), h)
                    mm(wide[:, 0, 0:128], q_of(h, 0, 0, 128), k_of(h, 0, 0, 128), start=True, stop=False)
                    mm(wide[:, 0, 0:128], anti8, trev[:, h % TREV, 128:256], start=False, stop=True)
                    mm(wide[:, 0, 128:384], q_of(h, 0, 128, 256), k_of(h, 0, 0, 256), start=True, stop=False)
                    mm(wide[:, 0, 128:384], anti8, trev[:, h % TREV, :], start=False, stop=True)
                    mm(wide[:, 2, 0:256], k_of(h, 1, 0, 128), q_of(h, 1, 0, 256), start=True, stop=True)
                    mm(wide[:, 2, 256:384], k_of(h, 1, 128, 256), q_of(h, 1, 128, 256), start=True,
                       stop=True).then_inc(sem("qk_done"), 1)
                if h:
                    transposed_probs(h - 1)
                    stick_exponents(h - 1)
                if h < NH:
                    if h >= 2:
                        pe.wait_ge(sem("gate_evac"), h - 1)
                    j = LIN_GATE + h
                    features(j, j % SPL, halves(bank[j % 2]), 0, T)
                if h:
                    weighted_values(h - 1)
            for i in range(4):
                j = LIN_BR + i
                pe.wait_ge(sem("lo_done"), j + 1)
                if i == 0:
                    pe.wait_ge(sem("att_lo"), 4)
                if i == 2:
                    sum_squares("even_ctx")
                if i >= 2:
                    pe.wait_ge(sem("br_evac"), i - 1)
                for m in range(4):
                    out = wide[:, 2 * (i % 2) + m // 2, (m % 2) * T:(m % 2 + 1) * T]
                    for k in range(4):
                        last = triple(out, whl(j % SPL, 512 * k + P * m, P), hhl(4 * (i % 2) + k, T, T), k == 0, k == 3)
                last.then_inc(sem("lin_done"), 1)
            pe.wait_ge(sem("gate_evac"), 8)
            for i in range(4):
                j = LIN_OUT + i
                if i >= 2:
                    pe.wait_ge(sem("out_evac"), 2 * (i - 1))
                features(j, j % SPL, halves(bank[i % 2]), 0, T,
                         ready=None if i else lambda k: pe.wait_ge(sem("mixed_lo"), k // 4 + 1))
            sum_squares("ffn")
            pe.wait_ge(sem("zeros_set"), 1)
            for b in range(4):
                mm(wide[:, b, :], zeros[:, 0:P], zeros[:, :], start=True, stop=False, skip_group_check=True)

            def down(j, slot, c):
                pe.wait_ge(sem("lo_done"), j + 1)
                pe.wait_ge(sem("g_lo_done"), c + 1)
                for k in range(2):
                    for m in range(KT):
                        last = triple(wide[:, m // 2, (m % 2) * T:(m % 2 + 1) * T], whl(slot, 1024 * k + P * m, P),
                                      (g_hi[:, k, :], g_lo[:, k, :]), False, True, skip=True)
                last.then_inc(sem("lin_done"), 1)

            features(LIN_FFN, LIN_FFN % SPL, halves(bank[0]), 0, T, ready=tile_ready("ffn"))
            features(LIN_FFN + 1, (LIN_FFN + 1) % SPL, halves(bank[1]), 0, T)
            j0, r0 = LIN_FFN + 2, RAW_OF_LIN[LIN_FFN + 2]
            with pe.Fori(0, FF_STEPS - 1) as i:
                j = 3 * i + j0
                pe.wait_ge(sem("value_conv"), i + 1)
                features(j, j0 % SPL, halves(bank[0]), 0, T)
                pe.wait_ge(sem("gate_conv"), i + 1)
                features(j + 1, (j0 + 1) % SPL, halves(bank[1]), 0, T)
                down(j + 2, (j0 + 2) % SPL, i)
            j = LIN_EIN - 1
            pe.wait_ge(sem("lo_done"), j + 1)
            pe.wait_ge(sem("g_lo_done"), FF_STEPS)
            for m in range(KT):
                for k in range(2):
                    last = triple(wide[:, m // 2, (m % 2) * T:(m % 2 + 1) * T], whl(j % SPL, 1024 * k + P * m, P),
                                  (g_hi[:, k, :], g_lo[:, k, :]), False, True, skip=True)
                if m % 2:
                    last.then_inc(sem("down_bank" if m < KT - 1 else "lin_done"), 1)
            for k in range(KT):
                pe.wait_ge(sem("squares"), squares_before(3) + 2 * k + 2)
                mm(bank[2][:, 0:T], ones, norm_tmp[:, k, :], start=(k == 0), stop=(k == KT - 1))
                last = mm(bank[3][:, 0:T], ones, gain_sq[:, k, :], start=(k == 0), stop=(k == KT - 1))
            last.then_inc(sem("sumsq"), 1)
            pe.wait_ge(sem("c2_loaded"), 48)
            mm(bank[0][:, :], dft_d[:, 0:P], fw, start=True, stop=True)
            mm(bank[1][:, :], dft_d[:, P:2 * P], fw, start=True, stop=True).then_inc(sem("fold_done"), 1)

            def fourier_a(g):
                if g:
                    pe.wait_ge(sem("four_ready"), 2 * g)
                else:
                    pe.wait_ge(sem("fold_ready"), 2)
                    pe.wait_ge(sem("ein_evac"), 6)
                for s in range(2):
                    for lt in range(2):
                        last = mm(bank[2 * s][:, lt * T:(lt + 1) * T], b_val[:, g, s * T + lt * P:s * T + (lt + 1) * P],
                                  fold[:, g, :, :].rearrange("p c n -> p (c n)"), start=True, stop=True)
                    last.then_inc(sem("four_a"), 1)

            def fourier_b(g):
                pe.wait_ge(sem("four_ready"), 2 * g + 2)
                if g:
                    pe.wait_ge(sem("y_b_raw"), g)
                for s in range(2):
                    for q, (part, table) in enumerate(((0, cos_l), (1, sin_l))):
                        for lt in range(2):
                            last = mm(bank[1][:, s * T:(s + 1) * T], four[s][:, lt * T + part * P:lt * T + (part + 1) * P],
                                      table[:, lt, :], start=(q == 0 and lt == 0), stop=(q == 1 and lt == 1))
                last.then_inc(sem("four_b"), 1)

            for i in range(10):
                j = LIN_EIN + i
                b = 2 * (i % 2)
                if i >= 2:
                    pe.wait_ge(sem("ein_evac"), i - 1)
                if i:
                    features(j, j % SPL, (wide[:, b, :], wide[:, b + 1, :]), 0, 2 * T)
                else:
                    pe.wait_ge(sem("lo_done"), j + 1)
                    for s, ready in enumerate((tile_ready("even_x"), tile_ready("even_ctx"))):
                        for m in range(2):
                            for k in range(KT):
                                if m == 0:
                                    ready(k)
                                last = triple(wide[:, m, s * T:(s + 1) * T], whl(j % SPL, 256 * k + P * m, P),
                                              hhl(k, s * T, T), k == 0, k == KT - 1)
                    last.then_inc(sem("lin_done"), 1)
                if i >= 7:
                    fourier_b(i - 7)
                if i >= 6:
                    fourier_a(i - 6)
            fourier_b(3)
            pe.wait_ge(sem("four_ready"), 8)
            for n, t in enumerate((0, 2, 1, 3)):
                if t != 1:
                    pe.wait_ge(sem("conv_tap"), CONV_W * {0: 1, 2: 2, 3: 3}[t])
                if t in (1, 3):
                    pe.wait_ge(sem("prod_used"), (CONV_W - 1) * (1 if t == 1 else 2))
                last = mm(bank[2][:, :], ones, conv[:, t, :], start=(n == 0), stop=(n == 3))
            last.then_inc(sem("ln_sum"), 1)
            for t in range(4):
                pe.wait_ge(sem("ln_squares"), t + 1)
                last = mm(bank[3][:, :], ones, ln_tmp[:, t, :], start=(t == 0), stop=(t == 3))
            last.then_inc(sem("ln_sumsq"), 1)
            pe.wait_ge(sem("lo_done"), LIN_PW + 1)
            pe.wait_ge(sem("ein_evac"), 10)
            for m in range(4):
                for k in range(4):
                    if m == 0:
                        pe.wait_ge(sem("u_lo"), k + 1)
                    last = triple(wide[:, m, :], whl(LIN_PW % SPL, 512 * k + P * m, P), hhl(k, 0, 2 * T), k == 0, k == 3)
                last.then_inc(sem("pw_tile" if m < 3 else "lin_done"), 1)
            for i in range(4):
                j = LIN_EOUT + i
                b = 2 * (i % 2)
                if i >= 2:
                    pe.wait_ge(sem("eout_evac"), 4 * (i - 1))
                features(j, j % SPL, (wide[:, b, :], wide[:, b + 1, :]), 0, 2 * T, [(k, (k + 4) % KT) for k in range(KT)],
                         None if i else lambda hk: pe.wait_ge(sem("y_lo"), (hk + 4) % KT + 1))
            sum_squares("odd_x")
            sum_squares("odd_ctx")
            pe.wait_ge(sem("eout_evac"), 16)
            for i in range(2):
                features(LIN_OIN + i, (LIN_OIN + i) % SPL, halves(wide[:, i, :]), 0, T, ready=None if i else tile_ready("odd_x"))
            j = LIN_OIN + 2
            pe.wait_ge(sem("lo_done"), j + 1)
            for s in range(2):
                for k in range(KT):
                    if s:
                        tile_ready("odd_ctx")(k)
                    triple(wide[:, 2, s * T:(s + 1) * T], whl(j % SPL, 256 * k, P), hhl(k, s * T, T), k == 0, k == KT - 1)
                for tt in range(2 * s, 2 * s + 2):
                    for k in range(KT):
                        last = triple(wide[:, 3, tt * P:(tt + 1) * P], hhl(k, tt * P, P), whl(j % SPL, 256 * k + P, P),
                                      k == 0, k == KT - 1)
            last.then_inc(sem("lin_done"), 1)
            pe.wait_ge(sem("q_raw"), 3)
            pe.wait_ge(sem("rstd_ready"), 6)
            pe.wait_ge(sem("c3_loaded"), 16)
            mm(bank[0][:, :], swap, q_raw[:, 0:512], start=True, stop=True)
            mm(bank[1][:, :], swap, q_raw[:, 512:1024], start=True, stop=True)
            mm(bank[2][:, 0:T], swap, k_raw, start=True, stop=True).then_inc(sem("rot_done"), 1)
            def odd_part(c, m):
                j = LIN_OIN + 3 + c
                if m == 0:
                    pe.wait_ge(sem("lo_done"), j + 1)
                    n = c - 2
                    if n >= 0:
                        if n < 4 and n % 2:
                            pe.wait_ge(sem("ccx_done"), n // 2 + 1)
                        else:
                            pe.wait_ge(sem("oin_evac"), n // 2 + 1 if n < 4 else n - 1)
                for k in range(KT):
                    last = triple(wide[:, c % 2, m * T:(m + 1) * T], whl(j % SPL, 256 * k + P * m, P), hhl(k, 0, T),
                                  k == 0, k == KT - 1)
                if m:
                    last.then_inc(sem("lin_done"), 1)

            for c, m in OIN_PARTS[0]:
                odd_part(c, m)
            pe.wait_ge(sem("roped"), 2)
            pe.wait_ge(sem("kv_evac"), 2)

            def unit(u):
                return (u // 2) % 4, u // 8, u % 2

            for u in range(18):
                if u < 16:
                    t, b, qt = unit(u)
                    p0 = HD * b
                    if u >= 2:
                        pe.wait_ge(sem("wexp"), 2 * (u - 1) - 1)
                    keys = slice(P, 2 * P) if qt == 0 else slice(0, P)
                    mm(bank[u % 2][:, :], q_rot[p0:p0 + HD, t, qt * P:(qt + 1) * P], k_all[p0:p0 + HD, :],
                       start=True, stop=False)
                    mm(bank[u % 2][:, keys], ident, band[:, qt * P:(qt + 1) * P], start=False,
                       stop=True).then_inc(sem("ws_done"), 1)
                if u:
                    for c, m in OIN_PARTS.get(u, ()):
                        odd_part(c, m)
                if 1 <= u < 17:
                    v = u - 1
                    pe.wait_ge(sem("wprob_ready"), v + 1)
                    if v >= 2:
                        pe.wait_ge(sem("wpt_ready"), v - 1)
                    for k in range(4):
                        last = nc.tensor.transpose(bank[2 + v % 2][:, k * P:(k + 1) * P],
                                                   w_prob[v % 2][:, k * P:(k + 1) * P], ident)
                    last.then_inc(sem("wt_done"), 1)
                if u >= 2:
                    v = u - 2
                    t, b, qt = unit(v)
                    pe.wait_ge(sem("wpt_ready"), v + 1)
                    out = wide[HD * b:HD * (b + 1), 2 + t // 2, (t % 2) * T + qt * P:(t % 2) * T + (qt + 1) * P]
                    for k in range(4):
                        last = mm(out, v_tok[:, k, HD * b:HD * (b + 1)], w_pt[v % 2][:, k * P:(k + 1) * P],
                                  start=(k == 0), stop=(k == 3))
                    last.then_inc(sem("wpv_done"), 1)
            for i in range(4):
                j = LIN_OOUT + i
                if i >= 2:
                    pe.wait_ge(sem("oout_evac"), 2 * (i - 1))
                features(j, j % SPL, halves(bank[i % 2]), 0, T,
                         ready=None if i else lambda k: pe.wait_ge(sem("yo_lo"), k // 4 + 1))
            sum_squares("last")


def shape_constants():
    f = np.float32
    i, j = np.meshgrid(np.arange(P), np.arange(P), indexing="ij")
    c0 = np.concatenate([np.eye(P), np.ones((P, P))], 1).astype(f)
    c1 = np.zeros((P, N_C1), f)
    c1[:, 0:128] = 8.0 * (i + j == P - 1)
    c1[:, 128:256] = -8.0 * (i >= j)
    c1[:, 256:384] = -8.0
    past = np.concatenate([i < j, np.ones((P, P), bool), i < j], 1)
    c1[:, 384:768] = past
    c1[:, 768:1152] = np.where(past, BIG, NEG)
    dist = 255 - np.arange(383)
    n = np.maximum(dist, 0)
    n_f = np.maximum(n, 16).astype(f)
    large = 16 + (np.log(n_f / f(16)) / f(np.log(128 / 16)) * f(16)).astype(np.int32)
    bucket = np.where(n < 16, n, np.minimum(large, 31))
    hot = np.zeros((33, 384), f)
    hot[:32, :383] = (np.arange(32)[:, None] == bucket[None, :]) & (dist >= 0)[None, :]
    hot[32, :383] = np.where(dist >= 0, 0.0, NEG)
    c1[0:33, 1152:1536] = hot
    l = np.arange(T)
    ang = 2 * np.pi * (np.outer(l, l) % T) / T
    scale = 1.0 / np.sqrt(T * P)
    cos_l = (np.cos(ang) * scale).reshape(2, P, T).transpose(1, 0, 2).reshape(P, 512)
    sin_l = (-np.sin(ang) * scale).reshape(2, P, T).transpose(1, 0, 2).reshape(P, 512)
    d = np.arange(P)
    ang = 2 * np.pi * (np.outer(d, d) % P) / P
    pos = np.arange(T)
    row, cl = (pos // 64).astype(f), (pos % 64).astype(f)
    inv = np.power(f(10000.0), -np.arange(16, dtype=f) / f(16)).astype(f)
    r = np.arange(P) % HD
    coord = np.where((r // 32 == 0)[:, None], row[None, :], cl[None, :])
    a = (coord * inv[r % 16][:, None]).astype(f)
    sign = np.where((r % 32) // 16 == 0, -1.0, 1.0)[:, None]
    partner = np.where((np.arange(P) % 32) // 16 == 0, np.arange(P) + 16, np.arange(P) - 16)
    swap = (np.arange(P)[:, None] == partner[None, :]).astype(f)
    band = np.concatenate([np.where(j <= i, 0.0, 8 * NEG), np.where(j >= i, 0.0, 8 * NEG)], 1)
    c2 = np.concatenate([cos_l, sin_l, np.cos(ang), np.sin(ang)], 1).astype(f)
    c3 = np.concatenate([np.cos(a), np.sin(a) * sign, swap, band], 1).astype(f)
    assert c2.shape == (P, N_C2) and c3.shape == (P, N_C3)
    return c0, c1, c2, c3


def k8(w):
    n = w.shape[1] // 256
    return list(w.reshape(8, P, n, 256).transpose(2, 1, 0, 3).reshape(n, P, CHUNK))


def transposed(w):
    n = w.shape[1] // 256
    return list(w.T.reshape(n, 2, P, 1024).transpose(0, 2, 1, 3).reshape(n, P, CHUNK))


def k4(w):
    n = w.shape[1] // 512
    return list(w.reshape(4, P, n, 512).transpose(2, 1, 0, 3).reshape(n, P, CHUNK))


def k2(w):
    n = w.shape[0] // 256
    return list(w.reshape(n, 2, P, 1024).transpose(0, 2, 1, 3).reshape(n, P, CHUNK))


def tiles(v):
    return v.reshape(-1, P).T


def rows(m):
    return np.concatenate([tiles(r) for r in m], 1)


def kernel(**inputs):
    import concourse.bacc as bacc
    from concourse.bass_utils import run_bass_kernel_spmd as run

    a = {k: np.asarray(v) for k, v in inputs.items()}
    x, cx = a["x"][0], a["ctx_2"][0]
    xs = np.concatenate([x.T.reshape(8, P, T), cx.T.reshape(8, P, T)], 2).transpose(1, 0, 2)

    wi = a["w_in"][0]
    part = [wi[:, 512 * i:512 * (i + 1)] for i in range(6)] + [wi[:, 3072:]]
    lin = []
    for b in (0, 3):
        for n in range(3):
            lin += k8(part[b + n])
    lin += k8(part[6])
    bm, bs = k4(a["w_br_moba"][0]), k4(a["w_br_sb"][0])
    lin += [bm[0], bs[0], bm[1], bs[1]]
    lin += k8(a["w_out"][0])
    up = a["w_up"][0]
    uv, ug, dn = k8(up[:, :2816]), k8(up[:, 2816:]), k2(a["w_down"][0])
    lin += [uv[0], ug[0]]
    for i in range(10):
        lin += [uv[i + 1], ug[i + 1], dn[i]]
    lin += [dn[10]]
    ei = a["e_w_in_2"][0]
    av, ag, at, bv, bg = (k8(ei[:, 512 * i:512 * (i + 1)]) for i in range(5))
    lin += [av[0], ag[0], av[1], ag[1]] + bv + at + bg
    lin += k4(a["e_a_pw_w_2"][0])
    lin += k8(a["e_w_out_2"][0])
    oi = a["o_w_in_2"][0]
    heads = [0, 4, 1, 5, 2, 6, 3, 7]
    hperm = np.concatenate([np.arange(HD * h, HD * (h + 1)) for h in heads])
    cb, cc, cxx, cg = (k8(oi[:, 512 * i:512 * (i + 1)]) for i in range(4))
    q, kv, og = oi[:, 2048:2560][:, hperm], oi[:, 2560:2816], oi[:, 2816:3328][:, hperm]
    lin += k8(q) + k8(kv) + [cc[0], cxx[0], cc[1], cxx[1]] + cb + cg + k8(og)
    oo = a["o_w_out_2"][0]
    lin += k8(np.concatenate([oo[:512], oo[512:][hperm]], 0))
    assert len(lin) == N_LIN
    ada = a["w_ada"][0]
    sh_m, sc_m, gt_m, sh_f, sc_f, gt_f = (transposed(ada[:, D * i:D * (i + 1)]) for i in range(6))
    mod = sc_m + sh_m + gt_m + sh_f + sc_f + gt_f
    for w in (a["e_w_mod_2"][0], a["o_w_mod_2"][0]):
        sh, sc, gt = (transposed(w[:, D * i:D * (i + 1)]) for i in range(3))
        mod += sc + sh + gt
    assert len(mod) == N_MOD
    w = np.stack([(lin if kind == "lin" else mod)[n] for kind, n in ORDER])

    cond = np.stack([a["c"][0], a["c_2"][0], a["c_ctx_2"]])
    ba = a["b_ada"][0]
    bias = [ba[D:2 * D], ba[:D], ba[2 * D:3 * D], ba[3 * D:4 * D], ba[4 * D:5 * D], ba[5 * D:]]
    for b in (a["e_b_mod_2"][0], a["o_b_mod_2"][0]):
        bias += [b[D:2 * D], b[:D], b[2 * D:]]
    bias = np.repeat(tiles(np.concatenate(bias)), 2, axis=1)
    sink = np.broadcast_to(a["o_sink_2"][0][None, :], (P, 8))
    vec = np.concatenate([bias, tiles(a["g_mix"][0]), tiles(a["g_ffn"][0]), tiles(a["g_final"]),
                          tiles(a["e_norm_2"][0]), tiles(a["o_norm_2"][0]), tiles(a["final_norm_2"]),
                          rows(a["w_conv"][0]), tiles(a["b_conv"][0]), rows(a["e_a_conv_w_2"][0]),
                          tiles(a["e_a_conv_b_2"][0]), tiles(a["e_a_ln_g_2"][0]), tiles(a["e_a_ln_b_2"][0]),
                          tiles(a["e_a_pw_b_2"][0]), rows(a["o_c_conv_w_2"][0]), sink], 1)
    assert vec.shape == (P, N_VEC)
    fw = a["e_b_fw_2"][0].transpose(1, 0, 2).reshape(P, 512)
    c0, c1, c2, c3 = shape_constants()
    arrays = {"xs": xs, "cond": cond, "vec": vec, "rel": a["rel_bias"].T, "w": w, "fw": fw, "c0": c0, "c1": c1,
              "c2": c2, "c3": c3}
    arrays = {k: np.ascontiguousarray(v) for k, v in arrays.items()}

    nc = bacc.Bacc("TRN2", target_bir_lowering=False, num_devices=1)
    aps = [nc.dram_tensor("in_" + k, v.shape, F32, kind="ExternalInput").ap() for k, v in arrays.items()]
    diff = nc.dram_tensor("diff", (8, 384), F32).ap()
    out = nc.dram_tensor("out", (P, KT, T), F32, kind="ExternalOutput").ap()
    build(nc, *aps, diff, out)
    r = run(nc, [{"in_" + k: v for k, v in arrays.items()}], core_ids=[0])
    return r.results[0]["out"].transpose(2, 1, 0).reshape(1, T, D)
```
